# Optimizing a Trainium2 kernel written in Bass

```python
import math
import jax, jax.numpy as jnp
from jax import lax
import numpy as np

D_MODEL = 1024
BATCH = 1
SEQ = 256
DEPTH = 2

CTX_LEN = 256
GRID_W = 64
EPS = 1e-6

A_WIDTH = D_MODEL // 4
A_HEADS = 4
A_HEAD_DIM = A_WIDTH // A_HEADS
CHUNK = 128

B_WIDTH = D_MODEL // 2
B_HEADS = 4
B_V_DIM = B_WIDTH // B_HEADS
B_QK_DIM = B_V_DIM // 2
ROPE_AXIS_DIM = B_QK_DIM // 2
ROPE_THETA = 10000.0
Q_BLOCK = 128

C_WIDTH = D_MODEL // 4
C_CONV = 31

MIX_WIDTH = A_WIDTH + B_WIDTH + C_WIDTH
QK_COLS = B_HEADS * 2 * B_QK_DIM
COL_A = 0
COL_Q = COL_A + 2 * A_WIDTH
COL_K = COL_Q + QK_COLS
COL_V = COL_K + QK_COLS
COL_C = COL_V + B_WIDTH
IN_COLS = COL_C + 2 * C_WIDTH

D_FF = ((8 * D_MODEL // 3 + 127) // 128) * 128
FFN_CONV = 3


F32 = jnp.float32

def rms_norm(x, g):
    xf = x.astype(F32)
    y = xf * lax.rsqrt(jnp.mean(xf * xf, axis=-1, keepdims=True) + EPS)
    return (y * g.astype(F32)).astype(x.dtype)

def layer_norm(x, g, b):
    xf = x.astype(F32)
    xc = xf - jnp.mean(xf, axis=-1, keepdims=True)
    y = xc * lax.rsqrt(jnp.mean(xc * xc, axis=-1, keepdims=True) + EPS)
    return (y * g.astype(F32) + b.astype(F32)).astype(x.dtype)

def dwconv(x, w, b):
    k = w.shape[0]
    y = lax.conv_general_dilated(
        x, w[:, None, :].astype(x.dtype), window_strides=(1,), padding=[(k // 2, k // 2)],
        dimension_numbers=("NWC", "WIO", "NWC"), feature_group_count=x.shape[-1])
    return y + b

def adaln(cvec, w, b, n):
    m = jax.nn.silu(cvec) @ w[:, : n * D_MODEL] + b[: n * D_MODEL]
    return jnp.split(m, n, axis=-1)

def modulate(x, shift, scale):
    return x * (1 + scale) + shift

def axial_rope_tables(n_tokens, dtype):
    rows = n_tokens // GRID_W
    row = jnp.repeat(jnp.arange(rows), GRID_W).astype(F32)
    col = jnp.tile(jnp.arange(GRID_W), rows).astype(F32)
    inv = ROPE_THETA ** (-jnp.arange(0, ROPE_AXIS_DIM, 2, dtype=F32) / ROPE_AXIS_DIM)
    ang = jnp.stack([row[:, None] * inv, col[:, None] * inv], axis=1)
    ang = ang[None, :, None, None]
    return (jnp.cos(ang).astype(dtype), jnp.sin(ang).astype(dtype))

def axial_rope(t, cos, sin):
    sh = t.shape
    t = t.reshape(*sh[:-1], 2, 2, ROPE_AXIS_DIM // 2)
    t1, t2 = t[..., 0, :], t[..., 1, :]
    out = jnp.stack([t1 * cos - t2 * sin, t2 * cos + t1 * sin], axis=-2)
    return out.reshape(sh)

def qk_heads(p, g, rope):
    b, n, _ = p.shape
    t = rms_norm(p.reshape(b, n, B_HEADS, 2, B_QK_DIM), g)
    return t if rope is None else axial_rope(t, *rope)

def project(h, P, rope):
    p = h @ P["w_in"]
    b, n, _ = p.shape
    q = qk_heads(p[..., COL_Q:COL_K], P["q_norm_g"], rope)
    k = qk_heads(p[..., COL_K:COL_V], P["k_norm_g"], rope)
    v = p[..., COL_V:COL_C].reshape(b, n, B_HEADS, B_V_DIM)
    return (p[..., COL_A:COL_Q], q, k, v, p[..., COL_C:])

def diff_attn(q, k, v, lam):
    s = jnp.einsum("bqhmd,bkhmd->bhmqk", q.astype(F32), k.astype(F32)) * (B_QK_DIM ** -0.5)
    p = jax.nn.softmax(s, axis=-1)
    a = p[:, :, 0] - lam * p[:, :, 1]
    return jnp.einsum("bhqk,bkhd->bqhd", a, v.astype(F32))

def blocked_diff_attn(q, k, v, lam):
    b, n = q.shape[:2]
    qb = jnp.moveaxis(q.reshape(b, n // Q_BLOCK, Q_BLOCK, *q.shape[2:]), 1, 0)
    o = lax.map(lambda qi: diff_attn(qi, k, v, lam), qb)
    return jnp.moveaxis(o, 0, 1).reshape(b, n, B_HEADS, B_V_DIM)

def chunk_gmlp(pa, P):
    z = jax.nn.gelu(pa)
    u, v = jnp.split(z, 2, axis=-1)
    v = layer_norm(v, P["ln_v_g"], P["ln_v_b"])
    b, n, _ = v.shape
    vb = v.reshape(b, n // CHUNK, CHUNK, A_HEADS, A_HEAD_DIM)
    gate = jnp.einsum("hpq,bnqhd->bnphd", P["w_s"], vb) + P["b_s"].T[:, :, None]
    return u * gate.reshape(b, n, A_WIDTH)

def conformer_conv(pc, P):
    a, g = jnp.split(pc, 2, axis=-1)
    y = dwconv(a * jax.nn.sigmoid(g), P["conv_w"], P["conv_b"])
    return jax.nn.silu(layer_norm(y, P["ln_c_g"], P["ln_c_b"]))

def mixer_merge(pa, o, pc, P, lam_init):
    b, n, _ = pa.shape
    ya = chunk_gmlp(pa, P)
    yb = (rms_norm(o, P["subln_g"]) * (1.0 - lam_init)).astype(pa.dtype).reshape(b, n, B_WIDTH)
    yc = conformer_conv(pc, P)
    return jnp.concatenate([ya, yb, yc], axis=-1) @ P["w_out"]

def conv_ffn(h, P):
    gt = dwconv(h @ P["w_gate"], P["ffn_conv_w"], P["ffn_conv_b"])
    return (jax.nn.silu(gt) * (h @ P["w_val"])) @ P["w_down"]

def first_inputs(seed: int = 0) -> dict:
    key = jax.random.key(seed)
    ks = jax.random.split(key, 30)
    L = DEPTH

    def nrm(i, shape, s):
        return jax.random.normal(ks[i], shape, F32) * s

    return {
        "x": nrm(0, (BATCH, SEQ, D_MODEL), 1.0),
        "c": nrm(1, (BATCH, D_MODEL), 1.0),
        "ctx": nrm(2, (BATCH, CTX_LEN, D_MODEL), 1.0),
        "c_ctx": nrm(3, (D_MODEL,), 1.0),
        "w_mod": nrm(4, (L, D_MODEL, 6 * D_MODEL), D_MODEL ** -0.5),
        "b_mod": nrm(5, (L, 6 * D_MODEL), 0.02),
        "norm1_g": 1.0 + nrm(6, (L, D_MODEL), 0.05),
        "w_in": nrm(7, (L, D_MODEL, IN_COLS), D_MODEL ** -0.5),
        "ln_v_g": 1.0 + nrm(8, (L, A_WIDTH), 0.05),
        "ln_v_b": nrm(9, (L, A_WIDTH), 0.02),
        "w_s": nrm(10, (L, A_HEADS, CHUNK, CHUNK), CHUNK ** -0.5),
        "b_s": nrm(11, (L, A_HEADS, CHUNK), 0.02),
        "q_norm_g": 1.0 + nrm(12, (L, B_QK_DIM), 0.05),
        "k_norm_g": 1.0 + nrm(13, (L, B_QK_DIM), 0.05),
        "lam_q1": nrm(14, (L, B_QK_DIM), 0.1),
        "lam_k1": nrm(15, (L, B_QK_DIM), 0.1),
        "lam_q2": nrm(16, (L, B_QK_DIM), 0.1),
        "lam_k2": nrm(17, (L, B_QK_DIM), 0.1),
        "subln_g": 1.0 + nrm(18, (L, B_V_DIM), 0.05),
        "conv_w": nrm(19, (L, C_CONV, C_WIDTH), C_CONV ** -0.5),
        "conv_b": nrm(20, (L, C_WIDTH), 0.02),
        "ln_c_g": 1.0 + nrm(21, (L, C_WIDTH), 0.05),
        "ln_c_b": nrm(22, (L, C_WIDTH), 0.02),
        "w_out": nrm(23, (L, MIX_WIDTH, D_MODEL), MIX_WIDTH ** -0.5),
        "norm2_g": 1.0 + nrm(24, (L, D_MODEL), 0.05),
        "w_gate": nrm(25, (L, D_MODEL, D_FF), D_MODEL ** -0.5),
        "w_val": nrm(26, (L, D_MODEL, D_FF), D_MODEL ** -0.5),
        "ffn_conv_w": nrm(27, (L, FFN_CONV, D_FF), FFN_CONV ** -0.5),
        "ffn_conv_b": nrm(28, (L, D_FF), 0.02),
        "w_down": nrm(29, (L, D_FF, D_MODEL), D_FF ** -0.5),
    }

def first_block(x, c, ctx, c_ctx, w_mod, b_mod, norm1_g, w_in, ln_v_g, ln_v_b, w_s, b_s,
              q_norm_g, k_norm_g, lam_q1, lam_k1, lam_q2, lam_k2, subln_g, conv_w, conv_b,
              ln_c_g, ln_c_b, w_out, norm2_g, w_gate, w_val, ffn_conv_w, ffn_conv_b, w_down):
    rope = axial_rope_tables(x.shape[1], x.dtype)
    x_lat, x_ctx = x, ctx
    for l in range(DEPTH):
        last = l == DEPTH - 1
        P = {
            "w_in": w_in[l], "ln_v_g": ln_v_g[l], "ln_v_b": ln_v_b[l], "w_s": w_s[l], "b_s": b_s[l],
            "q_norm_g": q_norm_g[l], "k_norm_g": k_norm_g[l], "subln_g": subln_g[l],
            "conv_w": conv_w[l], "conv_b": conv_b[l], "ln_c_g": ln_c_g[l], "ln_c_b": ln_c_b[l],
            "w_out": w_out[l], "w_gate": w_gate[l], "w_val": w_val[l],
            "ffn_conv_w": ffn_conv_w[l], "ffn_conv_b": ffn_conv_b[l], "w_down": w_down[l],
        }
        lam_init = 0.8 - 0.6 * math.exp(-0.3 * l)
        lam = (jnp.exp(jnp.sum(lam_q1[l].astype(F32) * lam_k1[l].astype(F32)))
               - jnp.exp(jnp.sum(lam_q2[l].astype(F32) * lam_k2[l].astype(F32))) + lam_init)

        cmod = adaln(c_ctx, w_mod[l], b_mod[l], 2 if last else 6)
        hc = modulate(rms_norm(x_ctx, norm1_g[l]), cmod[0], cmod[1])
        if last:
            pkv = hc @ w_in[l][:, COL_K:COL_C]
            k_c = qk_heads(pkv[..., :QK_COLS], k_norm_g[l], None)
            v_c = pkv[..., QK_COLS:].reshape(hc.shape[0], hc.shape[1], B_HEADS, B_V_DIM)
        else:
            pa_c, q_c, k_c, v_c, pc_c = project(hc, P, None)
            o_c = diff_attn(q_c, k_c, v_c, lam)
            x_ctx = x_ctx + cmod[2] * mixer_merge(pa_c, o_c, pc_c, P, lam_init)
            h2c = modulate(rms_norm(x_ctx, norm2_g[l]), cmod[3], cmod[4])
            x_ctx = x_ctx + cmod[5] * conv_ffn(h2c, P)

        sh1, sc1, g1, sh2, sc2, g2 = [m[:, None, :] for m in adaln(c, w_mod[l], b_mod[l], 6)]
        hl = modulate(rms_norm(x_lat, norm1_g[l]), sh1, sc1)
        pa, q, k, v, pc = project(hl, P, rope)
        k_all = jnp.concatenate([k, k_c], axis=1)
        v_all = jnp.concatenate([v, v_c], axis=1)
        o = blocked_diff_attn(q, k_all, v_all, lam)
        x_lat = x_lat + g1 * mixer_merge(pa, o, pc, P, lam_init)
        h2 = modulate(rms_norm(x_lat, norm2_g[l]), sh2, sc2)
        x_lat = x_lat + g2 * conv_ffn(h2, P)
    return x_lat


CHUNK_2 = 64
HEAD_DIM = 64
ROT_DIM = HEAD_DIM // 4
ROPE_THETA_2 = 500000.0
N_HEADS_A = 6
N_HEADS_B = 5
N_HEADS_C = 5
WIDTH_A = N_HEADS_A * HEAD_DIM
WIDTH_B = N_HEADS_B * HEAD_DIM
WIDTH_C = N_HEADS_C * HEAD_DIM
MIX_WIDTH_2 = WIDTH_A + WIDTH_B + WIDTH_C
IDX_HEADS = 8
IDX_DIM = 64
TOPK_MAX = 256
PREV_CHUNKS = 8
BAND = (PREV_CHUNKS + 1) * CHUNK_2
REL_CLIP = 128
N_BRANCH = 3
FFN_HIDDEN = -(-8 * D_MODEL // (3 * 256)) * 256
RMS_EPS = 1e-6
FORGET_BIAS_LO = 2.0
FORGET_BIAS_HI = 6.0
SPLIT_SIZES = (WIDTH_A, WIDTH_A, WIDTH_A, IDX_HEADS * IDX_DIM, IDX_DIM, IDX_HEADS,
               3 * WIDTH_B, 3 * WIDTH_C, N_HEADS_C, N_BRANCH * D_MODEL)
IN_WIDTH = sum(SPLIT_SIZES)


def rmsnorm(x, g):
    xf = x.astype(jnp.float32)
    y = xf * lax.rsqrt(jnp.mean(xf * xf, axis=-1, keepdims=True) + RMS_EPS)
    return (y * g.astype(jnp.float32)).astype(x.dtype)

def rope_tables(positions):
    inv = ROPE_THETA_2 ** (-jnp.arange(0, ROT_DIM, 2, dtype=jnp.float32) / ROT_DIM)
    ang = positions.astype(jnp.float32)[..., None] * inv
    return jnp.cos(ang), jnp.sin(ang)

def partial_rope(t, cos, sin):
    half = ROT_DIM // 2
    cs = cos[:, :, None, :].astype(t.dtype)
    sn = sin[:, :, None, :].astype(t.dtype)
    x1 = t[..., :half]
    x2 = t[..., half:ROT_DIM]
    return jnp.concatenate([x1 * cs - x2 * sn, x2 * cs + x1 * sn, t[..., ROT_DIM:]], axis=-1)

def dsa_attention(q, k, v, q_idx, k_idx, w_idx):
    B, S = q.shape[0], q.shape[1]
    topk = min(TOPK_MAX, S // 4)
    n_blk = S // Q_BLOCK
    key_chunk = jnp.arange(S) // CHUNK_2
    scale = HEAD_DIM ** -0.5
    kf = k_idx.astype(jnp.float32)
    gather = jax.vmap(lambda arr, ix: arr[ix])

    def block(i):
        start = i * Q_BLOCK
        qs = lax.dynamic_slice_in_dim(q, start, Q_BLOCK, axis=1)
        qis = lax.dynamic_slice_in_dim(q_idx, start, Q_BLOCK, axis=1).astype(jnp.float32)
        ws = lax.dynamic_slice_in_dim(w_idx, start, Q_BLOCK, axis=1).astype(jnp.float32)
        q_chunk = (start + jnp.arange(Q_BLOCK)) // CHUNK_2
        idx_scores = jnp.einsum('bqhs,bqh->bqs',
                                jax.nn.relu(jnp.einsum('bqhd,bsd->bqhs', qis, kf)), ws)
        adm = key_chunk[None, :] <= q_chunk[:, None]
        idx_scores = jnp.where(adm[None], idx_scores, -jnp.inf)
        _, sel = lax.top_k(idx_scores, topk)
        valid = (sel // CHUNK_2) <= q_chunk[None, :, None]
        k_sel = gather(k, sel)
        v_sel = gather(v, sel)
        logits = jnp.einsum('bqhd,bqkhd->bhqk', qs, k_sel).astype(jnp.float32) * scale
        logits = jnp.where(valid[:, None], logits, -jnp.inf)
        p = jax.nn.softmax(logits, axis=-1).astype(v.dtype)
        return jnp.einsum('bhqk,bqkhd->bqhd', p, v_sel)

    out = lax.map(block, jnp.arange(n_blk))
    return jnp.moveaxis(out, 0, 1).reshape(B, S, -1)

def chunk_band_attention(q, k, v, rel_bias):
    B, S, H, Dh = q.shape
    n_c = S // CHUNK_2
    pad = PREV_CHUNKS * CHUNK_2
    qc = q.reshape(B, n_c, CHUNK_2, H, Dh)
    kp = jnp.pad(k, ((0, 0), (pad, 0), (0, 0), (0, 0))).reshape(B, n_c + PREV_CHUNKS, CHUNK_2, H, Dh)
    vp = jnp.pad(v, ((0, 0), (pad, 0), (0, 0), (0, 0))).reshape(B, n_c + PREV_CHUNKS, CHUNK_2, H, Dh)
    kband = jnp.concatenate([kp[:, j:j + n_c] for j in range(PREV_CHUNKS + 1)], axis=2)
    vband = jnp.concatenate([vp[:, j:j + n_c] for j in range(PREV_CHUNKS + 1)], axis=2)
    logits = jnp.einsum('bcqhd,bckhd->bchqk', qc, kband).astype(jnp.float32) * (Dh ** -0.5)
    qi = jnp.arange(CHUNK_2)
    kj = jnp.arange(BAND)
    dist = jnp.clip(qi[:, None] + pad - kj[None, :], -REL_CLIP, REL_CLIP) + REL_CLIP
    bias = rel_bias[:, dist].astype(jnp.float32)
    band_chunk = jnp.arange(n_c)[:, None] - PREV_CHUNKS + kj[None, :] // CHUNK_2
    valid = band_chunk >= 0
    logits = jnp.where(valid[None, :, None, None, :], logits + bias[None, None], -jnp.inf)
    p = jax.nn.softmax(logits, axis=-1).astype(v.dtype)
    out = jnp.einsum('bchqk,bckhd->bcqhd', p, vband)
    return out.reshape(B, S, H * Dh)

def forgetting_attention(q, k, v, f_logit):
    B, S, H, Dh = q.shape
    n_blk = S // Q_BLOCK
    log_f = jax.nn.log_sigmoid(f_logit.astype(jnp.float32))
    F = jnp.moveaxis(jnp.cumsum(log_f, axis=1), 1, 2)
    key_pos = jnp.arange(S)
    scale = Dh ** -0.5

    def block(i):
        start = i * Q_BLOCK
        qs = lax.dynamic_slice_in_dim(q, start, Q_BLOCK, axis=1)
        Fq = lax.dynamic_slice_in_dim(F, start, Q_BLOCK, axis=2)
        logits = (jnp.einsum('bqhd,bshd->bhqs', qs, k).astype(jnp.float32) * scale
                  + Fq[..., :, None] - F[:, :, None, :])
        qpos = start + jnp.arange(Q_BLOCK)
        logits = jnp.where((key_pos[None, :] <= qpos[:, None])[None, None], logits, -jnp.inf)
        p = jax.nn.softmax(logits, axis=-1).astype(v.dtype)
        return jnp.einsum('bhqs,bshd->bqhd', p, v)

    out = lax.map(block, jnp.arange(n_blk))
    return jnp.moveaxis(out, 0, 1).reshape(B, S, H * Dh)

def hybrid_mixer(h, cos, sin, w_in, b_in, rel_bias, w_branch, w_out):
    B, S, D = h.shape
    proj = h @ w_in + b_in
    parts = []
    off = 0
    for size in SPLIT_SIZES:
        parts.append(proj[..., off:off + size])
        off += size
    qa, ka, va, qi, ki, wi, qkv_b, qkv_c, f_c, gate_logits = parts
    qa = partial_rope(qa.reshape(B, S, N_HEADS_A, HEAD_DIM), cos, sin)
    ka = partial_rope(ka.reshape(B, S, N_HEADS_A, HEAD_DIM), cos, sin)
    va = va.reshape(B, S, N_HEADS_A, HEAD_DIM)
    qi = partial_rope(qi.reshape(B, S, IDX_HEADS, IDX_DIM), cos, sin)
    ki = partial_rope(ki[:, :, None, :], cos, sin)[:, :, 0, :]
    wi = wi * (IDX_HEADS ** -0.5 * IDX_DIM ** -0.5)
    o_a = dsa_attention(qa, ka, va, qi, ki, wi)
    qkv_b = qkv_b.reshape(B, S, 3, N_HEADS_B, HEAD_DIM)
    o_b = chunk_band_attention(qkv_b[:, :, 0], qkv_b[:, :, 1], qkv_b[:, :, 2], rel_bias)
    qkv_c = qkv_c.reshape(B, S, 3, N_HEADS_C, HEAD_DIM)
    o_c = forgetting_attention(qkv_c[:, :, 0], qkv_c[:, :, 1], qkv_c[:, :, 2], f_c)
    gates = jax.nn.sigmoid(gate_logits.reshape(B, S, N_BRANCH, D))
    y = (gates[:, :, 0] * (o_a @ w_branch[:WIDTH_A])
         + gates[:, :, 1] * (o_b @ w_branch[WIDTH_A:WIDTH_A + WIDTH_B])
         + gates[:, :, 2] * (o_c @ w_branch[WIDTH_A + WIDTH_B:]))
    return y @ w_out

def swiglu(h, w_ffn_in, w_ffn_out):
    gu = h @ w_ffn_in
    g, u = gu[..., :FFN_HIDDEN], gu[..., FFN_HIDDEN:]
    return (jax.nn.silu(g) * u) @ w_ffn_out

def second_inputs(seed: int = 0) -> dict:
    key = jax.random.key(seed)
    ks = jax.random.split(key, 16)
    f32 = jnp.float32
    D = D_MODEL
    nrm = jax.random.normal
    x = nrm(ks[0], (BATCH, SEQ, D), f32)
    c = nrm(ks[1], (BATCH, D), f32)
    offset = jax.random.randint(ks[2], (BATCH, 1), 0, 4096, dtype=jnp.int32)
    positions = offset + jnp.arange(SEQ, dtype=jnp.int32)[None, :]
    ada_w = 0.5 * D ** -0.5 * nrm(ks[3], (DEPTH, D, 6 * D), f32)
    ada_b = 0.01 * nrm(ks[4], (DEPTH, 6 * D), f32)
    norm1_g = 1.0 + 0.05 * nrm(ks[5], (DEPTH, D), f32)
    w_in = D ** -0.5 * nrm(ks[6], (DEPTH, D, IN_WIDTH), f32)
    f_off = sum(SPLIT_SIZES[:8])
    forget_b = jax.random.uniform(ks[7], (DEPTH, N_HEADS_C), f32, FORGET_BIAS_LO, FORGET_BIAS_HI)
    b_in = (0.01 * nrm(ks[8], (DEPTH, IN_WIDTH), f32)).at[:, f_off:f_off + N_HEADS_C].add(forget_b)
    rel_bias = 0.5 * nrm(ks[9], (DEPTH, N_HEADS_B, 2 * REL_CLIP + 1), f32)
    w_branch = WIDTH_B ** -0.5 * nrm(ks[10], (DEPTH, MIX_WIDTH_2, D), f32)
    w_out = D ** -0.5 * nrm(ks[11], (DEPTH, D, D), f32)
    norm2_g = 1.0 + 0.05 * nrm(ks[12], (DEPTH, D), f32)
    w_ffn_in = D ** -0.5 * nrm(ks[13], (DEPTH, D, 2 * FFN_HIDDEN), f32)
    w_ffn_out = FFN_HIDDEN ** -0.5 * nrm(ks[14], (DEPTH, FFN_HIDDEN, D), f32)
    final_g = 1.0 + 0.05 * nrm(ks[15], (D,), f32)
    return {'x': x, 'c': c, 'positions': positions, 'ada_w': ada_w, 'ada_b': ada_b,
            'norm1_g': norm1_g, 'w_in': w_in, 'b_in': b_in, 'rel_bias': rel_bias,
            'w_branch': w_branch, 'w_out': w_out, 'norm2_g': norm2_g,
            'w_ffn_in': w_ffn_in, 'w_ffn_out': w_ffn_out, 'final_g': final_g}

def second_block(x, c, positions, ada_w, ada_b, norm1_g, w_in, b_in, rel_bias,
              w_branch, w_out, norm2_g, w_ffn_in, w_ffn_out, final_g):
    cos, sin = rope_tables(positions)
    cond = jax.nn.silu(c)
    for l in range(DEPTH):
        mod = (cond @ ada_w[l] + ada_b[l])[:, None, :]
        sh1, sc1, g1, sh2, sc2, g2 = jnp.split(mod, 6, axis=-1)
        h = rmsnorm(x, norm1_g[l]) * (1 + sc1) + sh1
        x = x + g1 * hybrid_mixer(h, cos, sin, w_in[l], b_in[l], rel_bias[l], w_branch[l], w_out[l])
        h = rmsnorm(x, norm2_g[l]) * (1 + sc2) + sh2
        x = x + g2 * swiglu(h, w_ffn_in[l], w_ffn_out[l])
    return rmsnorm(x, final_g)


def setup_inputs(seed=0):
    out = dict(first_inputs(seed))
    for name, value in second_inputs(seed + 1).items():
        if name != "x":
            out[name + "_2"] = value
    return out


def reference(
    x, c, ctx, c_ctx, w_mod, b_mod, norm1_g, w_in, ln_v_g, ln_v_b, w_s, b_s, q_norm_g, k_norm_g,
    lam_q1, lam_k1, lam_q2, lam_k2, subln_g, conv_w, conv_b, ln_c_g, ln_c_b, w_out, norm2_g,
    w_gate, w_val, ffn_conv_w, ffn_conv_b, w_down, c_2, positions_2, ada_w_2, ada_b_2,
    norm1_g_2, w_in_2, b_in_2, rel_bias_2, w_branch_2, w_out_2, norm2_g_2, w_ffn_in_2,
    w_ffn_out_2, final_g_2,
):
    x = first_block(
        x, c, ctx, c_ctx, w_mod, b_mod, norm1_g, w_in, ln_v_g, ln_v_b, w_s, b_s, q_norm_g,
        k_norm_g, lam_q1, lam_k1, lam_q2, lam_k2, subln_g, conv_w, conv_b, ln_c_g, ln_c_b,
        w_out, norm2_g, w_gate, w_val, ffn_conv_w, ffn_conv_b, w_down,
    )
    return second_block(
        x, c_2, positions_2, ada_w_2, ada_b_2, norm1_g_2, w_in_2, b_in_2, rel_bias_2,
        w_branch_2, w_out_2, norm2_g_2, w_ffn_in_2, w_ffn_out_2, final_g_2,
    )


_drawn_inputs = setup_inputs


def setup_inputs(seed=0):
    import zlib

    import numpy as np

    out = dict(_drawn_inputs(seed))
    spreads = {}
    factors = {'ln_v_g': 3.315,
     'ln_v_b': 7.24,
     'b_s': 7.297,
     'q_norm_g': 5.54,
     'k_norm_g': 5.204,
     'conv_b': 8.0,
     'ln_c_g': 4.159,
     'ln_c_b': 8.0,
     'ffn_conv_b': 4.86,
     'ada_b_2': 5.612,
     'norm1_g_2': 5.146,
     'rel_bias_2': 4.992,
     'norm2_g_2': 3.903}
    for name, (base, spread) in spreads.items():
        noise = np.random.default_rng([zlib.crc32(name.encode()), seed]).standard_normal(out[name].shape)
        drawn = base * np.exp(spread * noise) if base else spread * noise
        out[name] = __import__('jax').numpy.asarray(drawn.astype(out[name].dtype))
    for name, factor in factors.items():
        out[name] = (out[name] * factor).astype(out[name].dtype)
    return out
```

```python
import math

import numpy as np

import concourse.bass as bass
from concourse import mybir
from concourse.alu_op_type import AluOpType as ALU

F32 = mybir.dt.float32
I32 = mybir.dt.int32
ACT = mybir.ActivationFunctionType
AX = mybir.AxisListType.X

P = 128
D = 1024
KT = D // P
T = 256
TT = T // P
EPS = 1e-6
DEPTH = 2
FF = 2816
HT = FF // P
H1, V1 = 4, 128
QK1 = 64
TAPS = 31
HALO = TAPS // 2
NT2 = 6 * D // P
CHUNK = 4096
MODCHUNK = 2048
MODS_PER_LAYER = 6 * D // 256
NHA, NHB, NHC = 6, 5, 5
HD = 64
IDX_H = 8
TOPK = 64
VW = HD * (NHA + NHB + NHC)
FILL, TAKEN, TAKEN_UNDER = -3.0e38, -3.3e38, -3.2e38
MASKED = -1.0e30
ARENA = 12704


def columns(*parts):
    at, out = 0, {}
    for name, n in parts:
        out[name] = at
        at += n
    return out, at


C1, N1 = columns(("norm1", KT), ("norm2", KT), ("qg", 1), ("kg", 1), ("subg", 1), ("conv_b", 2),
                 ("lnc_g", 2), ("lnc_b", 2), ("fw", 3 * HT), ("fb", HT), ("conv_w", 2 * TAPS),
                 ("lnv_g", 256), ("lnv_b", 256), ("lam", 4 * QK1), ("b_s", 2 * P), ("w_sT", 4 * P))
B2_TILES = 21
C2, N2 = columns(("norm1", KT), ("norm2", KT), ("bin", B2_TILES), ("bgate", 3 * KT), ("bf", 1),
                 ("bv", VW), ("bwi", IDX_H), ("rel", NHB * T))
CC, NC = columns(("ident", P), ("ones", P), ("half", P), ("rot1", P), ("rot2", P), ("cos1", T),
                 ("sin1", T), ("inv", 1), ("eps", 1), ("final", KT), ("c", 3 * KT),
                 ("b_mod", 4 * NT2), ("onehot", NHC * P), ("halfpi", 1))


class Plan:

    def __init__(self):
        self.per_turn, self.released = {}, {}


class Token:

    def __init__(self, sem, count, loops):
        self.sem, self.count, self.loops = sem, count, loops


class Sem:
    def __init__(self, prog, name):
        self.prog, self.name, self.h, self.count = prog, name, prog.nc.alloc_semaphore(name), 0
        prog.sems.append(self)

    def add(self, n):
        self.count += n
        return Token(self, self.count, tuple(self.prog.loops))

    def now(self):
        return self.add(0)


TILE_CHUNKS = [("ki", "qi0", "qi1", "qi2"), ("qi3", "kb0", "kb1", "kc0"), ("kc1", "kbc4", "qb0", "qb1"),
               ("qc0", "qc1", "qbc4", "ka0"), ("ka1", "ka2", "qa0", "qa1"), ("qa2",)]


class Loop:
    def __init__(self, number, turns):
        self.number, self.turns, self.it, self.open = number, turns, None, True


class Prog:
    def __init__(self, nc, plan, final):
        self.nc, self.plan, self.final = nc, plan, final
        self.loops, self.sems, self.n_loops = [], [], 0

    def value(self, token, turns_back=0):
        v = token.count
        for loop in token.loops:
            k = self.plan.per_turn.get((token.sem.name, loop.number), 0)
            if loop.open:
                if k:
                    v = v + loop.it * k
            else:
                v = v + (loop.turns - 1) * k
        if turns_back:
            k = self.plan.per_turn.get((token.sem.name, self.loops[-1].number), 0)
            v = v - turns_back * k
        return v

    def loop(self, turns, body):
        loop = Loop(self.n_loops, turns)
        self.n_loops += 1
        start = [s.count for s in self.sems]
        with self.nc.Fori(0, turns) as it:
            loop.it = it
            self.loops.append(loop)
            body(it)
            self.loops.pop()
        loop.open = False
        for s, c in zip(self.sems, start):
            k = s.count - c
            if not self.final:
                self.plan.per_turn[(s.name, loop.number)] = k
            s.count = c + k * turns


class Engine:
    CREDIT = 2048

    def __init__(self, prog, name, e):
        self.prog, self.e, self.sem, self.seen = prog, e, Sem(prog, "steps_" + name), {}
        e.sem_inc(self.sem.h, self.CREDIT)
        self.sem.count = self.CREDIT

    def wait(self, *tokens):
        for t in tokens:
            key = (t.sem.name, t.loops)
            if t.loops == tuple(self.prog.loops) and self.seen.get(key, 0) >= t.count:
                continue
            self.e.wait_ge(t.sem.h, self.prog.value(t))
            if t.loops == tuple(self.prog.loops):
                self.seen[key] = t.count

    def did(self, instruction):
        instruction.then_inc(self.sem.h, 1)
        return self.sem.add(1)

    def dma(self, out, in_, sem):
        self.e.dma_start(out, in_).then_inc(sem.h, 16)
        return sem.add(16)


class Slot:

    def __init__(self, prog, name, ap, free=()):
        self.prog, self.name, self.ap, self.free, self.home = prog, name, ap, list(free), ()
        self.turns, self.held = None, False

    def claim(self, engine):
        engine.wait(*self.free)
        if self.prog.loops and self.home != tuple(self.prog.loops):
            for t in self.prog.plan.released.get((self.prog.loops[-1].number, self.name), []):
                sem = next(s for s in self.prog.sems if s.name == t[0])
                token = Token(sem, t[1], tuple(self.prog.loops))
                engine.e.wait_ge(sem.h, self.prog.value(token, turns_back=1))
        return self.ap

    def release(self, *tokens):
        self.free, self.home = list(tokens), tuple(self.prog.loops)
        if self.held:
            self.held = False
            self.turns.idle.append(self)
        if self.prog.loops and not self.prog.final:
            self.prog.plan.released[(self.prog.loops[-1].number, self.name)] = [
                (t.sem.name, t.count) for t in tokens]


class Turns:

    def __init__(self, slots):
        self.slots, self.idle = slots, list(slots)
        for s in slots:
            s.turns = self

    def next(self):
        s = self.idle.pop(0)
        s.held = True
        return s


def interleave(*tasks, beside=()):
    for _ in together(*tasks):
        for b in beside:
            next(b, None)


def together(*tasks):
    tasks = list(tasks)
    while tasks:
        for t in list(tasks):
            if next(t, "done") == "done":
                tasks.remove(t)
        yield


def abreast(width, tasks):
    waiting, running = list(tasks), []
    while waiting or running:
        while waiting and len(running) < width:
            running.append(waiting.pop(0))
        for t in list(running):
            if next(t, "done") == "done":
                running.remove(t)
        yield


def in_turn(*tasks):
    for t in tasks:
        yield from t


def build(nc, a, plan, final):
    g = Prog(nc, plan, final)
    PE, ACTE, V, POOL, SP = (Engine(g, n, e) for n, e in (
        ("pe", nc.tensor), ("act", nc.scalar), ("dve", nc.vector), ("pool", nc.gpsimd), ("sp", nc.sync)))
    A = ACTE

    def sb(name, *shape):
        return nc.alloc_sbuf_tensor("sb_" + name, [P, *shape], F32)

    ring = Turns([Slot(g, f"ring{i}", sb(f"ring{i}", CHUNK)) for i in range(2)])
    ring_full = [Sem(g, f"weights_landed{i}") for i in range(2)]
    modring = Turns([Slot(g, f"modring{i}", sb(f"modring{i}", MODCHUNK)) for i in range(2)])
    mod_full = [Sem(g, f"mod_weights_landed{i}") for i in range(2)]
    param_full = [Sem(g, f"params_landed{i}") for i in range(2)]
    setup_full = Sem(g, "setup_landed")
    out_full = Sem(g, "out_landed")

    x = sb("x", KT, 2 * T)
    h = sb("h", KT, 2 * T)
    mix = sb("mix", KT, 2 * T)
    h_slot, mix_slot = Slot(g, "h", h), Slot(g, "mix", mix)
    arena = sb("arena", ARENA)
    arena_slot = Slot(g, "arena", arena)
    const = sb("const", NC)
    params = [sb(f"params{i}", max(N1, N2)) for i in range(2)]
    mods = sb("mods", 4 * NT2, 2)
    acoef = sb("acoef", 2, KT)
    acoef_slot = Slot(g, "acoef", acoef)
    tmps = Turns([Slot(g, f"tmp{i}", sb(f"tmp{i}", 2 * T)) for i in range(8)])
    cols = Turns([Slot(g, f"cols{i}", sb(f"cols{i}", 16)) for i in range(16)])
    probs_t = Turns([Slot(g, f"probsT{i}", sb(f"probsT{i}", 4, T)) for i in range(2)])
    psum = nc.alloc_psum_tensor("psum", [P, 8, 512], F32)
    banks = Turns([Slot(g, f"bank{i}", psum[:, i, :]) for i in range(7)])
    mod_bank = Slot(g, "mod_bank", psum[:, 7, :])
    cos2, sin2 = sb("cos2", T), sb("sin2", T)

    def C(name, n):
        return const[:, CC[name]:CC[name] + n]

    ident, ones, half = C("ident", P), C("ones", P), C("half", P)
    eps = C("eps", 1)

    SP.dma(const[:], a["const"], setup_full)
    SP.dma(x[:, :, 0:T], a["x"], setup_full)
    s_x = SP.dma(x[:, :, T:2 * T], a["ctx"], setup_full)
    for e in (PE, A, V, POOL):
        e.wait(s_x)

    stream = {"main": 0}

    def load_chunk(index=None, src=None, width=CHUNK):
        slot = ring.next()
        n = ring.slots.index(slot)
        slot.claim(SP)
        if src is None:
            src = a["w_main"][bass.ds(index, 1)].rearrange("a p n -> p (a n)")
        return slot, SP.dma(slot.ap[:, 0:width], src, ring_full[n])

    def next_chunk():
        i = stream["main"]
        stream["main"] += 1
        return load_chunk(i)

    def btile(w, rhs, col, width=512, m=P, kts=KT, n=T, ready=None, pause=KT):
        bank = banks.next()
        bank.claim(PE)
        for k in range(kts):
            if ready is not None:
                PE.wait(ready[k])
            i = nc.tensor.matmul(bank.ap[0:m, 0:n], w[:, k * width + col:k * width + col + m],
                                 rhs[:, k, 0:n], start=k == 0, stop=k == kts - 1)
            if k % pause == pause - 1 and k < kts - 1:
                yield
        return bank, PE.did(i)

    def atile(w, lhs, tok0, col, ncols, width=512, pause=KT):
        bank = banks.next()
        bank.claim(PE)
        for k in range(KT):
            i = nc.tensor.matmul(bank.ap[:, 0:ncols], lhs[:, k, tok0:tok0 + P],
                                 w[:, k * width + col:k * width + col + ncols],
                                 start=k == 0, stop=k == KT - 1)
            if k % pause == pause - 1 and k < KT - 1:
                yield
        return bank, PE.did(i)

    c_cols = sb("c_cols", 3 * KT)
    t_c = A.did(nc.scalar.activation(c_cols[:], C("c", 3 * KT), ACT.Silu))
    V.wait(t_c)
    turn_cols = sb("turn_cols", 11, KT)
    for turn in range(11):
        v = 0 if turn < 4 else 2
        t_turn = V.did(nc.vector.tensor_copy(turn_cols[:, turn, :], c_cols[:, v * KT:(v + 1) * KT]))
    acc = Turns([Slot(g, f"modacc{i}", sb(f"modacc{i}", 256)) for i in range(4)])
    mods_done = [None]

    def load_mod_chunk(j):
        slot = modring.next()
        slot.claim(POOL)
        return slot, POOL.dma(slot.ap[:], a["w_mod"][bass.ds(j, 1)].rearrange("a p n -> p (a n)"),
                              mod_full[modring.slots.index(slot)])

    def mod_out(j, vectors, t_sum):
        V.wait(t_sum)
        for v in range(vectors):
            t_mod = V.did(nc.vector.tensor_tensor(
                mods[:, bass.ds(j * 2, 2), v], mod_bank.ap[:, 2 * v:2 * v + 2],
                const[:, bass.ds(j * 2 + CC["b_mod"], 2)], ALU.add))
        mod_bank.release(t_mod)
        mods_done[0] = t_mod

    def mod_tasks(chunks):
        sums = None
        for j, vectors in chunks:
            for k in mod_over_k(j, vectors):
                if k == KT - 2 and sums:
                    mod_over_partitions(*sums)
                    sums = None
                if isinstance(k, tuple):
                    sums = k
                    break
                yield
        if sums:
            yield
            mod_over_partitions(*sums)

    def mod_over_k(j, vectors):
        slot, landed = load_mod_chunk(j)
        V.wait(landed, t_turn)
        accs = [acc.next() for _ in vectors]
        last = [None] * len(vectors)
        for ac in accs:
            ac.claim(V)
        for k in range(KT):
            for v, cv in enumerate(vectors):
                w = slot.ap[:, k * 256:(k + 1) * 256]
                if k == 0:
                    last[v] = V.did(nc.vector.tensor_scalar(accs[v].ap[:], w, cv[:, k:k + 1], None, ALU.mult))
                else:
                    V.wait(last[v])
                    last[v] = V.did(nc.vector.scalar_tensor_tensor(
                        accs[v].ap[:], w, cv[:, k:k + 1], accs[v].ap[:], ALU.mult, ALU.add))
            if k < KT - 1:
                yield k
        slot.release(last[-1])
        yield j, accs, last

    def mod_over_partitions(j, accs, last):
        mod_bank.claim(PE)
        for v, ac in enumerate(accs):
            PE.wait(last[v])
            for t in range(2):
                i = nc.tensor.matmul(mod_bank.ap[:, 2 * v + t:2 * v + t + 1], ac.ap[:, t * P:(t + 1) * P],
                                     ones[:, 0:1], start=True, stop=True)
            t_sum = PE.did(i)
            ac.release(t_sum)
        mod_out(j, len(accs), t_sum)

    def mod_direct(j):
        slot, landed = load_mod_chunk(j)
        PE.wait(landed, t_c)
        mod_bank.claim(PE)
        both = c_cols[:, 0:2 * KT].rearrange("p (v k) -> p k v", v=2)
        for t in range(2):
            for k in range(KT):
                i = nc.tensor.matmul(mod_bank.ap[:, 0:4].rearrange("p (v t) -> p t v", t=2)[:, t, :],
                                     slot.ap[:, k * 256 + t * P:k * 256 + (t + 1) * P], both[:, k, :],
                                     start=k == 0, stop=k == KT - 1)
            yield
        t_sum = PE.did(i)
        slot.release(t_sum)
        mod_out(j, 2, t_sum)

    lat_c, ctx_c, c2 = (c_cols[:, v * KT:(v + 1) * KT] for v in range(3))

    def mod(layer, which, k, v):
        t = layer * NT2 + which * KT + k
        return mods[:, t, v:v + 1]

    def rstd_of(bank, token, n, scale, tmp=None):
        s = tmp or tmps.next()
        s.claim(A)
        A.wait(token)
        t = A.did(nc.scalar.activation(s.ap[:, 0:n], bank.ap[:, 0:n], ACT.Sqrt, bias=eps, scale=scale))
        bank.release(t)
        V.wait(t)
        return s, V.did(nc.vector.reciprocal(s.ap[:, 0:n], s.ap[:, 0:n]))

    def sum_squares(src, tiles, n, sum_matrix=None, after=()):
        bank = banks.next()
        bank.claim(PE)
        for k in range(tiles):
            sq = tmps.next()
            sq.claim(A)
            A.wait(*after)
            t = A.did(nc.scalar.activation(sq.ap[:, 0:n], src(k), ACT.Square))
            PE.wait(t)
            t = PE.did(nc.tensor.matmul(bank.ap[:, 0:n], sum_matrix if sum_matrix is not None else ones,
                                        sq.ap[:, 0:n], start=k == 0, stop=k == tiles - 1))
            sq.release(t)
        return bank, t

    sqacc = arena[:, ARENA - 2 * T:ARENA]

    def add_squares(k, n, t_x, first=False):
        V.wait(t_x)
        xs = x[:, bass.ds(k, 1), 0:n].rearrange("p a n -> p (a n)")
        if first:
            return V.did(nc.vector.tensor_tensor(sqacc[:, 0:n], xs, xs, ALU.mult))
        sq = tmps.next()
        sq.claim(V)
        t = V.did(nc.vector.tensor_tensor(sq.ap[:, 0:n], xs, xs, ALU.mult))
        V.wait(t)
        t = V.did(nc.vector.tensor_tensor(sqacc[:, 0:n], sqacc[:, 0:n], sq.ap[:, 0:n], ALU.add))
        sq.release(t)
        return t

    def x_rstd(n, t_sq):
        bank = banks.next()
        bank.claim(PE)
        PE.wait(t_sq)
        t = PE.did(nc.tensor.matmul(bank.ap[:, 0:n], ones, sqacc[:, 0:n], start=True, stop=True))
        return rstd_of(bank, t, n, 1.0 / D)

    def norm_modulated(layer, norm_g, scale_v, shift_v, n, rs, t_r):
        V.wait(mods_done[0])
        A.wait(mods_done[0])
        acoef_slot.claim(V)
        for v in range(n // T):
            base = layer * NT2 + scale_v * KT
            t_a = V.did(nc.vector.scalar_tensor_tensor(
                acoef[:, v, :], mods[:, base:base + KT, v], 1.0, norm_g, ALU.add, ALU.mult))
        V.wait(t_a, t_r)
        h_slot.claim(V)
        ready = []
        for k in range(KT):
            for v in range(n // T):
                seg = slice(v * T, (v + 1) * T)
                t = V.did(nc.vector.scalar_tensor_tensor(
                    h[:, k, seg], x[:, k, seg], acoef[:, v, k:k + 1], rs.ap[:, seg], ALU.mult, ALU.mult))
                A.wait(t)
                t_h = A.did(nc.scalar.activation(h[:, k, seg], h[:, k, seg], ACT.Identity,
                                                 bias=mod(layer, shift_v, k, v)))
            ready.append(t_h)
        rs.release(t)
        acoef_slot.release(t)
        return ready

    def residual(bank, token, k, gate, n):
        V.wait(token)
        for v in range(n // T):
            seg = slice(v * T, (v + 1) * T)
            xs = x[:, bass.ds(k, 1), seg].rearrange("p a n -> p (a n)")
            t = V.did(nc.vector.scalar_tensor_tensor(xs, bank.ap[:, seg], gate(v), xs, ALU.mult, ALU.add))
        bank.release(t)
        return t

    def project_residual(layer, which, n, src, ready):
        V.wait(mods_done[0])
        for c in range(2):
            slot, landed = next_chunk()
            PE.wait(landed)
            for i in range(4):
                k = c * 4 + i
                bank, t_pe = yield from btile(slot.ap, src, i * P, n=n, ready=ready)
                t = residual(bank, t_pe, k, lambda v: mod(layer, which, k, v), n)
                t = add_squares(k, n, t, first=k == 0)
                yield
            slot.release(t_pe)
        return t, t_pe

    hid = arena[:, 0:HT * 2 * T].rearrange("p (k n) -> p k n", k=HT)

    def feed_forward(layer, par, n, ready, mods_beside, mods_down, pause=4):
        arena_slot.claim(V)
        V.wait(mods_done[0])
        first = stream["main"]
        tokens = {}

        def gate_value(turn, i, ready=None):
            slot, landed = load_chunk(turn * 2 + (first + i))
            PE.wait(landed)
            for j in range(2):
                gate, t_gate = yield from btile(slot.ap, h, j * P, n=n, ready=ready, pause=pause)
                value, t_value = yield from btile(slot.ap, h, 256 + j * P, n=n, pause=pause)
                tile = turn * 4 + (2 * i + j)
                out = hid[:, bass.ds(tile, 1), 0:n].rearrange("p a n -> p (a n)")
                act = tmps.next()
                act.claim(A)
                A.wait(t_gate)
                if par is None:
                    t_act = A.did(nc.scalar.activation(act.ap[:, 0:n], gate.ap[:, 0:n], ACT.Silu))
                    gate.release(t_act)
                else:
                    def tap(d):
                        return par[:, bass.ds(tile * 3 + (C1["fw"] + d), 1)]
                    t_act = A.did(nc.scalar.activation(
                        act.ap[:, 0:n], gate.ap[:, 0:n], ACT.Identity,
                        bias=par[:, bass.ds(tile + C1["fb"], 1)], scale=tap(1)))
                    V.wait(t_act)
                    a3 = act.ap[:, 0:n].rearrange("p (g t) -> p g t", t=T)
                    g3 = gate.ap[:, 0:n].rearrange("p (g t) -> p g t", t=T)
                    t_tap = V.did(nc.vector.scalar_tensor_tensor(
                        a3[:, :, 1:T], g3[:, :, 0:T - 1], tap(0), a3[:, :, 1:T], ALU.mult, ALU.add))
                    V.wait(t_tap)
                    t_tap = V.did(nc.vector.scalar_tensor_tensor(
                        a3[:, :, 0:T - 1], g3[:, :, 1:T], tap(2), a3[:, :, 0:T - 1], ALU.mult, ALU.add))
                    gate.release(t_tap)
                    A.wait(t_tap)
                    t_act = A.did(nc.scalar.activation(act.ap[:, 0:n], act.ap[:, 0:n], ACT.Silu))
                V.wait(t_act, t_value)
                tokens["hid"] = V.did(nc.vector.tensor_tensor(out, act.ap[:, 0:n], value.ap[:, 0:n], ALU.mult))
                act.release(tokens["hid"])
                value.release(tokens["hid"])
                yield
            slot.release(t_value)
            tokens["pe"] = t_value

        interleave(gate_value(0, 0, ready), mods_beside(0, 0))

        def body(it):
            for i in range(2):
                interleave(gate_value(it, 1 + i), mods_beside(it, 1 + i))
        g.loop((HT // 2 - 1) // 2, body)
        h_slot.release(tokens["pe"])
        stream["main"] += HT // 2
        PE.wait(tokens["hid"])
        down = stream.setdefault("down", 0)

        def down_tile(it, i, first_of_all=False):
            slot, landed = load_chunk(width=HT * P, src=a["w_down"][bass.ds(it * 2 + (down + i), 1)]
                                      .rearrange("a p n -> p (a n)"))
            PE.wait(landed)
            bank, t = yield from btile(slot.ap, hid, 0, width=P, kts=HT, n=n, pause=2)
            slot.release(t)
            tokens["pe"] = t
            t = residual(bank, t, it * 2 + i,
                         lambda v: mods[:, bass.ds(it * 2 + (layer * NT2 + 5 * KT + i), 1), v], n)
            tokens["sq"] = add_squares(it * 2 + i, n, t, first=first_of_all)
            yield

        for i in range(2):
            interleave(down_tile(0, i, i == 0), mods_down(i))

        def down_body(it):
            for i in range(2):
                interleave(down_tile(it, 2 + i), mods_down(it * 2 + (2 + i)))
        g.loop(KT // 2 - 1, down_body)
        stream["down"] += KT
        arena_slot.release(tokens["pe"], tokens["sq"])
        return tokens["sq"]

    par_slots = [Slot(g, "params0", params[0]), Slot(g, "params1", params[1])]

    def load_params(layer):
        slot = par_slots[layer % 2]
        slot.claim(POOL)
        if layer < 2:
            return POOL.dma(slot.ap[:, 0:N1], a["p1"][layer], param_full[layer % 2])
        return POOL.dma(slot.ap[:, 0:N2], a["p2"][layer - 2], param_full[layer % 2])

    def rope(src, t_src, rot, cos, sin, out):
        bank = banks.next()
        bank.claim(PE)
        PE.wait(t_src)
        t_rot = PE.did(nc.tensor.matmul(bank.ap[:, 0:T], rot, src, start=True, stop=True))
        yield
        tc, ts = tmps.next(), tmps.next()
        tc.claim(POOL)
        POOL.wait(t_src)
        t_c = POOL.did(nc.gpsimd.tensor_tensor(tc.ap[:, 0:T], src, cos, ALU.mult))
        ts.claim(V)
        V.wait(t_rot)
        t_s = V.did(nc.vector.tensor_tensor(ts.ap[:, 0:T], bank.ap[:, 0:T], sin, ALU.mult))
        bank.release(t_s)
        yield
        V.wait(t_c, t_s)
        t = V.did(nc.vector.tensor_tensor(out, tc.ap[:, 0:T], ts.ap[:, 0:T], ALU.add))
        tc.release(t)
        ts.release(t)
        return t

    def tiles_then(jobs, last=None):
        before = last
        for product, finisher in jobs:
            got = {}

            def run(product=product):
                got["r"] = yield from product
            yield from together(run(), *([before] if before else []))
            before = finisher(*got["r"]) if finisher else None
        if before:
            yield from before

    def carve(at, *shape):
        n = 1
        for s in shape:
            n *= s
        ap = arena[:, at:at + n]
        if len(shape) == 2:
            ap = ap.rearrange("p (a b) -> p a b", a=shape[0])
        if len(shape) == 3:
            ap = ap.rearrange("p (a b c) -> p a b c", a=shape[0], b=shape[1])
        return ap, at + n

    qT, at = carve(0, H1, 2 * T)
    kT, at = carve(at, H1, 2 * T)
    vtok, at = carve(at, 2 * TT, H1 * V1)
    u, at = carve(at, 2, 2 * T)
    vg, at = carve(at, 2 * TT, 256)
    cpad, at = carve(at, 2, 2, T + 2 * HALO)
    assert at <= ARENA

    def first_layer(layer, par_full, rs, t_r, spare):
        last = layer == DEPTH - 1
        nq = T if last else 2 * T
        groups = nq // T
        lam_init = 0.8 - 0.6 * math.exp(-0.3 * layer)
        par = params[layer % 2]

        def pc(name, n, off=0):
            return par[:, C1[name] + off:C1[name] + off + n]

        for e in (PE, A, V, POOL):
            e.wait(par_full)
        ready = norm_modulated(layer, pc("norm1", KT), 1, 0, 2 * T, rs, t_r)

        dots = cols.next()
        dots.claim(V)
        prod = tmps.next()
        prod.claim(V)
        for i in range(2):
            t = V.did(nc.vector.tensor_tensor(prod.ap[:, i * QK1:(i + 1) * QK1], pc("lam", QK1, 2 * i * QK1),
                                              pc("lam", QK1, (2 * i + 1) * QK1), ALU.mult))
            V.wait(t)
            t = V.did(nc.vector.reduce_sum(dots.ap[:, i:i + 1], prod.ap[:, i * QK1:(i + 1) * QK1], AX))
        prod.release(t)
        A.wait(t)
        t = A.did(nc.scalar.activation(dots.ap[:, 2:4], dots.ap[:, 0:2], ACT.Exp))
        V.wait(t)
        t = V.did(nc.vector.tensor_tensor(dots.ap[:, 4:5], dots.ap[:, 3:4], dots.ap[:, 2:3], ALU.subtract))
        V.wait(t)
        lam_neg = sb(f"lam_neg{layer}", 2)
        t = V.did(nc.vector.tensor_scalar(lam_neg[:, 0:1], dots.ap[:, 4:5], -lam_init, None, ALU.add))
        t_lam = V.did(nc.vector.tensor_scalar(lam_neg[:, 1:2], pc("subg", 1), 1.0 - lam_init, None, ALU.mult))
        dots.release(t)
        for e in (A, V, POOL):
            arena_slot.claim(e)
            mix_slot.claim(e)
        done = {}

        def conv_inputs():
            slot, landed = next_chunk()
            PE.wait(landed)
            t_pad = V.did(nc.vector.memset(cpad[:, :, :, :], 0.0))
            V.wait(t_pad)
            for i in range(2):
                gb, t_gb = yield from btile(slot.ap, h, (2 + i) * P, n=nq, ready=ready)
                ab, t_ab = yield from btile(slot.ap, h, i * P, n=nq)
                sg = tmps.next()
                sg.claim(A)
                A.wait(t_gb)
                t_sg = A.did(nc.scalar.activation(sg.ap[:, 0:nq], gb.ap[:, 0:nq], ACT.Sigmoid))
                gb.release(t_sg)
                V.wait(t_sg, t_ab)
                done["cin"] = V.did(nc.vector.tensor_tensor(
                    cpad[:, i, 0:groups, HALO:HALO + T], ab.ap[:, 0:nq].rearrange("p (g t) -> p g t", t=T),
                    sg.ap[:, 0:nq].rearrange("p (g t) -> p g t", t=T), ALU.mult))
                ab.release(done["cin"])
                sg.release(done["cin"])
                yield
            slot.release(t_ab)

        def convolution():
            ys, ts = [], [None, None]
            for i in range(2):
                y = tmps.next()
                y.claim(V)
                ys.append(y)
            V.wait(done["cin"])
            for d in range(TAPS):
                for i in range(2):
                    y3 = ys[i].ap[:, 0:nq].rearrange("p (g t) -> p g t", t=T)
                    if d == 0:
                        ts[i] = V.did(nc.vector.tensor_scalar(y3, cpad[:, i, 0:groups, 0:T], pc("conv_w", 1, i * TAPS),
                                                              pc("conv_b", 1, i), ALU.mult, ALU.add))
                    else:
                        V.wait(ts[i])
                        ts[i] = V.did(nc.vector.scalar_tensor_tensor(
                            y3, cpad[:, i, 0:groups, d:d + T], pc("conv_w", 1, i * TAPS + d), y3, ALU.mult, ALU.add))
                yield
            PE.wait(*ts)
            bank = banks.next()
            bank.claim(PE)
            for i in range(2):
                ins = nc.tensor.matmul(bank.ap[:, 0:nq], ones, ys[i].ap[:, 0:nq], start=i == 0, stop=i == 1)
            t = PE.did(ins)
            yield
            V.wait(t)
            for i in range(2):
                t = V.did(nc.vector.scalar_tensor_tensor(ys[i].ap[:, 0:nq], bank.ap[:, 0:nq], -1.0 / 256,
                                                         ys[i].ap[:, 0:nq], ALU.mult, ALU.add))
            bank.release(t)
            yield
            bank, t = sum_squares(lambda k: ys[k].ap[:, 0:nq], 2, nq, after=[t])
            yield
            rs, t_rs = rstd_of(bank, t, nq, 1.0 / 256)
            yield
            for i in range(2):
                V.wait(t_rs)
                t = V.did(nc.vector.tensor_tensor(ys[i].ap[:, 0:nq], ys[i].ap[:, 0:nq], rs.ap[:, 0:nq], ALU.mult))
                A.wait(t)
                done["yc"] = A.did(nc.scalar.activation(mix[:, 6 + i, 0:nq], ys[i].ap[:, 0:nq], ACT.Silu,
                                                        bias=pc("lnc_b", 1, i), scale=pc("lnc_g", 1, i)))
                ys[i].release(done["yc"])
            rs.release(t)
            yield

        def qk_finish(bank, t_pe, name, hd, out, gain, n):
            A.wait(t_pe)
            raw, sq = tmps.next(), tmps.next()
            raw.claim(A)
            t_raw = A.did(nc.scalar.activation(raw.ap[:, 0:n], bank.ap[:, 0:n], ACT.Copy))
            sq.claim(A)
            t_sq = A.did(nc.scalar.activation(sq.ap[:, 0:n], bank.ap[:, 0:n], ACT.Square))
            bank.release(t_sq)
            yield
            ss = banks.next()
            ss.claim(PE)
            PE.wait(t_sq)
            t_ss = PE.did(nc.tensor.matmul(ss.ap[:, 0:n], half, sq.ap[:, 0:n], start=True, stop=True))
            yield
            rs, t_rs = rstd_of(ss, t_ss, n, 1.0 / QK1, tmp=sq)
            V.wait(t_raw, t_rs)
            t_n = V.did(nc.vector.scalar_tensor_tensor(
                raw.ap[:, 0:T], raw.ap[:, 0:T], gain, rs.ap[:, 0:T], ALU.mult, ALU.mult))
            t_c = t_n
            if n > T:
                t_c = V.did(nc.vector.scalar_tensor_tensor(
                    out[:, hd, T:n], raw.ap[:, T:n], gain, rs.ap[:, T:n], ALU.mult, ALU.mult))
            rs.release(t_c)
            yield
            done[name, hd] = yield from rope(raw.ap[:, 0:T], t_n, C("rot1", P), C("cos1", T), C("sin1", T),
                                             out[:, hd, 0:T])
            raw.release(done[name, hd])

        def in_chunk(jobs):
            slot, landed = next_chunk()
            PE.wait(landed)
            jobs = jobs(slot.ap)
            for n, (product, finisher) in enumerate(jobs):
                def run(product=product, n=n):
                    bank, t = yield from product
                    if n == len(jobs) - 1:
                        slot.release(t)
                    return bank, t
                yield run(), finisher

        def finish_value(tt):
            def f(bank, t_pe):
                A.wait(t_pe)
                done["v"] = A.did(nc.scalar.activation(vtok[:, tt, :], bank.ap[:, :], ACT.Copy))
                bank.release(done["v"])
                yield
            return f

        def gmlp():
            slot, landed = next_chunk()
            PE.wait(landed)
            for i in range(2):
                bank, t_pe = yield from btile(slot.ap, h, i * P, n=nq, pause=2)
                A.wait(t_pe)
                t_u = A.did(nc.scalar.activation(u[:, i, 0:nq], bank.ap[:, 0:nq], ACT.Gelu_apprx_tanh))
                bank.release(t_u)
                yield
            for tt in range(nq // P):
                bank, t_pe = yield from atile(slot.ap, h, tt * P, 256, 256, pause=2)
                A.wait(t_pe)
                t_vg = A.did(nc.scalar.activation(vg[:, tt, :], bank.ap[:, 0:256], ACT.Gelu_apprx_tanh))
                bank.release(t_vg)
                yield
            slot.release(t_pe)
            h_slot.release(t_pe)
            V.wait(t_vg)
            stats = [cols.next() for _ in range(nq // P)]
            for tt, st in enumerate(stats):
                st.claim(V)
                t = V.did(nc.vector.bn_stats(st.ap[:, 0:6], vg[:, tt, :]))
            V.wait(t)
            for st in stats:
                t = V.did(nc.vector.bn_aggr(st.ap[:, 6:8], st.ap[:, 0:6]))
            yield
            A.wait(t)
            for st in stats:
                t = A.did(nc.scalar.activation(st.ap[:, 8:9], st.ap[:, 7:8], ACT.Sqrt, bias=eps))
            yield
            V.wait(t)
            for st in stats:
                t = V.did(nc.vector.reciprocal(st.ap[:, 9:10], st.ap[:, 8:9]))
            V.wait(t)
            for tt, st in enumerate(stats):
                t = V.did(nc.vector.tensor_scalar(vg[:, tt, :], vg[:, tt, :], st.ap[:, 6:7], st.ap[:, 9:10],
                                                  ALU.subtract, ALU.mult))
                st.release(t)
            yield
            V.wait(t)
            for tt in range(nq // P):
                t = V.did(nc.vector.tensor_tensor(vg[:, tt, :], vg[:, tt, :], pc("lnv_g", 256), ALU.mult))
            yield
            V.wait(t)
            for tt in range(nq // P):
                t = V.did(nc.vector.tensor_tensor(vg[:, tt, :], vg[:, tt, :], pc("lnv_b", 256), ALU.add))
            yield
            PE.wait(t)
            for i in range(2):
                bank = banks.next()
                bank.claim(PE)
                for j in range(2):
                    hd = 2 * i + j
                    for tt in range(nq // P):
                        ins = nc.tensor.matmul(bank.ap[64 * j:64 * j + 64, tt * P:(tt + 1) * P],
                                               vg[:, tt, hd * 64:hd * 64 + 64], pc("w_sT", P, hd * P),
                                               start=True, stop=True)
                t = PE.did(ins)
                gated = tmps.next()
                gated.claim(V)
                V.wait(t)
                for tt in range(nq // P):
                    t = V.did(nc.vector.tensor_tensor(gated.ap[:, tt * P:(tt + 1) * P],
                                                      bank.ap[:, tt * P:(tt + 1) * P], pc("b_s", P, i * P), ALU.add))
                bank.release(t)
                V.wait(t, t_u)
                done["ya"] = V.did(nc.vector.tensor_tensor(mix[:, i, 0:nq], gated.ap[:, 0:nq], u[:, i, 0:nq], ALU.mult))
                gated.release(done["ya"])
                yield

        def diff_head(hd, qtiles, k0, nk):
            nkt = nk // P
            pt = probs_t.next()
            pt.claim(A)
            for i, qt in enumerate(qtiles):
                sm, pm = [], []
                stat = cols.next()
                stat.claim(V)
                PE.wait(done["q", hd], done["k", hd])
                for m in range(2):
                    s = banks.next()
                    s.claim(PE)
                    t_s = PE.did(nc.tensor.matmul(s.ap[:, 0:nk], qT[64 * m:64 * m + 64, hd, qt * P:(qt + 1) * P],
                                                  kT[64 * m:64 * m + 64, hd, k0:k0 + nk], start=True, stop=True))
                    sm.append((s, t_s))
                yield
                for m, (s, t_s) in enumerate(sm):
                    V.wait(t_s)
                    t = V.did(nc.vector.reduce_max(stat.ap[:, m:m + 1], s.ap[:, 0:nk], AX))
                V.wait(t)
                t = V.did(nc.vector.tensor_scalar(stat.ap[:, 2:4], stat.ap[:, 0:2], -QK1 ** -0.5, None, ALU.mult))
                yield
                A.wait(t)
                for m, (s, _) in enumerate(sm):
                    p = tmps.next()
                    p.claim(A)
                    t = A.did(nc.scalar.activation(p.ap[:, 0:nk], s.ap[:, 0:nk], ACT.Exp, bias=stat.ap[:, 2 + m:3 + m],
                                                   scale=QK1 ** -0.5, accum_out=stat.ap[:, 4 + m:5 + m]))
                    s.release(t)
                    pm.append(p)
                yield
                V.wait(t)
                t = V.did(nc.vector.reciprocal(stat.ap[:, 6:8], stat.ap[:, 4:6]))
                V.wait(t, t_lam)
                t1 = V.did(nc.vector.tensor_scalar(stat.ap[:, 8:9], stat.ap[:, 7:8], lam_neg[:, 0:1], None, ALU.mult))
                t0 = V.did(nc.vector.tensor_scalar(pm[0].ap[:, 0:nk], pm[0].ap[:, 0:nk], stat.ap[:, 6:7], None, ALU.mult))
                V.wait(t0, t1)
                t = V.did(nc.vector.scalar_tensor_tensor(pm[0].ap[:, 0:nk], pm[1].ap[:, 0:nk], stat.ap[:, 8:9],
                                                         pm[0].ap[:, 0:nk], ALU.mult, ALU.add))
                pm[1].release(t)
                stat.release(t)
                yield
                PE.wait(t)
                tr = banks.next()
                tr.claim(PE)
                for kt in range(nkt):
                    ins = nc.tensor.transpose(tr.ap[:, kt * P:(kt + 1) * P], pm[0].ap[:, kt * P:(kt + 1) * P], ident)
                t = PE.did(ins)
                pm[0].release(t)
                yield
                A.wait(t)
                t_pt = A.did(nc.scalar.activation(pt.ap[:, 0:nkt, i * P:(i + 1) * P],
                                                  tr.ap[:, 0:nk].rearrange("p (k q) -> p k q", q=P), ACT.Copy))
                tr.release(t_pt)
                yield
            PE.wait(t_pt, done["v"])
            o = banks.next()
            o.claim(PE)
            for kt in range(nkt):
                ins = nc.tensor.matmul(o.ap[:, 0:T], vtok[:, k0 // P + kt, hd * V1:(hd + 1) * V1],
                                       pt.ap[:, kt, :], start=kt == 0, stop=kt == nkt - 1)
            t = PE.did(ins)
            pt.release(t)
            yield
            V.wait(t)
            q0 = qtiles[0] * P
            done["o", hd] = V.did(nc.vector.tensor_copy(mix[:, 2 + hd, q0:q0 + T], o.ap[:, 0:T]))
            o.release(done["o", hd])
            yield

        def sub_norm(hd):
            m = mix[:, 2 + hd, 0:nq]
            bank, t = sum_squares(lambda k: m, 1, nq, after=[done["o", hd]])
            yield
            rs, t = rstd_of(bank, t, nq, 1.0 / V1)
            yield
            V.wait(t)
            done["yb", hd] = V.did(nc.vector.scalar_tensor_tensor(m, m, lam_neg[:, 1:2], rs.ap[:, 0:nq],
                                                                  ALU.mult, ALU.mult))
            rs.release(done["yb", hd])
            yield

        interleave(conv_inputs(), beside=[spare])

        def projections():
            for name, out, gain, n in (("k", kT, pc("kg", 1), 2 * T), ("q", qT, pc("qg", 1), nq)):
                yield from in_chunk(lambda w: [
                    (btile(w, h, hd * P, n=n, pause=2, ready=ready),
                     lambda bank, t, hd=hd: qk_finish(bank, t, name, hd, out, gain, n)) for hd in range(H1)])
            yield from in_chunk(lambda w: [(atile(w, h, tt * P, 0, H1 * V1, pause=2), finish_value(tt))
                                           for tt in range(2 * TT)])

        interleave(tiles_then(projections()), convolution(), beside=[spare])
        units = []
        for hd in range(H1):
            units.append(diff_head(hd, (0, 1), 0, 2 * T))
            if not last:
                units.append(diff_head(hd, (2, 3), T, T))
        interleave(abreast(2, units), gmlp(), beside=[spare])
        interleave(abreast(2, [sub_norm(hd) for hd in range(H1)]), beside=[spare])
        outs = [done["ya"], done["ya"], *(done["yb", hd] for hd in range(H1)), done["yc"], done["yc"]]
        got = {}

        def out_task():
            got["r"] = yield from project_residual(layer, 2, nq, mix, outs)
        interleave(out_task(), spare)
        t_sq, t_pe = got["r"]
        mix_slot.release(t_pe)
        arena_slot.release(t_pe, done["yc"], t_sq)
        rs, t_r = x_rstd(nq, t_sq)
        return nq, par, norm_modulated(layer, pc("norm2", KT), 4, 3, nq, rs, t_r)

    def finished(task):
        while True:
            try:
                next(task)
            except StopIteration as e:
                return e.value

    def none(*_):
        return iter(())

    interleave(in_turn(*[mod_direct(j) for j in range(0, 8, 2)]),
               mod_tasks((j, [lat_c, ctx_c]) for j in range(1, 8, 2)))
    par_tok = [load_params(0), load_params(1)]
    bank, t = sum_squares(lambda k: x[:, k, :], KT, 2 * T)
    rs, t_r = rstd_of(bank, t, 2 * T, 1.0 / D)
    spare = mod_tasks((j, [lat_c, ctx_c]) for j in range(8, 24))
    nq, par, ready = first_layer(0, par_tok[0], rs, t_r, spare)

    def beside_first(turn, i):
        n = turn * 2 + i
        cv = turn_cols[:, bass.ds(n, 1), :].rearrange("p a k -> p (a k)")
        return mod_tasks((n * 4 + (32 + m), [cv]) for m in range(4))

    t_sq = feed_forward(0, par, nq, ready, beside_first, lambda i: mod_tasks([(i + 24, [lat_c, ctx_c])]), pause=1)
    par_slots[0].release(t_sq)
    par_tok.append(load_params(2))
    rs, t_r = x_rstd(nq, t_sq)
    nq, par, ready = first_layer(1, par_tok[1], rs, t_r, iter(()))
    t_sq = feed_forward(1, par, nq, ready, lambda turn, i: iter(()) if i == 0 else
                        mod_tasks((turn * 4 + (2 * i + 74 + m), [c2]) for m in range(2)), none, pause=2)
    par_slots[1].release(t_sq)
    par_tok.append(load_params(3))

    pos_i = nc.alloc_sbuf_tensor("sb_pos", [P, T], I32)
    t = SP.dma(pos_i[:], a["pos"], setup_full)
    ang, turns_f = tmps.next(), tmps.next()
    turns_i = nc.alloc_sbuf_tensor("sb_turns", [P, T], I32)
    ang.claim(V)
    turns_f.claim(V)
    V.wait(t)
    t = V.did(nc.vector.tensor_copy(ang.ap[:, 0:T], pos_i[:]))
    V.wait(t)
    t_ang = V.did(nc.vector.tensor_scalar(ang.ap[:, 0:T], ang.ap[:, 0:T], C("inv", 1), None, ALU.mult))
    parts, rest = [], 2 * math.pi
    for bits in (8, 11, 11):
        e = 2.0 ** (math.floor(math.log2(rest)) - bits + 1)
        parts.append(math.floor(rest / e) * e)
        rest -= parts[-1]
    parts.append(rest)
    for table, shift in ((sin2, 0.0), (cos2, 0.25)):
        V.wait(t_ang)
        t = V.did(nc.vector.tensor_scalar(turns_f.ap[:, 0:T], ang.ap[:, 0:T], 1 / (2 * math.pi), shift, ALU.mult, ALU.add))
        V.wait(t)
        t = V.did(nc.vector.tensor_copy(turns_i[:], turns_f.ap[:, 0:T]))
        V.wait(t)
        t = V.did(nc.vector.tensor_copy(turns_f.ap[:, 0:T], turns_i[:]))
        V.wait(t)
        t = V.did(nc.vector.tensor_copy(table[:], ang.ap[:, 0:T]))
        for part in parts:
            V.wait(t)
            t = V.did(nc.vector.scalar_tensor_tensor(table[:], turns_f.ap[:, 0:T], -part, table[:], ALU.mult, ALU.add))
        V.wait(t)
        t = V.did(nc.vector.tensor_scalar(table[:], table[:], shift * 2 * math.pi, math.pi, ALU.add, ALU.min))
        V.wait(t)
        t = V.did(nc.vector.tensor_scalar(table[:], table[:], -math.pi, None, ALU.max))
        A.wait(t)
        t_tab = A.did(nc.scalar.activation(table[:], table[:], ACT.Sin))
    ang.release(t)
    turns_f.release(t)
    for e in (V, POOL):
        e.wait(t_tab)

    qT2, kT2 = mix[:, :, T:2 * T], h[:, :, T:2 * T]
    qiT, at = carve(0, 4, T)
    kiT, at = carve(at, T)
    v2, at = carve(at, TT, VW)
    gates, at = carve(at, 3 * KT, T)
    idx, at = carve(at, TT, T)
    work, at = carve(at, TT, T)
    wi, at = carve(at, TT, IDX_H)
    cmask, at = carve(at, NHC, 3 * P)
    fcum, at = carve(at, T)
    fcol, at = carve(at, TT, NHC)
    assert at <= ARENA, at

    def second_layer(layer, par_full, t_sq):
        par = params[layer % 2]

        def pc(name, n, off=0):
            return par[:, C2[name] + off:C2[name] + off + n]

        rel = pc("rel", NHB * T).rearrange("p (h n) -> p h n", h=NHB)
        for e in (PE, A, V, POOL):
            e.wait(par_full)
        t_rel = V.did(nc.vector.memset(rel[0:64, :, T - 64:T], MASKED))
        rs, t_r = x_rstd(T, t_sq)
        for e in (A, V, POOL):
            arena_slot.claim(e)
            mix_slot.claim(e)
            h_slot.claim(e)
        ready = norm_modulated(layer, pc("norm1", KT), 1, 0, T, rs, t_r)
        done = {}
        n5, nb = slice(0, NHC), NHB * HD

        def chunk_jobs(make):
            slot, landed = next_chunk()
            PE.wait(landed)
            jobs = make(slot.ap)
            for n, (product, finisher) in enumerate(jobs):
                def run(product=product, n=n):
                    bank, t = yield from product
                    if n == len(jobs) - 1:
                        slot.release(t)
                    return bank, t
                yield run(), finisher

        def placed(bias, out, name):
            def f(bank, t_pe):
                A.wait(t_pe)
                done[name] = A.did(nc.scalar.activation(out, bank.ap[:, 0:T], ACT.Identity, bias=pc("bin", 1, bias)))
                bank.release(done[name])
                yield
            return f

        def rotated(bias, out, name):
            def f(bank, t_pe):
                raw = tmps.next()
                raw.claim(A)
                A.wait(t_pe)
                t = A.did(nc.scalar.activation(raw.ap[:, 0:T], bank.ap[:, 0:T], ACT.Identity, bias=pc("bin", 1, bias)))
                bank.release(t)
                yield
                done[name] = yield from rope(raw.ap[:, 0:T], t, C("rot2", P), cos2[:], sin2[:], out)
                raw.release(done[name])
            return f

        def valued(tt, v0, n, name):
            def f(bank, t_pe):
                V.wait(t_pe)
                done[name] = V.did(nc.vector.tensor_tensor(v2[:, tt, v0:v0 + n], bank.ap[:, 0:n], pc("bv", n, v0), ALU.add))
                bank.release(done[name])
                yield
            return f

        def index_weights(tt):
            def f(bank, t_pe):
                V.wait(t_pe)
                t = V.did(nc.vector.tensor_tensor(wi[:, tt, :], bank.ap[:, 0:IDX_H], pc("bwi", IDX_H), ALU.add))
                bank.release(t)
                V.wait(t)
                done["wi"] = V.did(nc.vector.tensor_scalar(wi[:, tt, :], wi[:, tt, :], IDX_H ** -0.5 * HD ** -0.5,
                                                           None, ALU.mult))
                yield
            return f

        def forget_gates(bank, t_pe):
            f, e = tmps.next(), tmps.next()
            f.claim(A)
            e.claim(A)
            A.wait(t_pe)
            t = A.did(nc.scalar.activation(f.ap[n5, 0:T], bank.ap[n5, 0:T], ACT.Identity, bias=pc("bf", 1)[n5, :]))
            bank.release(t)
            A.wait(t)
            t = A.did(nc.scalar.activation(e.ap[n5, 0:T], f.ap[n5, 0:T], ACT.Abs))
            A.wait(t)
            t = A.did(nc.scalar.activation(e.ap[n5, 0:T], e.ap[n5, 0:T], ACT.Exp, scale=-1.0))
            A.wait(t)
            t = A.did(nc.scalar.activation(e.ap[n5, 0:T], e.ap[n5, 0:T], ACT.Ln, bias=ones[n5, 0:1]))
            yield
            V.wait(t)
            t = V.did(nc.vector.scalar_tensor_tensor(f.ap[n5, 0:T], f.ap[n5, 0:T], 0.0, e.ap[n5, 0:T], ALU.min, ALU.subtract))
            V.wait(t)
            t = V.did(nc.vector.memset(e.ap[n5, 0:T], 1.0))
            V.wait(t)
            t_f = V.did(nc.vector.tensor_tensor_scan(fcum[n5, :], e.ap[n5, 0:T], f.ap[n5, 0:T], 0.0, ALU.mult, ALU.add))
            f.release(t_f)
            e.release(t_f)
            yield
            PE.wait(t_f)
            for tt in range(TT):
                bank = banks.next()
                bank.claim(PE)
                t = PE.did(nc.tensor.transpose(bank.ap[:, 0:NHC], fcum[n5, tt * P:(tt + 1) * P], ident[n5, n5]))
                V.wait(t)
                t = V.did(nc.vector.tensor_copy(fcol[:, tt, :], bank.ap[:, 0:NHC]))
                bank.release(t)
                yield
            for hd in range(NHC):
                bank = banks.next()
                bank.claim(PE)
                t = PE.did(nc.tensor.matmul(bank.ap[:, 0:T], C("onehot", NHC * P)[n5, hd * P:(hd + 1) * P],
                                            fcum[n5, :], start=True, stop=True))
                yield
                A.wait(t)
                A.did(nc.scalar.activation(cmask[:, hd, 0:P], bank.ap[:, 0:P], ACT.Copy, scale=-1.0))
                t = A.did(nc.scalar.activation(cmask[:, hd, P:3 * P], bank.ap[:, 0:T], ACT.Copy, scale=-1.0))
                bank.release(t)
                POOL.wait(t)
                for c0, n, base in ((0, P, 0), (P, T, P)):
                    done["cmask"] = POOL.did(nc.gpsimd.affine_select(
                        out=cmask[:, hd, c0:c0 + n], in_=cmask[:, hd, c0:c0 + n], compare_op=ALU.is_ge,
                        fill=MASKED, base=base, pattern=[[-1, n]], channel_multiplier=1))
                yield

        def index(qt):
            nk = (qt + 1) * P
            PE.wait(done["qi3"], done["ki"], done["qi0"], done["qi1"], done["qi2"])
            for hd in range(IDX_H):
                p0 = 64 * (hd % 2)
                bank = banks.next()
                bank.claim(PE)
                t = PE.did(nc.tensor.matmul(bank.ap[:, 0:nk], qiT[p0:p0 + 64, hd // 2, qt * P:(qt + 1) * P],
                                            kiT[p0:p0 + 64, 0:nk], start=True, stop=True))
                r = tmps.next()
                r.claim(A)
                A.wait(t)
                t = A.did(nc.scalar.activation(r.ap[:, 0:nk], bank.ap[:, 0:nk], ACT.Relu))
                bank.release(t)
                yield
                V.wait(t, done["wi"])
                w = wi[:, qt, hd:hd + 1]
                if hd == 0:
                    t = V.did(nc.vector.tensor_scalar(idx[:, qt, 0:nk], r.ap[:, 0:nk], w, None, ALU.mult))
                else:
                    V.wait(t_idx)
                    t = V.did(nc.vector.scalar_tensor_tensor(idx[:, qt, 0:nk], r.ap[:, 0:nk], w, idx[:, qt, 0:nk],
                                                             ALU.mult, ALU.add))
                t_idx = t
                r.release(t)
            V.wait(t_idx)
            t = V.did(nc.vector.memset(idx[0:64, qt, nk - 64:nk], FILL))
            for _ in range(TOPK // 8):
                best = cols.next()
                best.claim(V)
                V.wait(t)
                t = V.did(nc.vector.max(best.ap[:, 0:8], idx[:, qt, 0:nk]))
                V.wait(t)
                t = V.did(nc.vector.match_replace(idx[:, qt, 0:nk], best.ap[:, 0:8], idx[:, qt, 0:nk], TAKEN))
                best.release(t)
                yield
            V.wait(t)
            done["sel"] = V.did(nc.vector.tensor_scalar(work[:, qt, 0:nk], idx[:, qt, 0:nk], TAKEN_UNDER, MASKED,
                                                        ALU.is_gt, ALU.mult))
            yield

        def head(tile, p0, vcol, bias, needs):
            rows = slice(p0, p0 + 64)
            pt = probs_t.next()
            pt.claim(A)
            PE.wait(*(done[n] for n in needs if n[0] in "qk"))
            V.wait(*(done[n] for n in needs))
            for qt in range(TT):
                nk = (qt + 1) * P
                s = banks.next()
                s.claim(PE)
                t = PE.did(nc.tensor.matmul(s.ap[:, 0:nk], qT2[rows, tile, qt * P:(qt + 1) * P],
                                            kT2[rows, tile, 0:nk], start=True, stop=True))
                yield
                lg, stat = tmps.next(), cols.next()
                lg.claim(V)
                stat.claim(V)
                V.wait(t)
                t = bias(lg.ap[:, 0:nk], s.ap[:, 0:nk], qt, nk)
                s.release(t)
                V.wait(t)
                t = V.did(nc.vector.reduce_max(stat.ap[:, 0:1], lg.ap[:, 0:nk], AX))
                V.wait(t)
                t = V.did(nc.vector.tensor_scalar(stat.ap[:, 1:2], stat.ap[:, 0:1], -1.0, None, ALU.mult))
                yield
                A.wait(t)
                p = tmps.next()
                p.claim(A)
                t = A.did(nc.scalar.activation(p.ap[:, 0:nk], lg.ap[:, 0:nk], ACT.Exp, bias=stat.ap[:, 1:2],
                                               accum_out=stat.ap[:, 2:3]))
                lg.release(t)
                yield
                V.wait(t)
                t = V.did(nc.vector.reciprocal(stat.ap[:, 3:4], stat.ap[:, 2:3]))
                V.wait(t)
                t = V.did(nc.vector.tensor_scalar(p.ap[:, 0:nk], p.ap[:, 0:nk], stat.ap[:, 3:4], None, ALU.mult))
                stat.release(t)
                yield
                PE.wait(t)
                tr = banks.next()
                tr.claim(PE)
                for kt in range(qt + 1):
                    ins = nc.tensor.transpose(tr.ap[:, kt * P:(kt + 1) * P], p.ap[:, kt * P:(kt + 1) * P], ident)
                t = PE.did(ins)
                p.release(t)
                yield
                A.wait(t)
                t_pt = A.did(nc.scalar.activation(pt.ap[:, 0:qt + 1, qt * P:(qt + 1) * P],
                                                  tr.ap[:, 0:nk].rearrange("p (k q) -> p k q", q=P), ACT.Copy))
                tr.release(t_pt)
                yield
            PE.wait(t_pt, *(done[n] for n in needs))
            o = banks.next()
            o.claim(PE)
            for qt in range(TT):
                for kt in range(qt + 1):
                    ins = nc.tensor.matmul(o.ap[rows, qt * P:(qt + 1) * P], v2[:, kt, vcol:vcol + HD],
                                           pt.ap[:, kt, qt * P:(qt + 1) * P], start=kt == 0, stop=kt == qt)
            t = PE.did(ins)
            pt.release(t)
            yield
            A.wait(t)
            done["o"] = A.did(nc.scalar.activation(mix[rows, tile, 0:T], o.ap[rows, 0:T], ACT.Copy))
            o.release(done["o"])
            yield

        def scaled_plus(table):
            def f(out, s, qt, nk):
                return V.did(nc.vector.scalar_tensor_tensor(out, s, HD ** -0.5, table(qt, nk), ALU.mult, ALU.add))
            return f

        def forget(hd):
            def f(out, s, qt, nk):
                lg = tmps.next()
                lg.claim(V)
                t = V.did(nc.vector.tensor_scalar(lg.ap[:, 0:nk], s, HD ** -0.5, fcol[:, qt, hd:hd + 1], ALU.mult, ALU.add))
                V.wait(t)
                c0 = qt * P
                t = V.did(nc.vector.tensor_tensor(out, lg.ap[:, 0:nk], cmask[:, hd, c0:c0 + nk], ALU.add))
                lg.release(t)
                return t
            return f

        places = {f"{n}{i}": (m[:, t0 + i, :]) for t0, b, c in ((0, "a", 3), (3, "b", 2), (5, "c", 2))
                  for i in range(c) for n, m in (("q" + b, qT2), ("k" + b, kT2))}
        places |= {"qbc4": qT2[:, 7, :], "kbc4": kT2[:, 7, :], "ki": kiT, **{f"qi{i}": qiT[:, i, :] for i in range(4)}}
        order = [n for chunk in TILE_CHUNKS for n in chunk]

        def tile_jobs(chunk):
            return lambda w: [(btile(w, h, i * P, pause=2, ready=ready),
                               (rotated if n[1] in "ai" else placed)(order.index(n), places[n], n))
                              for i, n in enumerate(chunk)]

        def value_jobs(col, v0, n, name):
            return lambda w: [(atile(w, h, tt * P, col, n, pause=2), valued(tt, v0, n, name)) for tt in range(TT)]

        def first_chunks():
            yield from chunk_jobs(lambda w: [
                (btile(w, h, nb + IDX_H, m=NHC, pause=2, ready=ready), forget_gates),
                *value_jobs(0, NHA * HD, nb, "vb")(w),
                *[(atile(w, h, tt * P, nb, IDX_H, pause=2), index_weights(tt)) for tt in range(TT)]])
            for chunk in TILE_CHUNKS[:2]:
                yield from chunk_jobs(tile_jobs(chunk))

        def other_chunks():
            yield from chunk_jobs(tile_jobs(TILE_CHUNKS[2]))
            yield from chunk_jobs(value_jobs(0, NHA * HD + nb, NHC * HD, "vc"))
            for chunk in TILE_CHUNKS[3:5]:
                yield from chunk_jobs(tile_jobs(chunk))
            yield from chunk_jobs(lambda w: tile_jobs(TILE_CHUNKS[5])(w) + value_jobs(P, 0, NHA * HD, "va")(w))

        def gated(j):
            def f(bank, t_pe):
                A.wait(t_pe)
                done["gates"] = A.did(nc.scalar.activation(gates[:, j, :], bank.ap[:, 0:T], ACT.Sigmoid,
                                                           bias=pc("bgate", 1, j)))
                bank.release(done["gates"])
                yield
            return f

        def gate_chunks():
            for c in range(6):
                yield from chunk_jobs(lambda w: [(btile(w, h, i * P, pause=3), gated(c * 4 + i)) for i in range(4)])

        interleave(tiles_then(first_chunks()))
        indexer = in_turn(index(0), index(1))
        interleave(tiles_then(other_chunks()), beside=[indexer])
        done["rel"] = t_rel
        bc_heads, a_heads = [], []
        for hd in range(NHB):
            tile, p0, q = (3 + hd // 2, 64 * (hd % 2), f"b{hd // 2}") if hd < 4 else (7, 0, "bc4")
            bc_heads.append(head(tile, p0, NHA * HD + hd * HD, scaled_plus(lambda qt, nk, hd=hd: rel[:, hd, T - nk:T]),
                                 ("q" + q, "k" + q, "rel", "vb")))
        for hd in range(NHC):
            tile, p0, q = (5 + hd // 2, 64 * (hd % 2), f"c{hd // 2}") if hd < 4 else (7, 64, "bc4")
            bc_heads.append(head(tile, p0, (NHA + NHB) * HD + hd * HD, forget(hd), ("q" + q, "k" + q, "cmask", "vc")))
        for hd in range(NHA):
            a_heads.append(head(hd // 2, 64 * (hd % 2), hd * HD, scaled_plus(lambda qt, nk: work[:, qt, 0:nk]),
                                (f"qa{hd // 2}", f"ka{hd // 2}", "sel", "va")))
        interleave(tiles_then(gate_chunks()), abreast(2, bc_heads), in_turn(indexer, abreast(2, a_heads)))

        h_slot.release(PE.sem.now())
        PE.wait(done["o"])
        V.wait(done["gates"])
        h_slot.claim(V)
        y_ready = []
        for c in range(2):
            slot, landed = next_chunk()
            PE.wait(landed)
            for i in range(4):
                j = c * 4 + i
                parts = []
                for br, kts in enumerate((((0, 0, P), (1, 0, P), (2, 0, P)), ((3, 0, P), (4, 0, P), (7, 0, 64)),
                                          ((5, 0, P), (6, 0, P), (7, 64, P)))):
                    bank = banks.next()
                    bank.claim(PE)
                    for n, (k, r0, r1) in enumerate(kts):
                        ins = nc.tensor.matmul(bank.ap[:, 0:T], slot.ap[r0:r1, k * 512 + i * P:k * 512 + (i + 1) * P],
                                               mix[r0:r1, k, 0:T], start=n == 0, stop=n == 2)
                    t_pe = PE.did(ins)
                    m = tmps.next()
                    m.claim(V)
                    V.wait(t_pe)
                    t = V.did(nc.vector.tensor_tensor(m.ap[:, 0:T], bank.ap[:, 0:T], gates[:, br * KT + j, :], ALU.mult))
                    bank.release(t)
                    parts.append(m)
                V.wait(t)
                t = V.did(nc.vector.tensor_tensor(parts[0].ap[:, 0:T], parts[0].ap[:, 0:T], parts[1].ap[:, 0:T], ALU.add))
                parts[1].release(t)
                V.wait(t)
                t_y = V.did(nc.vector.tensor_tensor(h[:, j, 0:T], parts[0].ap[:, 0:T], parts[2].ap[:, 0:T], ALU.add))
                parts[0].release(t_y)
                parts[2].release(t_y)
                y_ready.append(t_y)
            slot.release(t_pe)
        mix_slot.release(t_pe)
        got = {}

        def out_task():
            got["r"] = yield from project_residual(layer, 2, T, h, y_ready)
        interleave(out_task())
        t_sq, t_pe = got["r"]
        h_slot.release(t_pe)
        arena_slot.release(t_pe, t_sq)
        rs, t_r = x_rstd(T, t_sq)
        ready = norm_modulated(layer, pc("norm2", KT), 4, 3, T, rs, t_r)
        t_sq = feed_forward(layer, None, T, ready, none, none)
        par_slots[layer % 2].release(t_sq)
        return t_sq

    tmps = Turns([Slot(g, f"half{2 * i + j}", s.ap[:, j * T:(j + 1) * T], s.free)
                  for i, s in enumerate(tmps.slots) for j in range(2)])
    probs_t = Turns([Slot(g, f"half_probsT{2 * i + j}", s.ap[:, 2 * j:2 * j + 2, :], s.free)
                     for i, s in enumerate(probs_t.slots) for j in range(2)])
    t_sq = second_layer(2, par_tok[2], t_sq)
    t_sq = second_layer(3, par_tok[3], t_sq)

    rs, t_rs = x_rstd(T, t_sq)
    V.wait(t_rs)
    h_slot.claim(V)
    for k in range(KT):
        t = V.did(nc.vector.scalar_tensor_tensor(h[:, k, 0:T], x[:, k, 0:T], const[:, CC["final"] + k:CC["final"] + k + 1],
                                                 rs.ap[:, 0:T], ALU.mult, ALU.mult))
        SP.wait(t)
        t_out = SP.dma(a["out"][:, k, :], h[:, k, 0:T], out_full)
    SP.wait(t_out)
    return g.plan


def k_major(w):
    k, n = w.shape
    return w.reshape(k // P, P, n).transpose(1, 0, 2).reshape(P, -1)


def by_column(v):
    return v.reshape(-1, P).T


def on_all(v):
    return np.broadcast_to(v.reshape(1, -1), (P, v.size))


def lay_out(i):
    i = {n: np.asarray(v) for n, v in i.items()}
    f32 = np.float32

    def padded(w, n=CHUNK):
        out = np.zeros((P, n), f32)
        out[:, :w.shape[1]] = w
        return out

    main, down = [], []
    A0, Q0, K0, V0, CV0 = 0, 512, 1024, 1536, 2048
    for l in range(DEPTH):
        w = i["w_in"][l]
        main += [k_major(w[:, c:c + 512]) for c in (CV0, K0, Q0, V0, A0)]
        main += [k_major(i["w_out"][l][:, c:c + 512]) for c in (0, 512)]
        for c in range(0, FF, 256):
            main.append(k_major(np.concatenate([i["w_gate"][l][:, c:c + 256], i["w_val"][l][:, c:c + 256]], 1)))
        down += [k_major(i["w_down"][l][:, c:c + P]) for c in range(0, D, P)]
    qa, ka, va, qi, ki, wi = 0, 384, 768, 1152, 1664, 1728
    qb, kb, vb, qc, kc, vc, fc, ga = 1736, 2056, 2376, 2696, 3016, 3336, 3656, 3661
    r = lambda c, n: list(range(c, c + n))
    cols = {"ki": r(ki, 64) + r(ki, 64), "qbc4": r(qb + 256, 64) + r(qc + 256, 64),
            "kbc4": r(kb + 256, 64) + r(kc + 256, 64)}
    for name, at in (("qi", qi), ("qa", qa), ("ka", ka), ("qb", qb), ("kb", kb), ("qc", qc), ("kc", kc)):
        cols |= {f"{name}{n}": r(at + n * P, P) for n in range(4)}
    tiles = [cols[n] for chunk in TILE_CHUNKS for n in chunk]
    chunks = [sum((cols[n] for n in chunk), []) for chunk in TILE_CHUNKS]
    chunks[5] += r(va, 384)
    chunks = [r(vb, 320) + r(wi, 8) + r(fc, 5), *chunks[:3], r(vc, 320), *chunks[3:]]
    chunks_g = [r(ga + c, 512) for c in range(0, 3 * D, 512)]
    rows = r(0, 384) + r(384, 256) + r(704, 256) + r(640, 64) + r(960, 64)

    def take(w, cols):
        out = np.zeros((D, 512), f32)
        out[:, :len(cols)] = w[:, cols]
        return k_major(out)

    for l in range(DEPTH):
        w = i["w_in_2"][l]
        main += [take(w, c) for c in chunks + chunks_g]
        wb = i["w_branch_2"][l][rows]
        main += [k_major(wb[:, c:c + 512]) for c in (0, 512)]
        main += [k_major(i["w_out_2"][l][:, c:c + 512]) for c in (0, 512)]
        wf = i["w_ffn_in_2"][l]
        for c in range(0, FF, 256):
            main.append(k_major(np.concatenate([wf[:, c:c + 256], wf[:, FF + c:FF + c + 256]], 1)))
        down += [k_major(i["w_ffn_out_2"][l][:, c:c + P]) for c in range(0, D, P)]
    mod = [k_major(w[l][:, c:c + 256]) for w in (i["w_mod"], i["ada_w_2"]) for l in range(DEPTH)
           for c in range(0, 6 * D, 256)]

    p1 = np.zeros((DEPTH, P, N1), f32)
    p2 = np.zeros((DEPTH, P, N2), f32)

    def put(dst, where, name, v):
        dst[:, where[name]:where[name] + v.shape[1]] = v

    for l in range(DEPTH):
        q = p1[l]
        put(q, C1, "norm1", by_column(i["norm1_g"][l]))
        put(q, C1, "norm2", by_column(i["norm2_g"][l]))
        put(q, C1, "qg", np.concatenate([i["q_norm_g"][l]] * 2)[:, None])
        put(q, C1, "kg", np.concatenate([i["k_norm_g"][l]] * 2)[:, None])
        put(q, C1, "subg", i["subln_g"][l][:, None])
        put(q, C1, "conv_b", by_column(i["conv_b"][l]))
        put(q, C1, "lnc_g", by_column(i["ln_c_g"][l]))
        put(q, C1, "lnc_b", by_column(i["ln_c_b"][l]))
        put(q, C1, "fw", i["ffn_conv_w"][l].reshape(3, HT, P).transpose(2, 1, 0).reshape(P, -1))
        put(q, C1, "fb", by_column(i["ffn_conv_b"][l]))
        put(q, C1, "conv_w", i["conv_w"][l].reshape(TAPS, 2, P).transpose(2, 1, 0).reshape(P, -1))
        put(q, C1, "lnv_g", on_all(i["ln_v_g"][l]))
        put(q, C1, "lnv_b", on_all(i["ln_v_b"][l]))
        put(q, C1, "lam", on_all(np.concatenate([i[n][l] for n in ("lam_q1", "lam_k1", "lam_q2", "lam_k2")])))
        bs = np.repeat(i["b_s"][l].reshape(2, 2, P), 64, axis=1)
        put(q, C1, "b_s", bs.transpose(1, 0, 2).reshape(P, -1))
        put(q, C1, "w_sT", i["w_s"][l].transpose(2, 0, 1).reshape(P, -1))
        q = p2[l]
        b = i["b_in_2"][l]
        put(q, C2, "norm1", by_column(i["norm1_g_2"][l]))
        put(q, C2, "norm2", by_column(i["norm2_g_2"][l]))
        put(q, C2, "bin", np.stack([b[t] for t in tiles], 1))
        put(q, C2, "bgate", by_column(b[ga:ga + 3 * D]))
        q[0:NHC, C2["bf"]] = b[fc:fc + NHC]
        put(q, C2, "bv", on_all(np.concatenate([b[va:va + 384], b[vb:vb + 320], b[vc:vc + 320]])))
        put(q, C2, "bwi", on_all(b[wi:wi + IDX_H]))
        apart = np.minimum(np.arange(P)[:, None] + P - np.arange(T)[None], 128) + 128
        put(q, C2, "rel", i["rel_bias_2"][l][:, apart].transpose(1, 0, 2).reshape(P, -1))
    const = np.zeros((P, NC), f32)
    put(const, CC, "ident", np.eye(P, dtype=f32))
    put(const, CC, "ones", np.ones((P, P), f32))
    put(const, CC, "half", np.kron(np.eye(2), np.ones((64, 64))).astype(f32))
    rot1, rot2 = np.zeros((P, P), f32), np.zeros((P, P), f32)
    for blk in range(0, P, 32):
        for j in range(16):
            rot1[blk + 16 + j, blk + j], rot1[blk + j, blk + 16 + j] = -1, 1
    for blk in range(0, P, 64):
        for j in range(8):
            rot2[blk + 8 + j, blk + j], rot2[blk + j, blk + 8 + j] = -1, 1
    put(const, CC, "rot1", rot1)
    put(const, CC, "rot2", rot2)
    n = np.arange(T)
    inv1 = (10000.0 ** (-np.arange(0, 32, 2, dtype=np.float64) / 32)).astype(f32)
    ang = np.zeros((P, T), f32)
    for p in range(P):
        axis, j = (p % 64) // 32, p % 16
        ang[p] = ((n // 64) if axis == 0 else (n % 64)).astype(f32) * inv1[j]
    put(const, CC, "cos1", np.cos(ang.astype(np.float64)).astype(f32))
    put(const, CC, "sin1", np.sin(ang.astype(np.float64)).astype(f32))
    inv2 = (500000.0 ** (-np.arange(0, 16, 2, dtype=np.float64) / 16)).astype(f32)
    for p in range(P):
        if p % 64 < 16:
            const[p, CC["inv"]] = inv2[p % 8]
    const[:, CC["eps"]] = EPS
    put(const, CC, "final", by_column(i["final_g_2"]))
    put(const, CC, "c", np.concatenate([by_column(i["c"][0]), by_column(i["c_ctx"]), by_column(i["c_2"][0])], 1))
    put(const, CC, "b_mod", np.concatenate([by_column(b[l]) for b in (i["b_mod"], i["ada_b_2"]) for l in range(DEPTH)], 1))
    for hd in range(NHC):
        const[hd, CC["onehot"] + hd * P:CC["onehot"] + (hd + 1) * P] = 1

    tokens = lambda t: np.ascontiguousarray(t[0].T.reshape(KT, P, T).transpose(1, 0, 2))
    return {
        "w_main": np.stack(main), "w_down": np.stack(down), "w_mod": np.stack(mod), "p1": p1, "p2": p2,
        "const": const, "x": tokens(i["x"]), "ctx": tokens(i["ctx"]),
        "pos": np.ascontiguousarray(np.broadcast_to(i["positions_2"].astype(np.int32), (P, T))),
    }


def kernel(**inputs):
    import concourse.bacc as bacc
    from concourse.bass_utils import run_bass_kernel_spmd

    arrays = lay_out(inputs)
    plan = Plan()
    for final in (False, True):
        nc = bacc.Bacc("TRN2", target_bir_lowering=False, num_devices=1)
        aps = {n: nc.dram_tensor(n, list(v.shape), mybir.dt.from_np(v.dtype), kind="ExternalInput").ap()
               for n, v in arrays.items()}
        aps["out"] = nc.dram_tensor("out", [P, KT, T], F32, kind="ExternalOutput").ap()
        build(nc, aps, plan, final)
    r = run_bass_kernel_spmd(nc, [arrays], core_ids=[0])
    out = r.results[0]["out"]
    return np.ascontiguousarray(out.transpose(1, 0, 2).reshape(D, T).T)[None]
```

```python
import math

import numpy as np

import concourse.bass as bass
from concourse import mybir
from concourse.alu_op_type import AluOpType as ALU

F32 = mybir.dt.float32
F32R = mybir.dt.float32r
I32 = mybir.dt.int32
ACT = mybir.ActivationFunctionType
AX = mybir.AxisListType.X

P = 128
D = 1024
KT = D // P
T = 256
TT = T // P
EPS = 1e-6
DEPTH = 2
FF = 2816
HT = FF // P
H1, V1 = 4, 128
QK1 = 64
TAPS = 31
HALO = TAPS // 2
NT2 = 6 * D // P
CHUNK = 4096
GROUP = KT * P
FCHUNK = 2 * GROUP
DOWN_K = HT // 2
DOWN_KS = (0, 6, DOWN_K)
MODCHUNK = 2048
MODS_PER_LAYER = 6 * D // 256
NHA, NHB, NHC = 6, 5, 5
HD = 64
IDX_H = 8
TOPK = 64
VW = HD * (NHA + NHB + NHC)
FILL, TAKEN, TAKEN_UNDER = -3.0e38, -3.3e38, -3.2e38
MASKED = -1.0e30
ARENA = 12704


def columns(*parts):
    at, out = 0, {}
    for name, n in parts:
        out[name] = at
        at += n
    return out, at


C1, N1 = columns(("norm1", KT), ("norm2", KT), ("qg", 1), ("kg", 1), ("subg", 1), ("conv_b", 2),
                 ("lnc_g", 2), ("lnc_b", 2), ("fw", 3 * HT), ("fb", HT), ("conv_w", 2 * TAPS),
                 ("lnv_g", 256), ("lnv_b", 256), ("lam", 4 * QK1), ("b_s", 2 * P), ("w_sT", 4 * P))
B2_TILES = 21
C2, N2 = columns(("norm1", KT), ("norm2", KT), ("bin", B2_TILES), ("bgate", 3 * KT), ("bf", 1),
                 ("bv", VW), ("bwi", IDX_H), ("rel", NHB * T))
CC, NC = columns(("ident", P), ("ones", P), ("half", P), ("rot1", P), ("rot2", P), ("cos1", T),
                 ("sin1", T), ("inv", 1), ("eps", 1), ("final", KT), ("c", 3 * KT),
                 ("b_mod", 4 * NT2), ("onehot", NHC * P), ("halfpi", 1))


class Plan:

    def __init__(self):
        self.per_turn, self.released = {}, {}


class Token:

    def __init__(self, sem, count, loops):
        self.sem, self.count, self.loops = sem, count, loops


class Sem:
    def __init__(self, prog, name):
        self.prog, self.name, self.h, self.count = prog, name, prog.nc.alloc_semaphore(name), 0
        prog.sems.append(self)

    def add(self, n):
        self.count += n
        return Token(self, self.count, tuple(self.prog.loops))

    def now(self):
        return self.add(0)


TILE_CHUNKS = [("ki", "qi0", "qi1", "qi2"), ("qi3", "kb0", "kb1", "kc0"), ("kc1", "kbc4", "qb0", "qb1"),
               ("qc0", "qc1", "qbc4", "ka0"), ("ka1", "ka2", "qa0", "qa1"), ("qa2",)]


class Loop:
    def __init__(self, number, turns):
        self.number, self.turns, self.it, self.open = number, turns, None, True


class Prog:
    def __init__(self, nc, plan, final):
        self.nc, self.plan, self.final = nc, plan, final
        self.loops, self.sems, self.n_loops = [], [], 0

    def value(self, token, turns_back=0):
        v = token.count
        for loop in token.loops:
            k = self.plan.per_turn.get((token.sem.name, loop.number), 0)
            if loop.open:
                if k:
                    v = v + loop.it * k
            else:
                v = v + (loop.turns - 1) * k
        if turns_back:
            k = self.plan.per_turn.get((token.sem.name, self.loops[-1].number), 0)
            v = v - turns_back * k
        return v

    def loop(self, turns, body):
        loop = Loop(self.n_loops, turns)
        self.n_loops += 1
        start = [s.count for s in self.sems]
        with self.nc.Fori(0, turns) as it:
            loop.it = it
            self.loops.append(loop)
            body(it)
            self.loops.pop()
        loop.open = False
        for s, c in zip(self.sems, start):
            k = s.count - c
            if not self.final:
                self.plan.per_turn[(s.name, loop.number)] = k
            s.count = c + k * turns


class Engine:
    CREDIT = 2048

    def __init__(self, prog, name, e):
        self.prog, self.e, self.sem, self.seen = prog, e, Sem(prog, "steps_" + name), {}
        e.sem_inc(self.sem.h, self.CREDIT)
        self.sem.count = self.CREDIT

    def wait(self, *tokens):
        for t in tokens:
            key = (t.sem.name, t.loops)
            if t.loops == tuple(self.prog.loops) and self.seen.get(key, 0) >= t.count:
                continue
            self.e.wait_ge(t.sem.h, self.prog.value(t))
            if t.loops == tuple(self.prog.loops):
                self.seen[key] = t.count

    def did(self, instruction):
        instruction.then_inc(self.sem.h, 1)
        return self.sem.add(1)

    def dma(self, out, in_, sem):
        self.e.dma_start(out, in_).then_inc(sem.h, 16)
        return sem.add(16)


class Slot:

    def __init__(self, prog, name, ap, free=()):
        self.prog, self.name, self.ap, self.free, self.home = prog, name, ap, list(free), ()
        self.turns, self.held = None, False

    def claim(self, engine):
        engine.wait(*self.free)
        if self.prog.loops and self.home != tuple(self.prog.loops):
            for t in self.prog.plan.released.get((self.prog.loops[-1].number, self.name), []):
                sem = next(s for s in self.prog.sems if s.name == t[0])
                token = Token(sem, t[1], tuple(self.prog.loops))
                engine.e.wait_ge(sem.h, self.prog.value(token, turns_back=1))
        return self.ap

    def release(self, *tokens):
        self.free, self.home = list(tokens), tuple(self.prog.loops)
        if self.held:
            self.held = False
            self.turns.idle.append(self)
        if self.prog.loops and not self.prog.final:
            self.prog.plan.released[(self.prog.loops[-1].number, self.name)] = [
                (t.sem.name, t.count) for t in tokens]


class Turns:

    def __init__(self, slots):
        self.slots, self.idle = slots, list(slots)
        for s in slots:
            s.turns = self

    def only(self, n):
        aside = self.idle[n:]
        self.idle = self.idle[:n]
        return aside

    def back(self, aside):
        self.idle += aside

    def next(self):
        s = self.idle.pop(0)
        s.held = True
        return s


def interleave(*tasks, beside=()):
    for _ in together(*tasks):
        for b in beside:
            next(b, None)


def together(*tasks):
    tasks = list(tasks)
    while tasks:
        for t in list(tasks):
            if next(t, "done") == "done":
                tasks.remove(t)
        yield


def abreast(width, tasks):
    waiting, running = list(tasks), []
    while waiting or running:
        while waiting and len(running) < width:
            running.append(waiting.pop(0))
        for t in list(running):
            if next(t, "done") == "done":
                running.remove(t)
        yield


def quickened(task, every):
    for n, _ in enumerate(task):
        if n % every:
            yield


def in_turn(*tasks):
    for t in tasks:
        yield from t


def build(nc, a, plan, final):
    g = Prog(nc, plan, final)
    PE, ACTE, V, POOL, SP = (Engine(g, n, e) for n, e in (
        ("pe", nc.tensor), ("act", nc.scalar), ("dve", nc.vector), ("pool", nc.gpsimd), ("sp", nc.sync)))
    A = ACTE

    at_byte = {}

    def sb(name, *shape):
        at_byte[name] = -(-nc.sbuf_base // 32) * 32
        return nc.alloc_sbuf_tensor("sb_" + name, [P, *shape], F32)

    def rounded(name, *shape):
        return nc.alloc_sbuf_tensor_at("r_" + name, [P, *shape], F32R, offset=at_byte[name])

    ring_mem = [sb(f"ring{i}", CHUNK) for i in range(2)]
    ring = Turns([Slot(g, f"ring{i}", ring_mem[i]) for i in range(2)])
    ring_full = [Sem(g, f"weights_landed{i}") for i in range(2)]
    ring_r = [rounded(f"ring{i}", CHUNK) for i in range(2)]
    quarter_full = [Sem(g, f"quarter_landed{i}") for i in range(4)]
    lo_made = Sem(g, "low_parts_made")
    modring = Turns([Slot(g, f"modring{i}", sb(f"modring{i}", MODCHUNK)) for i in range(2)])
    mod_full = [Sem(g, f"mod_weights_landed{i}") for i in range(2)]
    param_full = [Sem(g, f"params_landed{i}") for i in range(2)]
    setup_full = Sem(g, "setup_landed")
    out_full = Sem(g, "out_landed")

    x = sb("x", KT, 2 * T)
    h = sb("h", KT, 2 * T)
    mix = sb("mix", KT, 2 * T)
    h_slot, mix_slot = Slot(g, "h", h), Slot(g, "mix", mix)
    h_r, mix_r = rounded("h", KT, 2 * T), rounded("mix", KT, 2 * T)
    arena = sb("arena", ARENA)
    hid_r = rounded("arena", HT, 2 * T)
    arena_slot = Slot(g, "arena", arena)
    const = sb("const", NC)
    params = [sb(f"params{i}", max(N1, N2)) for i in range(2)]
    mods = sb("mods", 4 * NT2, 2)
    acoef = sb("acoef", 2, KT)
    acoef_slot = Slot(g, "acoef", acoef)
    tmps = Turns([Slot(g, f"tmp{i}", sb(f"tmp{i}", 2 * T)) for i in range(8)])
    cols = Turns([Slot(g, f"cols{i}", sb(f"cols{i}", 16)) for i in range(16)])
    probs_t = Turns([Slot(g, f"probsT{i}", sb(f"probsT{i}", 4, T)) for i in range(2)])
    probs_r = [rounded(f"probsT{i}", GROUP) for i in range(2)]
    psum = nc.alloc_psum_tensor("psum", [P, 8, 512], F32)
    banks = Turns([Slot(g, f"bank{i}", psum[:, i, :]) for i in range(7)])
    mod_bank = Slot(g, "mod_bank", psum[:, 7, :])
    cos2, sin2 = sb("cos2", T), sb("sin2", T)

    def C(name, n):
        return const[:, CC[name]:CC[name] + n]

    ident, ones, half = C("ident", P), C("ones", P), C("half", P)
    eps = C("eps", 1)

    SP.dma(const[:], a["const"], setup_full)
    SP.dma(x[:, :, 0:T], a["x"], setup_full)
    s_x = SP.dma(x[:, :, T:2 * T], a["ctx"], setup_full)
    for e in (PE, A, V, POOL):
        e.wait(s_x)

    stream = {"main": 0}

    def load_chunk(index=None, src=None, width=CHUNK):
        slot = ring.next()
        n = ring.slots.index(slot)
        slot.claim(SP)
        if src is None:
            src = a["w_main"][bass.ds(index, 1)].rearrange("a p n -> p (a n)")
        return slot, SP.dma(slot.ap[:, 0:width], src, ring_full[n])

    def next_chunk():
        i = stream["main"]
        stream["main"] += 1
        return load_chunk(i)

    def btile(w, rhs, col, width=512, m=P, kts=KT, n=T, ready=None, pause=KT):
        bank = banks.next()
        bank.claim(PE)
        for k in range(kts):
            if ready is not None:
                PE.wait(ready[k])
            i = nc.tensor.matmul(bank.ap[0:m, 0:n], w[:, k * width + col:k * width + col + m],
                                 rhs[:, k, 0:n], start=k == 0, stop=k == kts - 1)
            if k % pause == pause - 1 and k < kts - 1:
                yield
        return bank, PE.did(i)

    def atile(w, lhs, tok0, col, ncols, width=512, pause=KT):
        bank = banks.next()
        bank.claim(PE)
        for k in range(KT):
            i = nc.tensor.matmul(bank.ap[:, 0:ncols], lhs[:, k, tok0:tok0 + P],
                                 w[:, k * width + col:k * width + col + ncols],
                                 start=k == 0, stop=k == KT - 1)
            if k % pause == pause - 1 and k < KT - 1:
                yield
        return bank, PE.did(i)

    class Quarters:

        def __init__(self, his):
            self.his, self.waiting, self.landed, self.split_up = Turns(his), [], {}, []
            self.ahead = len(his) - 1
            slots = []
            for big in ring.idle + [s for s in ring.slots if s.held]:
                b = ring.slots.index(big)
                for half in range(2):
                    at = slice(half * FCHUNK, (half + 1) * FCHUNK)
                    slot = Slot(g, f"quarter{len(slots)}", ring_mem[b][:, at], big.free)
                    slot.rounded, slot.big = ring_r[b][:, at], big
                    slots.append(slot)
            self.ring = Turns(slots)

        def refresh(self):
            for slot in self.ring.slots[2:]:
                slot.free = slot.big.free

        def load(self, src, width, groups):
            slot = self.ring.next()
            slot.claim(SP)
            self.landed[slot] = SP.dma(slot.ap[:, 0:width], src, quarter_full[self.ring.slots.index(slot)])
            self.waiting += [(slot, n == len(groups) - 1, *gr) for n, gr in enumerate(groups)]

        def split(self):
            slot, last, at, stride, k0, nk = self.waiting.pop(0)

            def view(ap):
                return ap[:, at:at + nk * stride].rearrange("p (k m) -> p k m", k=nk)[:, :, 0:P] \
                    if stride == P else ap[:, :].rearrange("p (k m) -> p k m", k=nk)[:, :, at:at + P]
            hs = self.his.next()
            hs.claim(A)
            A.wait(self.landed[slot])
            hi = hs.ap[:, 0:nk * P].rearrange("p (k m) -> p k m", k=nk)
            t = A.did(nc.scalar.activation(hi, view(slot.ap), ACT.Copy))
            V.wait(t)
            nc.vector.tensor_tensor(view(slot.rounded), view(slot.ap), hi.bitcast(F32),
                                    ALU.subtract).then_inc(lo_made.h, 1)
            self.split_up.append([slot, last, hs, hi, view(slot.rounded), k0, nk, lo_made.add(1)])

        def carried(self):
            here = tuple(g.loops)
            for slot in self.landed:
                sem = quarter_full[self.ring.slots.index(slot)]
                self.landed[slot] = Token(sem, sem.count, here)
            for n, entry in enumerate(reversed(self.split_up)):
                entry[-1] = Token(lo_made, lo_made.count - n, here)
            return [e[2] for e in self.split_up]

        def products(self, bank, rhs_hi, rhs_lo, n, start, stop, ready=None, pause=3):
            while self.waiting and len(self.split_up) <= self.ahead:
                self.split()
            slot, last, hs, hi, lo, k0, nk, made = self.split_up.pop(0)
            PE.wait(made)
            for k in range(nk):
                if ready is not None:
                    PE.wait(ready[k0 + k])
                for w, z in ((hi, rhs_hi), (hi, rhs_lo), (lo, rhs_hi)):
                    i = nc.tensor.matmul(bank.ap[:, 0:n], w[:, k, :], z[:, k0 + k, :],
                                         start=start and k == 0 and z is rhs_hi and w is hi,
                                         stop=stop and k == nk - 1 and w is lo)
                if k % pause == pause - 1 and k < nk - 1:
                    yield
            t = PE.did(i)
            hs.release(t)
            if last:
                slot.release(t)
            return t

        def close(self):
            for s in probs_t.slots:
                s.free = [PE.sem.now()]
            for big in ring.slots:
                big.free = [t for s in self.ring.slots if s.big is big for t in s.free]

    c_cols = sb("c_cols", 3 * KT)
    t_c = A.did(nc.scalar.activation(c_cols[:], C("c", 3 * KT), ACT.Silu))
    V.wait(t_c)
    acc = Turns([Slot(g, f"modacc{i}", sb(f"modacc{i}", 256)) for i in range(4)])
    mods_done = [None]

    def load_mod_chunk(j):
        slot = modring.next()
        slot.claim(POOL)
        return slot, POOL.dma(slot.ap[:], a["w_mod"][bass.ds(j, 1)].rearrange("a p n -> p (a n)"),
                              mod_full[modring.slots.index(slot)])

    def mod_out(j, vectors, t_sum):
        V.wait(t_sum)
        for v in range(vectors):
            t_mod = V.did(nc.vector.tensor_tensor(
                mods[:, bass.ds(j * 2, 2), v], mod_bank.ap[:, 2 * v:2 * v + 2],
                const[:, bass.ds(j * 2 + CC["b_mod"], 2)], ALU.add))
        mod_bank.release(t_mod)
        mods_done[0] = t_mod

    def mod_tasks(chunks):
        sums = []
        for j, vectors in chunks:
            for k in mod_over_k(j, vectors):
                if isinstance(k, tuple):
                    sums.append(k)
                    break
                if k == KT - 2:
                    while sums and sum(len(s[1]) for s in sums) + len(vectors) > 2:
                        mod_over_partitions(*sums.pop(0))
                yield
        for s in sums:
            for _ in range(5):
                yield
            mod_over_partitions(*s)

    def mod_over_k(j, vectors):
        slot, landed = load_mod_chunk(j)
        V.wait(landed)
        accs = [acc.next() for _ in vectors]
        last = [None] * len(vectors)
        for ac in accs:
            ac.claim(V)
        for k in range(KT):
            for v, cv in enumerate(vectors):
                w = slot.ap[:, k * 256:(k + 1) * 256]
                if k == 0:
                    last[v] = V.did(nc.vector.tensor_scalar(accs[v].ap[:], w, cv[:, k:k + 1], None, ALU.mult))
                else:
                    V.wait(last[v])
                    last[v] = V.did(nc.vector.scalar_tensor_tensor(
                        accs[v].ap[:], w, cv[:, k:k + 1], accs[v].ap[:], ALU.mult, ALU.add))
            if k < KT - 1:
                yield k
        slot.release(last[-1])
        yield j, accs, last

    def mod_over_partitions(j, accs, last):
        mod_bank.claim(PE)
        for v, ac in enumerate(accs):
            PE.wait(last[v])
            for t in range(2):
                i = nc.tensor.matmul(mod_bank.ap[:, 2 * v + t:2 * v + t + 1], ac.ap[:, t * P:(t + 1) * P],
                                     ones[:, 0:1], start=True, stop=True)
            t_sum = PE.did(i)
            ac.release(t_sum)
        mod_out(j, len(accs), t_sum)

    def mod_direct(j):
        slot, landed = load_mod_chunk(j)
        PE.wait(landed, t_c)
        mod_bank.claim(PE)
        both = c_cols[:, 0:2 * KT].rearrange("p (v k) -> p k v", v=2)
        for t in range(2):
            for k in range(KT):
                i = nc.tensor.matmul(mod_bank.ap[:, 0:4].rearrange("p (v t) -> p t v", t=2)[:, t, :],
                                     slot.ap[:, k * 256 + t * P:k * 256 + (t + 1) * P], both[:, k, :],
                                     start=k == 0, stop=k == KT - 1)
            yield
        t_sum = PE.did(i)
        slot.release(t_sum)
        mod_out(j, 2, t_sum)

    lat_c, ctx_c, c2 = (c_cols[:, v * KT:(v + 1) * KT] for v in range(3))

    def mod(layer, which, k, v):
        t = layer * NT2 + which * KT + k
        return mods[:, t, v:v + 1]

    def rstd_of(bank, token, n, scale, tmp=None):
        s = tmp or tmps.next()
        s.claim(A)
        A.wait(token)
        t = A.did(nc.scalar.activation(s.ap[:, 0:n], bank.ap[:, 0:n], ACT.Sqrt, bias=eps, scale=scale))
        bank.release(t)
        V.wait(t)
        return s, V.did(nc.vector.reciprocal(s.ap[:, 0:n], s.ap[:, 0:n]))

    def sum_squares(src, tiles, n, sum_matrix=None, after=()):
        bank = banks.next()
        bank.claim(PE)
        for k in range(tiles):
            sq = tmps.next()
            sq.claim(A)
            A.wait(*after)
            t = A.did(nc.scalar.activation(sq.ap[:, 0:n], src(k), ACT.Square))
            PE.wait(t)
            t = PE.did(nc.tensor.matmul(bank.ap[:, 0:n], sum_matrix if sum_matrix is not None else ones,
                                        sq.ap[:, 0:n], start=k == 0, stop=k == tiles - 1))
            sq.release(t)
        return bank, t

    sqacc = arena[:, ARENA - 2 * T:ARENA]

    def add_squares(k, n, t_x, first=False):
        V.wait(t_x)
        xs = x[:, bass.ds(k, 1), 0:n].rearrange("p a n -> p (a n)")
        if first:
            return V.did(nc.vector.tensor_tensor(sqacc[:, 0:n], xs, xs, ALU.mult))
        sq = tmps.next()
        sq.claim(V)
        t = V.did(nc.vector.tensor_tensor(sq.ap[:, 0:n], xs, xs, ALU.mult))
        V.wait(t)
        t = V.did(nc.vector.tensor_tensor(sqacc[:, 0:n], sqacc[:, 0:n], sq.ap[:, 0:n], ALU.add))
        sq.release(t)
        return t

    def x_rstd(n, t_sq):
        scratch = cols.next()
        scratch.claim(A)
        scratch.release(A.did(nc.scalar.activation(scratch.ap[:, 0:1], eps, ACT.Sqrt)))
        bank = banks.next()
        bank.claim(PE)
        PE.wait(t_sq)
        t = PE.did(nc.tensor.matmul(bank.ap[:, 0:n], ones, sqacc[:, 0:n], start=True, stop=True))
        return rstd_of(bank, t, n, 1.0 / D)

    def norm_modulated(layer, norm_g, scale_v, shift_v, n, rs, t_r, parts=None):
        V.wait(mods_done[0])
        A.wait(mods_done[0])
        acoef_slot.claim(V)
        for v in range(n // T):
            base = layer * NT2 + scale_v * KT
            t_a = V.did(nc.vector.scalar_tensor_tensor(
                acoef[:, v, :], mods[:, base:base + KT, v], 1.0, norm_g, ALU.add, ALU.mult))
        V.wait(t_a, t_r)
        h_slot.claim(V)
        ready = []
        if parts:
            hi, lo = parts
            late = []

            def low_part():
                k, seg, tmp, shift, t_hi = late.pop(0)
                V.wait(t_hi)
                t_lo = V.did(nc.vector.scalar_tensor_tensor(lo[:, k, seg], tmp.ap[:, 0:T], shift,
                                                            hi[:, k, seg].bitcast(F32), ALU.add, ALU.subtract))
                tmp.release(t_lo)
                if seg.stop == n:
                    ready.append(t_lo)
            for k in range(KT):
                for v in range(n // T):
                    seg = slice(v * T, (v + 1) * T)
                    tmp, shift = tmps.next(), mod(layer, shift_v, k, v)
                    tmp.claim(V)
                    t = V.did(nc.vector.scalar_tensor_tensor(
                        tmp.ap[:, 0:T], x[:, k, seg], acoef[:, v, k:k + 1], rs.ap[:, seg], ALU.mult, ALU.mult))
                    A.wait(t)
                    t_hi = A.did(nc.scalar.activation(hi[:, k, seg], tmp.ap[:, 0:T], ACT.Identity, bias=shift))
                    late.append((k, seg, tmp, shift, t_hi))
                    if len(late) > 1:
                        low_part()
            low_part()
            rs.release(t)
            acoef_slot.release(t)
            return ready
        for k in range(KT):
            for v in range(n // T):
                seg = slice(v * T, (v + 1) * T)
                t = V.did(nc.vector.scalar_tensor_tensor(
                    h[:, k, seg], x[:, k, seg], acoef[:, v, k:k + 1], rs.ap[:, seg], ALU.mult, ALU.mult))
                A.wait(t)
                t_h = A.did(nc.scalar.activation(h[:, k, seg], h[:, k, seg], ACT.Identity,
                                                 bias=mod(layer, shift_v, k, v)))
            ready.append(t_h)
        rs.release(t)
        acoef_slot.release(t)
        return ready

    def residual(bank, token, k, gate, n):
        V.wait(token)
        for v in range(n // T):
            seg = slice(v * T, (v + 1) * T)
            xs = x[:, bass.ds(k, 1), seg].rearrange("p a n -> p (a n)")
            t = V.did(nc.vector.scalar_tensor_tensor(xs, bank.ap[:, seg], gate(v), xs, ALU.mult, ALU.add))
        bank.release(t)
        return t

    def project_residual(layer, which, n, src, ready, late=None):
        V.wait(mods_done[0])
        for c in range(2):
            slot, landed = next_chunk()
            PE.wait(landed)
            for i in range(4):
                k = c * 4 + i
                bank, t_pe = yield from btile(slot.ap, src, i * P, n=n, ready=ready)
                t = residual(bank, t_pe, k, lambda v: mod(layer, which, k, v), n)
                t = add_squares(k, n, t, first=k == 0)
                if late and k == KT - 2:
                    late()
                yield
            slot.release(t_pe)
        return t, t_pe

    hid = arena[:, 0:HT * 2 * T].rearrange("p (k n) -> p k n", k=HT)

    def gate_value_chunk(j):
        return a["w_ffn"][bass.ds(j, 1)].rearrange("a p n -> p (a n)")

    def down_chunk(j):
        return a["w_downh"][bass.ds(j, 1)].rearrange("a p n -> p (a n)")

    def ffn_parts(n):
        each = len(probs_t.slots) // 2
        his = [Slot(g, f"hi{i}", probs_r[i], [t for s in probs_t.slots[i * each:(i + 1) * each] for t in s.free])
               for i in range(2)]
        if n == 2 * T:
            return (h_r, mix_r), his
        his += [Slot(g, f"hi{i}", mix_r.rearrange("p k n -> p (k n)")[:, (i - 2) * GROUP:(i - 1) * GROUP])
                for i in (2, 3)]
        return (h_r[:, :, 0:T], h_r[:, :, T:2 * T]), his

    def feed_forward(layer, par, n, ready, parts, quarters, mods_beside, mods_down):
        arena_slot.claim(V)
        V.wait(mods_done[0])
        h_hi, h_lo = parts
        aside, accs_aside = banks.only(4), acc.only(3)
        per_turn, turns = 4, (HT - 2) // 4 - 1
        first, first_down = layer * HT, (layer - 1) * 2 * KT
        gv_groups = [(0, 2 * P, 0, KT), (P, 2 * P, 0, KT)]
        tokens, before = {}, [None]

        def finish(tile, gate, value, t_gate, t_value):
            act = tmps.next()
            act.claim(A)
            A.wait(t_gate)
            if par is None:
                t_act = A.did(nc.scalar.activation(act.ap[:, 0:n], gate.ap[:, 0:n], ACT.Silu))
                gate.release(t_act)
            else:
                def tap(d):
                    return par[:, bass.ds(tile * 3 + (C1["fw"] + d), 1)]
                t_act = A.did(nc.scalar.activation(
                    act.ap[:, 0:n], gate.ap[:, 0:n], ACT.Identity,
                    bias=par[:, bass.ds(tile + C1["fb"], 1)], scale=tap(1)))
                V.wait(t_act)
                a3 = act.ap[:, 0:n].rearrange("p (g t) -> p g t", t=T)
                g3 = gate.ap[:, 0:n].rearrange("p (g t) -> p g t", t=T)
                t_tap = V.did(nc.vector.scalar_tensor_tensor(
                    a3[:, :, 1:T], g3[:, :, 0:T - 1], tap(0), a3[:, :, 1:T], ALU.mult, ALU.add))
                V.wait(t_tap)
                t_tap = V.did(nc.vector.scalar_tensor_tensor(
                    a3[:, :, 0:T - 1], g3[:, :, 1:T], tap(2), a3[:, :, 0:T - 1], ALU.mult, ALU.add))
                gate.release(t_tap)
                yield
                A.wait(t_tap)
                t_act = A.did(nc.scalar.activation(act.ap[:, 0:n], act.ap[:, 0:n], ACT.Silu))
            yield
            V.wait(t_act, t_value)
            if n == 2 * T:
                out = hid[:, bass.ds(tile, 1), 0:n].rearrange("p a n -> p (a n)")
                tokens["hid"] = V.did(nc.vector.tensor_tensor(out, act.ap[:, 0:n], value.ap[:, 0:n], ALU.mult))
                act.release(tokens["hid"])
                value.release(tokens["hid"])
                return
            t = V.did(nc.vector.tensor_tensor(act.ap[:, 0:n], act.ap[:, 0:n], value.ap[:, 0:n], ALU.mult))
            value.release(t)
            yield
            hid_hi, hid_lo = (hid_r[:, bass.ds(tile, 1), half * T:(half + 1) * T].rearrange("p a n -> p (a n)")
                              for half in range(2))
            A.wait(t)
            t_hi = A.did(nc.scalar.activation(hid_hi, act.ap[:, 0:T], ACT.Copy))
            POOL.wait(t_hi)
            tokens["hid"] = POOL.did(nc.gpsimd.tensor_tensor(hid_lo, act.ap[:, 0:T], hid_hi.bitcast(F32), ALU.subtract))
            act.release(tokens["hid"])
            yield

        def tile_task(tile, load, ready=None):
            got = {}

            def products():
                for name, r in (("gate", ready), ("value", None)):
                    bank = banks.next()
                    bank.claim(PE)
                    got["t_" + name] = yield from quarters.products(bank, h_hi, h_lo, n, True, True, r,
                                                                    pause=1 if n == 2 * T else 2)
                    got[name] = bank
                    yield
            yield from together(products(), *([before[0]] if before[0] else []))
            tokens["pe"] = got["t_value"]
            load()
            before[0] = finish(tile, got["gate"], got["value"], got["t_gate"], got["t_value"])

        def last_finish():
            yield from before[0]
            before[0] = None

        def loads_next(j):
            return lambda: quarters.load(gate_value_chunk(j), FCHUNK, gv_groups)

        def load_down(j):
            quarters.load(down_chunk(j), DOWN_K * P,
                          [(k0 * P, P, k0, k1 - k0) for k0, k1 in zip(DOWN_KS, DOWN_KS[1:])])

        interleave(in_turn(tile_task(0, loads_next(first + 4), ready), last_finish()), mods_beside("first", 0))

        def body(it):
            held = quarters.carried()
            interleave(in_turn(*[tile_task(it * per_turn + (1 + i), loads_next(it * per_turn + (first + 5 + i)))
                                 for i in range(per_turn)], last_finish()), mods_beside("loop", it))
            assert held == [e[2] for e in quarters.split_up]
        g.loop(turns, body)

        done_tiles = 1 + turns * per_turn

        def load_after(tile):
            if tile + 4 < HT:
                return loads_next(first + tile + 4)
            if n == T:
                return lambda: load_down(first_down + tile + 4 - HT)
            return lambda: None
        interleave(in_turn(*[tile_task(tile, load_after(tile)) for tile in range(done_tiles, HT)], last_finish()),
                   mods_beside("last", 0))
        banks.back(aside)
        acc.back(accs_aside)
        h_slot.release(tokens["pe"])
        if n == 2 * T:
            mix_slot.release(tokens["pe"])
            quarters.close()
        t_zero = V.did(nc.vector.memset(sqacc[:, 0:n], 0.0))
        V.wait(t_zero)

        def add_to_x(tile, bank, t):
            t = residual(bank, t, tile,
                         lambda v: mods[:, bass.ds(tile + (layer * NT2 + 5 * KT), 1), v], n)
            tokens["sq"] = add_squares(tile, n, t)

        def down_tile(tile):
            slot, landed = load_chunk(width=HT * P, src=a["w_down"][bass.ds(tile, 1)]
                                      .rearrange("a p n -> p (a n)"))
            PE.wait(landed)
            bank, t = yield from btile(slot.ap, hid, 0, width=P, kts=HT, n=n, pause=1)
            slot.release(t)
            tokens["pe"] = t
            add_to_x(tile, bank, t)
            yield

        def split_down_tile(tile, load):
            bank = banks.next()
            bank.claim(PE)
            for half in range(2):
                for part in range(2):
                    t = yield from quarters.products(
                        bank, hid_r[:, half * DOWN_K:(half + 1) * DOWN_K, 0:T],
                        hid_r[:, half * DOWN_K:(half + 1) * DOWN_K, T:2 * T], n,
                        half == 0 and part == 0, half == 1 and part == 1)
                load(half)
            tokens["pe"] = t
            add_to_x(tile, bank, t)
            yield

        if n == T:
            PE.wait(tokens["hid"])

            def down_body(it):
                held = quarters.carried()
                for i in range(2):
                    interleave(split_down_tile(it * 2 + i, lambda half: load_down(
                        it * 4 + (first_down + 4 + 2 * i + half))))
                assert held == [e[2] for e in quarters.split_up]
            g.loop(KT // 2 - 1, down_body)
            for tile in range(KT - 2, KT):
                interleave(split_down_tile(tile, lambda half: None))
            quarters.close()
            mix_slot.release(tokens["pe"])
        else:
            PE.wait(tokens["hid"])

            def down_body(it):
                interleave(in_turn(down_tile(it * 2), down_tile(it * 2 + 1)), mods_down(it))
            g.loop(KT // 2, down_body)
        arena_slot.release(tokens["pe"], tokens["sq"])
        return tokens["sq"]

    class FeedForwardStart:

        def __init__(self, layer, n):
            self.layer, self.n = layer, n

        def load(self, chunks):
            for c in chunks:
                self.quarters.load(gate_value_chunk(self.layer * HT + c), FCHUNK,
                                   [(0, 2 * P, 0, KT), (P, 2 * P, 0, KT)])

        def early(self):
            self.parts, his = ffn_parts(self.n)
            self.quarters = Quarters(his)
            self.load((0, 1))
            for _ in range(2):
                self.quarters.split()

        def rest(self):
            self.quarters.refresh()
            self.load((2, 3))
            if self.n == T:
                for s in self.quarters.his.slots[2:]:
                    s.free = mix_slot.free
            else:
                V.wait(*mix_slot.free)
                A.wait(*mix_slot.free)
            return self.parts, self.quarters

    par_slots = [Slot(g, "params0", params[0]), Slot(g, "params1", params[1])]

    def load_params(layer):
        slot = par_slots[layer % 2]
        slot.claim(POOL)
        if layer < 2:
            return POOL.dma(slot.ap[:, 0:N1], a["p1"][layer], param_full[layer % 2])
        return POOL.dma(slot.ap[:, 0:N2], a["p2"][layer - 2], param_full[layer % 2])

    def rope(src, t_src, rot, cos, sin, out):
        bank = banks.next()
        bank.claim(PE)
        PE.wait(t_src)
        t_rot = PE.did(nc.tensor.matmul(bank.ap[:, 0:T], rot, src, start=True, stop=True))
        yield
        tc, ts = tmps.next(), tmps.next()
        tc.claim(POOL)
        POOL.wait(t_src)
        t_c = POOL.did(nc.gpsimd.tensor_tensor(tc.ap[:, 0:T], src, cos, ALU.mult))
        ts.claim(V)
        V.wait(t_rot)
        t_s = V.did(nc.vector.tensor_tensor(ts.ap[:, 0:T], bank.ap[:, 0:T], sin, ALU.mult))
        bank.release(t_s)
        yield
        V.wait(t_c, t_s)
        t = V.did(nc.vector.tensor_tensor(out, tc.ap[:, 0:T], ts.ap[:, 0:T], ALU.add))
        tc.release(t)
        ts.release(t)
        return t

    def tiles_then(jobs, last=None):
        before = last
        for product, finisher in jobs:
            got = {}

            def run(product=product):
                got["r"] = yield from product
            yield from together(run(), *([before] if before else []))
            before = finisher(*got["r"]) if finisher else None
        if before:
            yield from before

    def carve(at, *shape):
        n = 1
        for s in shape:
            n *= s
        ap = arena[:, at:at + n]
        if len(shape) == 2:
            ap = ap.rearrange("p (a b) -> p a b", a=shape[0])
        if len(shape) == 3:
            ap = ap.rearrange("p (a b c) -> p a b c", a=shape[0], b=shape[1])
        return ap, at + n

    qT, at = carve(0, H1, 2 * T)
    kT, at = carve(at, H1, 2 * T)
    vtok, at = carve(at, 2 * TT, H1 * V1)
    u, at = carve(at, 2, 2 * T)
    vg, at = carve(at, 2 * TT, 256)
    cpad, at = carve(at, 2, 2, T + 2 * HALO)
    assert at <= ARENA

    def first_layer(layer, par_full, rs, t_r, spare):
        last = layer == DEPTH - 1
        nq = T if last else 2 * T
        groups = nq // T
        lam_init = 0.8 - 0.6 * math.exp(-0.3 * layer)
        par = params[layer % 2]

        def pc(name, n, off=0):
            return par[:, C1[name] + off:C1[name] + off + n]

        for e in (PE, A, V, POOL):
            e.wait(par_full)
        ready = norm_modulated(layer, pc("norm1", KT), 1, 0, 2 * T, rs, t_r)

        dots = cols.next()
        dots.claim(V)
        prod = tmps.next()
        prod.claim(V)
        for i in range(2):
            t = V.did(nc.vector.tensor_tensor(prod.ap[:, i * QK1:(i + 1) * QK1], pc("lam", QK1, 2 * i * QK1),
                                              pc("lam", QK1, (2 * i + 1) * QK1), ALU.mult))
            V.wait(t)
            t = V.did(nc.vector.reduce_sum(dots.ap[:, i:i + 1], prod.ap[:, i * QK1:(i + 1) * QK1], AX))
        prod.release(t)
        A.wait(t)
        t = A.did(nc.scalar.activation(dots.ap[:, 2:4], dots.ap[:, 0:2], ACT.Exp))
        V.wait(t)
        t = V.did(nc.vector.tensor_tensor(dots.ap[:, 4:5], dots.ap[:, 3:4], dots.ap[:, 2:3], ALU.subtract))
        V.wait(t)
        lam_neg = sb(f"lam_neg{layer}", 2)
        t = V.did(nc.vector.tensor_scalar(lam_neg[:, 0:1], dots.ap[:, 4:5], -lam_init, None, ALU.add))
        t_lam = V.did(nc.vector.tensor_scalar(lam_neg[:, 1:2], pc("subg", 1), 1.0 - lam_init, None, ALU.mult))
        dots.release(t)
        for e in (A, V, POOL):
            arena_slot.claim(e)
            mix_slot.claim(e)
        done = {}

        def conv_inputs():
            slot, landed = next_chunk()
            PE.wait(landed)
            t_pad = V.did(nc.vector.memset(cpad[:, :, :, :], 0.0))
            V.wait(t_pad)
            for i in range(2):
                gb, t_gb = yield from btile(slot.ap, h, (2 + i) * P, n=nq, ready=ready)
                ab, t_ab = yield from btile(slot.ap, h, i * P, n=nq)
                sg = tmps.next()
                sg.claim(A)
                A.wait(t_gb)
                t_sg = A.did(nc.scalar.activation(sg.ap[:, 0:nq], gb.ap[:, 0:nq], ACT.Sigmoid))
                gb.release(t_sg)
                V.wait(t_sg, t_ab)
                done["cin"] = V.did(nc.vector.tensor_tensor(
                    cpad[:, i, 0:groups, HALO:HALO + T], ab.ap[:, 0:nq].rearrange("p (g t) -> p g t", t=T),
                    sg.ap[:, 0:nq].rearrange("p (g t) -> p g t", t=T), ALU.mult))
                ab.release(done["cin"])
                sg.release(done["cin"])
                yield
            slot.release(t_ab)

        def convolution():
            ys, ts = [], [None, None]
            for i in range(2):
                y = tmps.next()
                y.claim(V)
                ys.append(y)
            V.wait(done["cin"])
            for d in range(TAPS):
                for i in range(2):
                    y3 = ys[i].ap[:, 0:nq].rearrange("p (g t) -> p g t", t=T)
                    if d == 0:
                        ts[i] = V.did(nc.vector.tensor_scalar(y3, cpad[:, i, 0:groups, 0:T], pc("conv_w", 1, i * TAPS),
                                                              pc("conv_b", 1, i), ALU.mult, ALU.add))
                    else:
                        V.wait(ts[i])
                        ts[i] = V.did(nc.vector.scalar_tensor_tensor(
                            y3, cpad[:, i, 0:groups, d:d + T], pc("conv_w", 1, i * TAPS + d), y3, ALU.mult, ALU.add))
                yield
            PE.wait(*ts)
            bank = banks.next()
            bank.claim(PE)
            for i in range(2):
                ins = nc.tensor.matmul(bank.ap[:, 0:nq], ones, ys[i].ap[:, 0:nq], start=i == 0, stop=i == 1)
            t = PE.did(ins)
            yield
            V.wait(t)
            for i in range(2):
                t = V.did(nc.vector.scalar_tensor_tensor(ys[i].ap[:, 0:nq], bank.ap[:, 0:nq], -1.0 / 256,
                                                         ys[i].ap[:, 0:nq], ALU.mult, ALU.add))
            bank.release(t)
            yield
            bank, t = sum_squares(lambda k: ys[k].ap[:, 0:nq], 2, nq, after=[t])
            yield
            rs, t_rs = rstd_of(bank, t, nq, 1.0 / 256)
            yield
            for i in range(2):
                V.wait(t_rs)
                t = V.did(nc.vector.tensor_tensor(ys[i].ap[:, 0:nq], ys[i].ap[:, 0:nq], rs.ap[:, 0:nq], ALU.mult))
                A.wait(t)
                done["yc"] = A.did(nc.scalar.activation(mix[:, 6 + i, 0:nq], ys[i].ap[:, 0:nq], ACT.Silu,
                                                        bias=pc("lnc_b", 1, i), scale=pc("lnc_g", 1, i)))
                ys[i].release(done["yc"])
            rs.release(t)
            yield

        def qk_finish(bank, t_pe, name, hd, out, gain, n):
            A.wait(t_pe)
            raw, sq = tmps.next(), tmps.next()
            raw.claim(A)
            t_raw = A.did(nc.scalar.activation(raw.ap[:, 0:n], bank.ap[:, 0:n], ACT.Copy))
            sq.claim(A)
            t_sq = A.did(nc.scalar.activation(sq.ap[:, 0:n], bank.ap[:, 0:n], ACT.Square))
            bank.release(t_sq)
            yield
            ss = banks.next()
            ss.claim(PE)
            PE.wait(t_sq)
            t_ss = PE.did(nc.tensor.matmul(ss.ap[:, 0:n], half, sq.ap[:, 0:n], start=True, stop=True))
            yield
            rs, t_rs = rstd_of(ss, t_ss, n, 1.0 / QK1, tmp=sq)
            V.wait(t_raw, t_rs)
            t_n = V.did(nc.vector.scalar_tensor_tensor(
                raw.ap[:, 0:T], raw.ap[:, 0:T], gain, rs.ap[:, 0:T], ALU.mult, ALU.mult))
            t_c = t_n
            if n > T:
                t_c = V.did(nc.vector.scalar_tensor_tensor(
                    out[:, hd, T:n], raw.ap[:, T:n], gain, rs.ap[:, T:n], ALU.mult, ALU.mult))
            rs.release(t_c)
            yield
            done[name, hd] = yield from rope(raw.ap[:, 0:T], t_n, C("rot1", P), C("cos1", T), C("sin1", T),
                                             out[:, hd, 0:T])
            raw.release(done[name, hd])

        def in_chunk(jobs):
            slot, landed = next_chunk()
            PE.wait(landed)
            jobs = jobs(slot.ap)
            for n, (product, finisher) in enumerate(jobs):
                def run(product=product, n=n):
                    bank, t = yield from product
                    if n == len(jobs) - 1:
                        slot.release(t)
                    return bank, t
                yield run(), finisher

        def finish_value(tt):
            def f(bank, t_pe):
                A.wait(t_pe)
                done["v"] = A.did(nc.scalar.activation(vtok[:, tt, :], bank.ap[:, :], ACT.Copy))
                bank.release(done["v"])
                yield
            return f

        def gmlp():
            slot, landed = next_chunk()
            PE.wait(landed)
            for i in range(2):
                bank, t_pe = yield from btile(slot.ap, h, i * P, n=nq, pause=2)
                A.wait(t_pe)
                t_u = A.did(nc.scalar.activation(u[:, i, 0:nq], bank.ap[:, 0:nq], ACT.Gelu_apprx_tanh))
                bank.release(t_u)
                yield
            for tt in range(nq // P):
                bank, t_pe = yield from atile(slot.ap, h, tt * P, 256, 256, pause=2)
                A.wait(t_pe)
                t_vg = A.did(nc.scalar.activation(vg[:, tt, :], bank.ap[:, 0:256], ACT.Gelu_apprx_tanh))
                bank.release(t_vg)
                yield
            slot.release(t_pe)
            h_slot.release(t_pe)
            V.wait(t_vg)
            stats = [cols.next() for _ in range(nq // P)]
            for tt, st in enumerate(stats):
                st.claim(V)
                t = V.did(nc.vector.bn_stats(st.ap[:, 0:6], vg[:, tt, :]))
            V.wait(t)
            for st in stats:
                t = V.did(nc.vector.bn_aggr(st.ap[:, 6:8], st.ap[:, 0:6]))
            yield
            A.wait(t)
            for st in stats:
                t = A.did(nc.scalar.activation(st.ap[:, 8:9], st.ap[:, 7:8], ACT.Sqrt, bias=eps))
            yield
            V.wait(t)
            for st in stats:
                t = V.did(nc.vector.reciprocal(st.ap[:, 9:10], st.ap[:, 8:9]))
            V.wait(t)
            for tt, st in enumerate(stats):
                t = V.did(nc.vector.tensor_scalar(vg[:, tt, :], vg[:, tt, :], st.ap[:, 6:7], st.ap[:, 9:10],
                                                  ALU.subtract, ALU.mult))
                st.release(t)
            yield
            V.wait(t)
            for tt in range(nq // P):
                t = V.did(nc.vector.tensor_tensor(vg[:, tt, :], vg[:, tt, :], pc("lnv_g", 256), ALU.mult))
            yield
            V.wait(t)
            for tt in range(nq // P):
                t = V.did(nc.vector.tensor_tensor(vg[:, tt, :], vg[:, tt, :], pc("lnv_b", 256), ALU.add))
            yield
            PE.wait(t)
            for i in range(2):
                bank = banks.next()
                bank.claim(PE)
                for j in range(2):
                    hd = 2 * i + j
                    for tt in range(nq // P):
                        ins = nc.tensor.matmul(bank.ap[64 * j:64 * j + 64, tt * P:(tt + 1) * P],
                                               vg[:, tt, hd * 64:hd * 64 + 64], pc("w_sT", P, hd * P),
                                               start=True, stop=True)
                t = PE.did(ins)
                gated = tmps.next()
                gated.claim(V)
                V.wait(t)
                for tt in range(nq // P):
                    t = V.did(nc.vector.tensor_tensor(gated.ap[:, tt * P:(tt + 1) * P],
                                                      bank.ap[:, tt * P:(tt + 1) * P], pc("b_s", P, i * P), ALU.add))
                bank.release(t)
                V.wait(t, t_u)
                done["ya"] = V.did(nc.vector.tensor_tensor(mix[:, i, 0:nq], gated.ap[:, 0:nq], u[:, i, 0:nq], ALU.mult))
                gated.release(done["ya"])
                yield

        def diff_head(hd, qtiles, k0, nk):
            nkt = nk // P
            pt = probs_t.next()
            pt.claim(A)
            for i, qt in enumerate(qtiles):
                sm, pm = [], []
                stat = cols.next()
                stat.claim(V)
                PE.wait(done["q", hd], done["k", hd])
                for m in range(2):
                    s = banks.next()
                    s.claim(PE)
                    t_s = PE.did(nc.tensor.matmul(s.ap[:, 0:nk], qT[64 * m:64 * m + 64, hd, qt * P:(qt + 1) * P],
                                                  kT[64 * m:64 * m + 64, hd, k0:k0 + nk], start=True, stop=True))
                    sm.append((s, t_s))
                yield
                for m, (s, t_s) in enumerate(sm):
                    V.wait(t_s)
                    t = V.did(nc.vector.reduce_max(stat.ap[:, m:m + 1], s.ap[:, 0:nk], AX))
                V.wait(t)
                t = V.did(nc.vector.tensor_scalar(stat.ap[:, 2:4], stat.ap[:, 0:2], -QK1 ** -0.5, None, ALU.mult))
                yield
                A.wait(t)
                for m, (s, _) in enumerate(sm):
                    p = tmps.next()
                    p.claim(A)
                    t = A.did(nc.scalar.activation(p.ap[:, 0:nk], s.ap[:, 0:nk], ACT.Exp, bias=stat.ap[:, 2 + m:3 + m],
                                                   scale=QK1 ** -0.5, accum_out=stat.ap[:, 4 + m:5 + m]))
                    s.release(t)
                    pm.append(p)
                yield
                V.wait(t)
                t = V.did(nc.vector.reciprocal(stat.ap[:, 6:8], stat.ap[:, 4:6]))
                V.wait(t, t_lam)
                t1 = V.did(nc.vector.tensor_scalar(stat.ap[:, 8:9], stat.ap[:, 7:8], lam_neg[:, 0:1], None, ALU.mult))
                t0 = V.did(nc.vector.tensor_scalar(pm[0].ap[:, 0:nk], pm[0].ap[:, 0:nk], stat.ap[:, 6:7], None, ALU.mult))
                V.wait(t0, t1)
                t = V.did(nc.vector.scalar_tensor_tensor(pm[0].ap[:, 0:nk], pm[1].ap[:, 0:nk], stat.ap[:, 8:9],
                                                         pm[0].ap[:, 0:nk], ALU.mult, ALU.add))
                pm[1].release(t)
                stat.release(t)
                yield
                PE.wait(t)
                tr = banks.next()
                tr.claim(PE)
                for kt in range(nkt):
                    ins = nc.tensor.transpose(tr.ap[:, kt * P:(kt + 1) * P], pm[0].ap[:, kt * P:(kt + 1) * P], ident)
                t = PE.did(ins)
                pm[0].release(t)
                yield
                A.wait(t)
                t_pt = A.did(nc.scalar.activation(pt.ap[:, 0:nkt, i * P:(i + 1) * P],
                                                  tr.ap[:, 0:nk].rearrange("p (k q) -> p k q", q=P), ACT.Copy))
                tr.release(t_pt)
                yield
            PE.wait(t_pt, done["v"])
            o = banks.next()
            o.claim(PE)
            for kt in range(nkt):
                ins = nc.tensor.matmul(o.ap[:, 0:T], vtok[:, k0 // P + kt, hd * V1:(hd + 1) * V1],
                                       pt.ap[:, kt, :], start=kt == 0, stop=kt == nkt - 1)
            t = PE.did(ins)
            pt.release(t)
            yield
            V.wait(t)
            q0 = qtiles[0] * P
            done["o", hd] = V.did(nc.vector.tensor_copy(mix[:, 2 + hd, q0:q0 + T], o.ap[:, 0:T]))
            o.release(done["o", hd])
            yield

        def sub_norm(hd):
            m = mix[:, 2 + hd, 0:nq]
            bank, t = sum_squares(lambda k: m, 1, nq, after=[done["o", hd]])
            yield
            rs, t = rstd_of(bank, t, nq, 1.0 / V1)
            yield
            V.wait(t)
            done["yb", hd] = V.did(nc.vector.scalar_tensor_tensor(m, m, lam_neg[:, 1:2], rs.ap[:, 0:nq],
                                                                  ALU.mult, ALU.mult))
            rs.release(done["yb", hd])
            yield

        interleave(conv_inputs(), beside=[spare])

        def projections():
            for name, out, gain, n in (("k", kT, pc("kg", 1), 2 * T), ("q", qT, pc("qg", 1), nq)):
                yield from in_chunk(lambda w: [
                    (btile(w, h, hd * P, n=n, pause=2, ready=ready),
                     lambda bank, t, hd=hd: qk_finish(bank, t, name, hd, out, gain, n)) for hd in range(H1)])
            yield from in_chunk(lambda w: [(atile(w, h, tt * P, 0, H1 * V1, pause=2), finish_value(tt))
                                           for tt in range(2 * TT)])

        interleave(tiles_then(projections()), convolution(), beside=[spare])
        units = []
        for hd in range(H1):
            units.append(diff_head(hd, (0, 1), 0, 2 * T))
            if not last:
                units.append(diff_head(hd, (2, 3), T, T))
        interleave(abreast(2, units), gmlp(), beside=[spare])
        interleave(abreast(2, [sub_norm(hd) for hd in range(H1)]), beside=[spare])
        ffn_start = FeedForwardStart(layer, nq)
        outs = [done["ya"], done["ya"], *(done["yb", hd] for hd in range(H1)), done["yc"], done["yc"]]
        got = {}

        def out_task():
            got["r"] = yield from project_residual(layer, 2, nq, mix, outs, ffn_start.early)
        interleave(out_task(), spare)
        t_sq, t_pe = got["r"]
        mix_slot.release(t_pe)
        arena_slot.release(t_pe, done["yc"], t_sq)
        parts, quarters = ffn_start.rest()
        rs, t_r = x_rstd(nq, t_sq)
        ready = norm_modulated(layer, pc("norm2", KT), 4, 3, nq, rs, t_r, parts)
        return nq, par, ready, parts, quarters

    def finished(task):
        while True:
            try:
                next(task)
            except StopIteration as e:
                return e.value

    def none(*_):
        return iter(())

    interleave(in_turn(*[mod_direct(j) for j in range(0, 8, 2)]),
               mod_tasks((j, [lat_c, ctx_c]) for j in range(1, 8, 2)))
    par_tok = [load_params(0), load_params(1)]
    bank, t = sum_squares(lambda k: x[:, k, :], KT, 2 * T)
    rs, t_r = rstd_of(bank, t, 2 * T, 1.0 / D)
    spare = mod_tasks((j, [lat_c, ctx_c]) for j in range(8, 24))
    nq, par, ready, parts, quarters = first_layer(0, par_tok[0], rs, t_r, spare)

    def beside_first(place, turn):
        j, n = {"first": (48, 2), "loop": (turn * 6 + 50, 6), "last": (74, 8)}[place]
        return mod_tasks((j + m, [c2]) for m in range(n))

    def beside_down(turn):
        return quickened(mod_tasks([((turn * 2 + (24 + n), [lat_c, ctx_c]) if m == 0 else
                                     (turn * 4 + (31 + 2 * n + m), [lat_c])) for n in range(2) for m in range(3)]), 3)

    t_sq = feed_forward(0, par, nq, ready, parts, quarters, beside_first, beside_down)
    par_slots[0].release(t_sq)
    par_tok.append(load_params(2))
    rs, t_r = x_rstd(nq, t_sq)
    nq, par, ready, parts, quarters = first_layer(1, par_tok[1], rs, t_r, mod_tasks((j, [c2]) for j in range(82, 96)))
    t_sq = feed_forward(1, par, nq, ready, parts, quarters, none, none)
    par_slots[1].release(t_sq)
    par_tok.append(load_params(3))

    pos_i = nc.alloc_sbuf_tensor("sb_pos", [P, T], I32)
    t = SP.dma(pos_i[:], a["pos"], setup_full)
    ang, turns_f = tmps.next(), tmps.next()
    turns_i = nc.alloc_sbuf_tensor("sb_turns", [P, T], I32)
    ang.claim(V)
    turns_f.claim(V)
    V.wait(t)
    t = V.did(nc.vector.tensor_copy(ang.ap[:, 0:T], pos_i[:]))
    V.wait(t)
    t_ang = V.did(nc.vector.tensor_scalar(ang.ap[:, 0:T], ang.ap[:, 0:T], C("inv", 1), None, ALU.mult))
    parts, rest = [], 2 * math.pi
    for bits in (8, 11, 11):
        e = 2.0 ** (math.floor(math.log2(rest)) - bits + 1)
        parts.append(math.floor(rest / e) * e)
        rest -= parts[-1]
    parts.append(rest)
    for table, shift in ((sin2, 0.0), (cos2, 0.25)):
        V.wait(t_ang)
        t = V.did(nc.vector.tensor_scalar(turns_f.ap[:, 0:T], ang.ap[:, 0:T], 1 / (2 * math.pi), shift, ALU.mult, ALU.add))
        V.wait(t)
        t = V.did(nc.vector.tensor_copy(turns_i[:], turns_f.ap[:, 0:T]))
        V.wait(t)
        t = V.did(nc.vector.tensor_copy(turns_f.ap[:, 0:T], turns_i[:]))
        V.wait(t)
        t = V.did(nc.vector.tensor_copy(table[:], ang.ap[:, 0:T]))
        for part in parts:
            V.wait(t)
            t = V.did(nc.vector.scalar_tensor_tensor(table[:], turns_f.ap[:, 0:T], -part, table[:], ALU.mult, ALU.add))
        V.wait(t)
        t = V.did(nc.vector.tensor_scalar(table[:], table[:], shift * 2 * math.pi, math.pi, ALU.add, ALU.min))
        V.wait(t)
        t = V.did(nc.vector.tensor_scalar(table[:], table[:], -math.pi, None, ALU.max))
        A.wait(t)
        t_tab = A.did(nc.scalar.activation(table[:], table[:], ACT.Sin))
    ang.release(t)
    turns_f.release(t)
    for e in (V, POOL):
        e.wait(t_tab)

    qT2, kT2 = mix[:, :, T:2 * T], h[:, :, T:2 * T]
    qiT, at = carve(0, 4, T)
    kiT, at = carve(at, T)
    v2, at = carve(at, TT, VW)
    gates, at = carve(at, 3 * KT, T)
    idx, at = carve(at, TT, T)
    work, at = carve(at, TT, T)
    wi, at = carve(at, TT, IDX_H)
    cmask, at = carve(at, NHC, 3 * P)
    fcum, at = carve(at, T)
    fcol, at = carve(at, TT, NHC)
    assert at <= ARENA, at

    def second_layer(layer, par_full, t_sq):
        par = params[layer % 2]

        def pc(name, n, off=0):
            return par[:, C2[name] + off:C2[name] + off + n]

        rel = pc("rel", NHB * T).rearrange("p (h n) -> p h n", h=NHB)
        for e in (PE, A, V, POOL):
            e.wait(par_full)
        t_rel = V.did(nc.vector.memset(rel[0:64, :, T - 64:T], MASKED))
        rs, t_r = x_rstd(T, t_sq)
        for e in (A, V, POOL):
            arena_slot.claim(e)
            mix_slot.claim(e)
            h_slot.claim(e)
        ready = norm_modulated(layer, pc("norm1", KT), 1, 0, T, rs, t_r)
        done = {}
        n5, nb = slice(0, NHC), NHB * HD

        def chunk_jobs(make):
            slot, landed = next_chunk()
            PE.wait(landed)
            jobs = make(slot.ap)
            for n, (product, finisher) in enumerate(jobs):
                def run(product=product, n=n):
                    bank, t = yield from product
                    if n == len(jobs) - 1:
                        slot.release(t)
                    return bank, t
                yield run(), finisher

        def placed(bias, out, name):
            def f(bank, t_pe):
                A.wait(t_pe)
                done[name] = A.did(nc.scalar.activation(out, bank.ap[:, 0:T], ACT.Identity, bias=pc("bin", 1, bias)))
                bank.release(done[name])
                yield
            return f

        def rotated(bias, out, name):
            def f(bank, t_pe):
                raw = tmps.next()
                raw.claim(A)
                A.wait(t_pe)
                t = A.did(nc.scalar.activation(raw.ap[:, 0:T], bank.ap[:, 0:T], ACT.Identity, bias=pc("bin", 1, bias)))
                bank.release(t)
                yield
                done[name] = yield from rope(raw.ap[:, 0:T], t, C("rot2", P), cos2[:], sin2[:], out)
                raw.release(done[name])
            return f

        def valued(tt, v0, n, name):
            def f(bank, t_pe):
                V.wait(t_pe)
                done[name] = V.did(nc.vector.tensor_tensor(v2[:, tt, v0:v0 + n], bank.ap[:, 0:n], pc("bv", n, v0), ALU.add))
                bank.release(done[name])
                yield
            return f

        def index_weights(tt):
            def f(bank, t_pe):
                V.wait(t_pe)
                t = V.did(nc.vector.tensor_tensor(wi[:, tt, :], bank.ap[:, 0:IDX_H], pc("bwi", IDX_H), ALU.add))
                bank.release(t)
                V.wait(t)
                done["wi"] = V.did(nc.vector.tensor_scalar(wi[:, tt, :], wi[:, tt, :], IDX_H ** -0.5 * HD ** -0.5,
                                                           None, ALU.mult))
                yield
            return f

        def forget_gates(bank, t_pe):
            f, e = tmps.next(), tmps.next()
            f.claim(A)
            e.claim(A)
            A.wait(t_pe)
            t = A.did(nc.scalar.activation(f.ap[n5, 0:T], bank.ap[n5, 0:T], ACT.Identity, bias=pc("bf", 1)[n5, :]))
            bank.release(t)
            A.wait(t)
            t = A.did(nc.scalar.activation(e.ap[n5, 0:T], f.ap[n5, 0:T], ACT.Abs))
            A.wait(t)
            t = A.did(nc.scalar.activation(e.ap[n5, 0:T], e.ap[n5, 0:T], ACT.Exp, scale=-1.0))
            A.wait(t)
            t = A.did(nc.scalar.activation(e.ap[n5, 0:T], e.ap[n5, 0:T], ACT.Ln, bias=ones[n5, 0:1]))
            yield
            V.wait(t)
            t = V.did(nc.vector.scalar_tensor_tensor(f.ap[n5, 0:T], f.ap[n5, 0:T], 0.0, e.ap[n5, 0:T], ALU.min, ALU.subtract))
            V.wait(t)
            t = V.did(nc.vector.memset(e.ap[n5, 0:T], 1.0))
            V.wait(t)
            t_f = V.did(nc.vector.tensor_tensor_scan(fcum[n5, :], e.ap[n5, 0:T], f.ap[n5, 0:T], 0.0, ALU.mult, ALU.add))
            f.release(t_f)
            e.release(t_f)
            yield
            PE.wait(t_f)
            for tt in range(TT):
                bank = banks.next()
                bank.claim(PE)
                t = PE.did(nc.tensor.transpose(bank.ap[:, 0:NHC], fcum[n5, tt * P:(tt + 1) * P], ident[n5, n5]))
                V.wait(t)
                t = V.did(nc.vector.tensor_copy(fcol[:, tt, :], bank.ap[:, 0:NHC]))
                bank.release(t)
                yield
            for hd in range(NHC):
                bank = banks.next()
                bank.claim(PE)
                t = PE.did(nc.tensor.matmul(bank.ap[:, 0:T], C("onehot", NHC * P)[n5, hd * P:(hd + 1) * P],
                                            fcum[n5, :], start=True, stop=True))
                yield
                A.wait(t)
                A.did(nc.scalar.activation(cmask[:, hd, 0:P], bank.ap[:, 0:P], ACT.Copy, scale=-1.0))
                t = A.did(nc.scalar.activation(cmask[:, hd, P:3 * P], bank.ap[:, 0:T], ACT.Copy, scale=-1.0))
                bank.release(t)
                POOL.wait(t)
                for c0, n, base in ((0, P, 0), (P, T, P)):
                    done["cmask"] = POOL.did(nc.gpsimd.affine_select(
                        out=cmask[:, hd, c0:c0 + n], in_=cmask[:, hd, c0:c0 + n], compare_op=ALU.is_ge,
                        fill=MASKED, base=base, pattern=[[-1, n]], channel_multiplier=1))
                yield

        def index(qt):
            nk = (qt + 1) * P
            PE.wait(done["qi3"], done["ki"], done["qi0"], done["qi1"], done["qi2"])
            for hd in range(IDX_H):
                p0 = 64 * (hd % 2)
                bank = banks.next()
                bank.claim(PE)
                t = PE.did(nc.tensor.matmul(bank.ap[:, 0:nk], qiT[p0:p0 + 64, hd // 2, qt * P:(qt + 1) * P],
                                            kiT[p0:p0 + 64, 0:nk], start=True, stop=True))
                r = tmps.next()
                r.claim(A)
                A.wait(t)
                t = A.did(nc.scalar.activation(r.ap[:, 0:nk], bank.ap[:, 0:nk], ACT.Relu))
                bank.release(t)
                yield
                V.wait(t, done["wi"])
                w = wi[:, qt, hd:hd + 1]
                if hd == 0:
                    t = V.did(nc.vector.tensor_scalar(idx[:, qt, 0:nk], r.ap[:, 0:nk], w, None, ALU.mult))
                else:
                    V.wait(t_idx)
                    t = V.did(nc.vector.scalar_tensor_tensor(idx[:, qt, 0:nk], r.ap[:, 0:nk], w, idx[:, qt, 0:nk],
                                                             ALU.mult, ALU.add))
                t_idx = t
                r.release(t)
            V.wait(t_idx)
            t = V.did(nc.vector.memset(idx[0:64, qt, nk - 64:nk], FILL))
            for _ in range(TOPK // 8):
                best = cols.next()
                best.claim(V)
                V.wait(t)
                t = V.did(nc.vector.max(best.ap[:, 0:8], idx[:, qt, 0:nk]))
                V.wait(t)
                t = V.did(nc.vector.match_replace(idx[:, qt, 0:nk], best.ap[:, 0:8], idx[:, qt, 0:nk], TAKEN))
                best.release(t)
                yield
            V.wait(t)
            done["sel"] = V.did(nc.vector.tensor_scalar(work[:, qt, 0:nk], idx[:, qt, 0:nk], TAKEN_UNDER, MASKED,
                                                        ALU.is_gt, ALU.mult))
            yield

        def head(tile, p0, vcol, bias, needs):
            rows = slice(p0, p0 + 64)
            pt = probs_t.next()
            pt.claim(A)
            PE.wait(*(done[n] for n in needs if n[0] in "qk"))
            V.wait(*(done[n] for n in needs))
            for qt in range(TT):
                nk = (qt + 1) * P
                s = banks.next()
                s.claim(PE)
                t = PE.did(nc.tensor.matmul(s.ap[:, 0:nk], qT2[rows, tile, qt * P:(qt + 1) * P],
                                            kT2[rows, tile, 0:nk], start=True, stop=True))
                yield
                lg, stat = tmps.next(), cols.next()
                lg.claim(V)
                stat.claim(V)
                V.wait(t)
                t = bias(lg.ap[:, 0:nk], s.ap[:, 0:nk], qt, nk)
                s.release(t)
                V.wait(t)
                t = V.did(nc.vector.reduce_max(stat.ap[:, 0:1], lg.ap[:, 0:nk], AX))
                V.wait(t)
                t = V.did(nc.vector.tensor_scalar(stat.ap[:, 1:2], stat.ap[:, 0:1], -1.0, None, ALU.mult))
                yield
                A.wait(t)
                p = tmps.next()
                p.claim(A)
                t = A.did(nc.scalar.activation(p.ap[:, 0:nk], lg.ap[:, 0:nk], ACT.Exp, bias=stat.ap[:, 1:2],
                                               accum_out=stat.ap[:, 2:3]))
                lg.release(t)
                yield
                V.wait(t)
                t = V.did(nc.vector.reciprocal(stat.ap[:, 3:4], stat.ap[:, 2:3]))
                V.wait(t)
                t = V.did(nc.vector.tensor_scalar(p.ap[:, 0:nk], p.ap[:, 0:nk], stat.ap[:, 3:4], None, ALU.mult))
                stat.release(t)
                yield
                PE.wait(t)
                tr = banks.next()
                tr.claim(PE)
                for kt in range(qt + 1):
                    ins = nc.tensor.transpose(tr.ap[:, kt * P:(kt + 1) * P], p.ap[:, kt * P:(kt + 1) * P], ident)
                t = PE.did(ins)
                p.release(t)
                yield
                A.wait(t)
                t_pt = A.did(nc.scalar.activation(pt.ap[:, 0:qt + 1, qt * P:(qt + 1) * P],
                                                  tr.ap[:, 0:nk].rearrange("p (k q) -> p k q", q=P), ACT.Copy))
                tr.release(t_pt)
                yield
            PE.wait(t_pt, *(done[n] for n in needs))
            o = banks.next()
            o.claim(PE)
            for qt in range(TT):
                for kt in range(qt + 1):
                    ins = nc.tensor.matmul(o.ap[rows, qt * P:(qt + 1) * P], v2[:, kt, vcol:vcol + HD],
                                           pt.ap[:, kt, qt * P:(qt + 1) * P], start=kt == 0, stop=kt == qt)
            t = PE.did(ins)
            pt.release(t)
            yield
            A.wait(t)
            done["o"] = A.did(nc.scalar.activation(mix[rows, tile, 0:T], o.ap[rows, 0:T], ACT.Copy))
            o.release(done["o"])
            yield

        def scaled_plus(table):
            def f(out, s, qt, nk):
                return V.did(nc.vector.scalar_tensor_tensor(out, s, HD ** -0.5, table(qt, nk), ALU.mult, ALU.add))
            return f

        def forget(hd):
            def f(out, s, qt, nk):
                lg = tmps.next()
                lg.claim(V)
                t = V.did(nc.vector.tensor_scalar(lg.ap[:, 0:nk], s, HD ** -0.5, fcol[:, qt, hd:hd + 1], ALU.mult, ALU.add))
                V.wait(t)
                c0 = qt * P
                t = V.did(nc.vector.tensor_tensor(out, lg.ap[:, 0:nk], cmask[:, hd, c0:c0 + nk], ALU.add))
                lg.release(t)
                return t
            return f

        places = {f"{n}{i}": (m[:, t0 + i, :]) for t0, b, c in ((0, "a", 3), (3, "b", 2), (5, "c", 2))
                  for i in range(c) for n, m in (("q" + b, qT2), ("k" + b, kT2))}
        places |= {"qbc4": qT2[:, 7, :], "kbc4": kT2[:, 7, :], "ki": kiT, **{f"qi{i}": qiT[:, i, :] for i in range(4)}}
        order = [n for chunk in TILE_CHUNKS for n in chunk]

        def tile_jobs(chunk):
            return lambda w: [(btile(w, h, i * P, pause=2, ready=ready),
                               (rotated if n[1] in "ai" else placed)(order.index(n), places[n], n))
                              for i, n in enumerate(chunk)]

        def value_jobs(col, v0, n, name):
            return lambda w: [(atile(w, h, tt * P, col, n, pause=2), valued(tt, v0, n, name)) for tt in range(TT)]

        def first_chunks():
            yield from chunk_jobs(lambda w: [
                (btile(w, h, nb + IDX_H, m=NHC, pause=2, ready=ready), forget_gates),
                *value_jobs(0, NHA * HD, nb, "vb")(w),
                *[(atile(w, h, tt * P, nb, IDX_H, pause=2), index_weights(tt)) for tt in range(TT)]])
            for chunk in TILE_CHUNKS[:2]:
                yield from chunk_jobs(tile_jobs(chunk))

        def other_chunks():
            yield from chunk_jobs(tile_jobs(TILE_CHUNKS[2]))
            yield from chunk_jobs(value_jobs(0, NHA * HD + nb, NHC * HD, "vc"))
            for chunk in TILE_CHUNKS[3:5]:
                yield from chunk_jobs(tile_jobs(chunk))
            yield from chunk_jobs(lambda w: tile_jobs(TILE_CHUNKS[5])(w) + value_jobs(P, 0, NHA * HD, "va")(w))

        def gated(j):
            def f(bank, t_pe):
                A.wait(t_pe)
                done["gates"] = A.did(nc.scalar.activation(gates[:, j, :], bank.ap[:, 0:T], ACT.Sigmoid,
                                                           bias=pc("bgate", 1, j)))
                bank.release(done["gates"])
                yield
            return f

        def gate_chunks():
            for c in range(6):
                yield from chunk_jobs(lambda w: [(btile(w, h, i * P, pause=3), gated(c * 4 + i)) for i in range(4)])

        interleave(tiles_then(first_chunks()))
        indexer = in_turn(index(0), index(1))
        interleave(tiles_then(other_chunks()), beside=[indexer])
        done["rel"] = t_rel
        bc_heads, a_heads = [], []
        for hd in range(NHB):
            tile, p0, q = (3 + hd // 2, 64 * (hd % 2), f"b{hd // 2}") if hd < 4 else (7, 0, "bc4")
            bc_heads.append(head(tile, p0, NHA * HD + hd * HD, scaled_plus(lambda qt, nk, hd=hd: rel[:, hd, T - nk:T]),
                                 ("q" + q, "k" + q, "rel", "vb")))
        for hd in range(NHC):
            tile, p0, q = (5 + hd // 2, 64 * (hd % 2), f"c{hd // 2}") if hd < 4 else (7, 64, "bc4")
            bc_heads.append(head(tile, p0, (NHA + NHB) * HD + hd * HD, forget(hd), ("q" + q, "k" + q, "cmask", "vc")))
        for hd in range(NHA):
            a_heads.append(head(hd // 2, 64 * (hd % 2), hd * HD, scaled_plus(lambda qt, nk: work[:, qt, 0:nk]),
                                (f"qa{hd // 2}", f"ka{hd // 2}", "sel", "va")))
        interleave(tiles_then(gate_chunks()), abreast(2, bc_heads), in_turn(indexer, abreast(2, a_heads)))

        h_slot.release(PE.sem.now())
        PE.wait(done["o"])
        V.wait(done["gates"])
        h_slot.claim(V)
        y_ready = []
        for c in range(2):
            slot, landed = next_chunk()
            PE.wait(landed)
            for i in range(4):
                j = c * 4 + i
                parts = []
                for br, kts in enumerate((((0, 0, P), (1, 0, P), (2, 0, P)), ((3, 0, P), (4, 0, P), (7, 0, 64)),
                                          ((5, 0, P), (6, 0, P), (7, 64, P)))):
                    bank = banks.next()
                    bank.claim(PE)
                    for n, (k, r0, r1) in enumerate(kts):
                        ins = nc.tensor.matmul(bank.ap[:, 0:T], slot.ap[r0:r1, k * 512 + i * P:k * 512 + (i + 1) * P],
                                               mix[r0:r1, k, 0:T], start=n == 0, stop=n == 2)
                    t_pe = PE.did(ins)
                    m = tmps.next()
                    m.claim(V)
                    V.wait(t_pe)
                    t = V.did(nc.vector.tensor_tensor(m.ap[:, 0:T], bank.ap[:, 0:T], gates[:, br * KT + j, :], ALU.mult))
                    bank.release(t)
                    parts.append(m)
                V.wait(t)
                t = V.did(nc.vector.tensor_tensor(parts[0].ap[:, 0:T], parts[0].ap[:, 0:T], parts[1].ap[:, 0:T], ALU.add))
                parts[1].release(t)
                V.wait(t)
                t_y = V.did(nc.vector.tensor_tensor(h[:, j, 0:T], parts[0].ap[:, 0:T], parts[2].ap[:, 0:T], ALU.add))
                parts[0].release(t_y)
                parts[2].release(t_y)
                y_ready.append(t_y)
            slot.release(t_pe)
        mix_slot.release(t_pe)
        got = {}
        ffn_start = FeedForwardStart(layer, T)

        def out_task():
            got["r"] = yield from project_residual(layer, 2, T, h, y_ready, ffn_start.early)
        interleave(out_task())
        t_sq, t_pe = got["r"]
        h_slot.release(t_pe)
        arena_slot.release(t_pe, t_sq)
        parts, quarters = ffn_start.rest()
        rs, t_r = x_rstd(T, t_sq)
        ready = norm_modulated(layer, pc("norm2", KT), 4, 3, T, rs, t_r, parts)
        t_sq = feed_forward(layer, None, T, ready, parts, quarters, none, none)
        par_slots[layer % 2].release(t_sq)
        return t_sq

    tmps = Turns([Slot(g, f"half{2 * i + j}", s.ap[:, j * T:(j + 1) * T], s.free)
                  for i, s in enumerate(tmps.slots) for j in range(2)])
    probs_t = Turns([Slot(g, f"half_probsT{2 * i + j}", s.ap[:, 2 * j:2 * j + 2, :], s.free)
                     for i, s in enumerate(probs_t.slots) for j in range(2)])
    t_sq = second_layer(2, par_tok[2], t_sq)
    t_sq = second_layer(3, par_tok[3], t_sq)

    rs, t_rs = x_rstd(T, t_sq)
    V.wait(t_rs)
    h_slot.claim(V)
    for k in range(KT):
        t = V.did(nc.vector.scalar_tensor_tensor(h[:, k, 0:T], x[:, k, 0:T], const[:, CC["final"] + k:CC["final"] + k + 1],
                                                 rs.ap[:, 0:T], ALU.mult, ALU.mult))
        SP.wait(t)
        t_out = SP.dma(a["out"][:, k, :], h[:, k, 0:T], out_full)
    SP.wait(t_out)
    return g.plan


def k_major(w):
    k, n = w.shape
    return w.reshape(k // P, P, n).transpose(1, 0, 2).reshape(P, -1)


def by_column(v):
    return v.reshape(-1, P).T


def on_all(v):
    return np.broadcast_to(v.reshape(1, -1), (P, v.size))


def lay_out(i):
    i = {n: np.asarray(v) for n, v in i.items()}
    f32 = np.float32

    def padded(w, n=CHUNK):
        out = np.zeros((P, n), f32)
        out[:, :w.shape[1]] = w
        return out

    main, ffn, down, downh = [], [], [], []

    def add_feed_forward(gate, value, w_down, split_down):
        ffn.extend(k_major(np.concatenate([gate[:, c:c + P], value[:, c:c + P]], 1)) for c in range(0, FF, P))
        tiles = [k_major(w_down[:, c:c + P]) for c in range(0, D, P)]
        if split_down:
            downh.extend(t[:, n:n + DOWN_K * P] for t in tiles for n in (0, DOWN_K * P))
        else:
            down.extend(tiles)
    A0, Q0, K0, V0, CV0 = 0, 512, 1024, 1536, 2048
    for l in range(DEPTH):
        w = i["w_in"][l]
        main += [k_major(w[:, c:c + 512]) for c in (CV0, K0, Q0, V0, A0)]
        main += [k_major(i["w_out"][l][:, c:c + 512]) for c in (0, 512)]
        add_feed_forward(i["w_gate"][l], i["w_val"][l], i["w_down"][l], l > 0)
    qa, ka, va, qi, ki, wi = 0, 384, 768, 1152, 1664, 1728
    qb, kb, vb, qc, kc, vc, fc, ga = 1736, 2056, 2376, 2696, 3016, 3336, 3656, 3661
    r = lambda c, n: list(range(c, c + n))
    cols = {"ki": r(ki, 64) + r(ki, 64), "qbc4": r(qb + 256, 64) + r(qc + 256, 64),
            "kbc4": r(kb + 256, 64) + r(kc + 256, 64)}
    for name, at in (("qi", qi), ("qa", qa), ("ka", ka), ("qb", qb), ("kb", kb), ("qc", qc), ("kc", kc)):
        cols |= {f"{name}{n}": r(at + n * P, P) for n in range(4)}
    tiles = [cols[n] for chunk in TILE_CHUNKS for n in chunk]
    chunks = [sum((cols[n] for n in chunk), []) for chunk in TILE_CHUNKS]
    chunks[5] += r(va, 384)
    chunks = [r(vb, 320) + r(wi, 8) + r(fc, 5), *chunks[:3], r(vc, 320), *chunks[3:]]
    chunks_g = [r(ga + c, 512) for c in range(0, 3 * D, 512)]
    rows = r(0, 384) + r(384, 256) + r(704, 256) + r(640, 64) + r(960, 64)

    def take(w, cols):
        out = np.zeros((D, 512), f32)
        out[:, :len(cols)] = w[:, cols]
        return k_major(out)

    for l in range(DEPTH):
        w = i["w_in_2"][l]
        main += [take(w, c) for c in chunks + chunks_g]
        wb = i["w_branch_2"][l][rows]
        main += [k_major(wb[:, c:c + 512]) for c in (0, 512)]
        main += [k_major(i["w_out_2"][l][:, c:c + 512]) for c in (0, 512)]
        wf = i["w_ffn_in_2"][l]
        add_feed_forward(wf[:, :FF], wf[:, FF:], i["w_ffn_out_2"][l], True)
    mod = [k_major(w[l][:, c:c + 256]) for w in (i["w_mod"], i["ada_w_2"]) for l in range(DEPTH)
           for c in range(0, 6 * D, 256)]

    p1 = np.zeros((DEPTH, P, N1), f32)
    p2 = np.zeros((DEPTH, P, N2), f32)

    def put(dst, where, name, v):
        dst[:, where[name]:where[name] + v.shape[1]] = v

    for l in range(DEPTH):
        q = p1[l]
        put(q, C1, "norm1", by_column(i["norm1_g"][l]))
        put(q, C1, "norm2", by_column(i["norm2_g"][l]))
        put(q, C1, "qg", np.concatenate([i["q_norm_g"][l]] * 2)[:, None])
        put(q, C1, "kg", np.concatenate([i["k_norm_g"][l]] * 2)[:, None])
        put(q, C1, "subg", i["subln_g"][l][:, None])
        put(q, C1, "conv_b", by_column(i["conv_b"][l]))
        put(q, C1, "lnc_g", by_column(i["ln_c_g"][l]))
        put(q, C1, "lnc_b", by_column(i["ln_c_b"][l]))
        put(q, C1, "fw", i["ffn_conv_w"][l].reshape(3, HT, P).transpose(2, 1, 0).reshape(P, -1))
        put(q, C1, "fb", by_column(i["ffn_conv_b"][l]))
        put(q, C1, "conv_w", i["conv_w"][l].reshape(TAPS, 2, P).transpose(2, 1, 0).reshape(P, -1))
        put(q, C1, "lnv_g", on_all(i["ln_v_g"][l]))
        put(q, C1, "lnv_b", on_all(i["ln_v_b"][l]))
        put(q, C1, "lam", on_all(np.concatenate([i[n][l] for n in ("lam_q1", "lam_k1", "lam_q2", "lam_k2")])))
        bs = np.repeat(i["b_s"][l].reshape(2, 2, P), 64, axis=1)
        put(q, C1, "b_s", bs.transpose(1, 0, 2).reshape(P, -1))
        put(q, C1, "w_sT", i["w_s"][l].transpose(2, 0, 1).reshape(P, -1))
        q = p2[l]
        b = i["b_in_2"][l]
        put(q, C2, "norm1", by_column(i["norm1_g_2"][l]))
        put(q, C2, "norm2", by_column(i["norm2_g_2"][l]))
        put(q, C2, "bin", np.stack([b[t] for t in tiles], 1))
        put(q, C2, "bgate", by_column(b[ga:ga + 3 * D]))
        q[0:NHC, C2["bf"]] = b[fc:fc + NHC]
        put(q, C2, "bv", on_all(np.concatenate([b[va:va + 384], b[vb:vb + 320], b[vc:vc + 320]])))
        put(q, C2, "bwi", on_all(b[wi:wi + IDX_H]))
        apart = np.minimum(np.arange(P)[:, None] + P - np.arange(T)[None], 128) + 128
        put(q, C2, "rel", i["rel_bias_2"][l][:, apart].transpose(1, 0, 2).reshape(P, -1))
    const = np.zeros((P, NC), f32)
    put(const, CC, "ident", np.eye(P, dtype=f32))
    put(const, CC, "ones", np.ones((P, P), f32))
    put(const, CC, "half", np.kron(np.eye(2), np.ones((64, 64))).astype(f32))
    rot1, rot2 = np.zeros((P, P), f32), np.zeros((P, P), f32)
    for blk in range(0, P, 32):
        for j in range(16):
            rot1[blk + 16 + j, blk + j], rot1[blk + j, blk + 16 + j] = -1, 1
    for blk in range(0, P, 64):
        for j in range(8):
            rot2[blk + 8 + j, blk + j], rot2[blk + j, blk + 8 + j] = -1, 1
    put(const, CC, "rot1", rot1)
    put(const, CC, "rot2", rot2)
    n = np.arange(T)
    inv1 = (10000.0 ** (-np.arange(0, 32, 2, dtype=np.float64) / 32)).astype(f32)
    ang = np.zeros((P, T), f32)
    for p in range(P):
        axis, j = (p % 64) // 32, p % 16
        ang[p] = ((n // 64) if axis == 0 else (n % 64)).astype(f32) * inv1[j]
    put(const, CC, "cos1", np.cos(ang.astype(np.float64)).astype(f32))
    put(const, CC, "sin1", np.sin(ang.astype(np.float64)).astype(f32))
    inv2 = (500000.0 ** (-np.arange(0, 16, 2, dtype=np.float64) / 16)).astype(f32)
    for p in range(P):
        if p % 64 < 16:
            const[p, CC["inv"]] = inv2[p % 8]
    const[:, CC["eps"]] = EPS
    put(const, CC, "final", by_column(i["final_g_2"]))
    put(const, CC, "c", np.concatenate([by_column(i["c"][0]), by_column(i["c_ctx"]), by_column(i["c_2"][0])], 1))
    put(const, CC, "b_mod", np.concatenate([by_column(b[l]) for b in (i["b_mod"], i["ada_b_2"]) for l in range(DEPTH)], 1))
    for hd in range(NHC):
        const[hd, CC["onehot"] + hd * P:CC["onehot"] + (hd + 1) * P] = 1

    tokens = lambda t: np.ascontiguousarray(t[0].T.reshape(KT, P, T).transpose(1, 0, 2))
    return {
        "w_main": np.stack(main), "w_down": np.stack(down), "w_ffn": np.stack(ffn), "w_downh": np.stack(downh), "w_mod": np.stack(mod), "p1": p1, "p2": p2,
        "const": const, "x": tokens(i["x"]), "ctx": tokens(i["ctx"]),
        "pos": np.ascontiguousarray(np.broadcast_to(i["positions_2"].astype(np.int32), (P, T))),
    }


def kernel(**inputs):
    import concourse.bacc as bacc
    from concourse.bass_utils import run_bass_kernel_spmd

    arrays = lay_out(inputs)
    plan = Plan()
    for final in (False, True):
        nc = bacc.Bacc("TRN2", target_bir_lowering=False, num_devices=1)
        aps = {n: nc.dram_tensor(n, list(v.shape), mybir.dt.from_np(v.dtype), kind="ExternalInput").ap()
               for n, v in arrays.items()}
        aps["out"] = nc.dram_tensor("out", [P, KT, T], F32, kind="ExternalOutput").ap()
        build(nc, aps, plan, final)
    r = run_bass_kernel_spmd(nc, [arrays], core_ids=[0])
    out = r.results[0]["out"]
    return np.ascontiguousarray(out.transpose(1, 0, 2).reshape(D, T).T)[None]
```

```python
import math

import numpy as np

import concourse.bass as bass
from concourse import mybir
from concourse.alu_op_type import AluOpType as ALU

F32 = mybir.dt.float32
F32R = mybir.dt.float32r
I32 = mybir.dt.int32
ACT = mybir.ActivationFunctionType
AX = mybir.AxisListType.X

P = 128
D = 1024
KT = D // P
T = 256
TT = T // P
EPS = 1e-6
DEPTH = 2
FF = 2816
HT = FF // P
H1, V1 = 4, 128
QK1 = 64
TAPS = 31
HALO = TAPS // 2
NT2 = 6 * D // P
CHUNK = 4096
GROUP = KT * P
FCHUNK = 2 * GROUP
DOWN_K = HT // 2
DOWN_KS = (0, 6, DOWN_K)
MODCHUNK = 2048
MODS_PER_LAYER = 6 * D // 256
NHA, NHB, NHC = 6, 5, 5
HD = 64
IDX_H = 8
TOPK = 64
VW = HD * (NHA + NHB + NHC)
FILL, TAKEN, TAKEN_UNDER = -3.0e38, -3.3e38, -3.2e38
MASKED = -1.0e30
ARENA = 12704


def columns(*parts):
    at, out = 0, {}
    for name, n in parts:
        out[name] = at
        at += n
    return out, at


C1, N1 = columns(("norm1", KT), ("norm2", KT), ("qg", 1), ("kg", 1), ("subg", 1), ("conv_b", 2),
                 ("lnc_g", 2), ("lnc_b", 2), ("fw", 3 * HT), ("fb", HT), ("conv_w", 2 * TAPS),
                 ("lnv_g", 256), ("lnv_b", 256), ("lam", 4 * QK1), ("b_s", 2 * P), ("w_sT", 4 * P))
B2_CHUNKS = 37
B2_TILES = 21
C2, N2 = columns(("norm1", KT), ("norm2", KT), ("bin", B2_TILES), ("bgate", 3 * KT), ("bf", 1),
                 ("bv", VW), ("bwi", IDX_H), ("rel", NHB * T))
CC, NC = columns(("ident", P), ("ones", P), ("half", P), ("rot1", P), ("rot2", P), ("cos1", T),
                 ("sin1", T), ("inv", 1), ("eps", 1), ("final", KT), ("c", 3 * KT),
                 ("b_mod", 4 * NT2), ("onehot", NHC * P), ("halfpi", 1))


class Plan:

    def __init__(self):
        self.per_turn, self.released = {}, {}


class Token:

    def __init__(self, sem, count, loops):
        self.sem, self.count, self.loops = sem, count, loops


class Sem:
    def __init__(self, prog, name):
        self.prog, self.name, self.h, self.count = prog, name, prog.nc.alloc_semaphore(name), 0
        prog.sems.append(self)

    def add(self, n):
        self.count += n
        return Token(self, self.count, tuple(self.prog.loops))

    def now(self):
        return self.add(0)


FIRST_TILES = ("ki", "qi0", "qi1", "qi2", "qi3", "kb0", "kb1", "kc0")
MORE_TILES = ("kc1", "kbc4", "qb0", "qb1")
LAST_TILES = ("qc0", "qc1", "qbc4", "ka0", "ka1", "ka2", "qa0", "qa1")
B2_ORDER = (*FIRST_TILES, *MORE_TILES, *LAST_TILES, "qa2")
COLUMN_GROUPS = ((0, 2 * P, 0, KT), (P, 2 * P, 0, KT))


def value_groups(k0):
    return tuple((n * GROUP, 512, k0 + 2 * n, 2) for n in range(2))


class Loop:
    def __init__(self, number, turns):
        self.number, self.turns, self.it, self.open = number, turns, None, True


class Prog:
    def __init__(self, nc, plan, final):
        self.nc, self.plan, self.final = nc, plan, final
        self.loops, self.sems, self.n_loops = [], [], 0

    def value(self, token, turns_back=0):
        v = token.count
        for loop in token.loops:
            k = self.plan.per_turn.get((token.sem.name, loop.number), 0)
            if loop.open:
                if k:
                    v = v + loop.it * k
            else:
                v = v + (loop.turns - 1) * k
        if turns_back:
            k = self.plan.per_turn.get((token.sem.name, self.loops[-1].number), 0)
            v = v - turns_back * k
        return v

    def loop(self, turns, body):
        loop = Loop(self.n_loops, turns)
        self.n_loops += 1
        start = [s.count for s in self.sems]
        with self.nc.Fori(0, turns) as it:
            loop.it = it
            self.loops.append(loop)
            body(it)
            self.loops.pop()
        loop.open = False
        for s, c in zip(self.sems, start):
            k = s.count - c
            if not self.final:
                self.plan.per_turn[(s.name, loop.number)] = k
            s.count = c + k * turns


class Engine:
    CREDIT = 2048

    def __init__(self, prog, name, e):
        self.prog, self.e, self.sem, self.seen = prog, e, Sem(prog, "steps_" + name), {}
        e.sem_inc(self.sem.h, self.CREDIT)
        self.sem.count = self.CREDIT

    def wait(self, *tokens):
        for t in tokens:
            key = (t.sem.name, t.loops)
            if t.loops == tuple(self.prog.loops) and self.seen.get(key, 0) >= t.count:
                continue
            self.e.wait_ge(t.sem.h, self.prog.value(t))
            if t.loops == tuple(self.prog.loops):
                self.seen[key] = t.count

    def did(self, instruction):
        instruction.then_inc(self.sem.h, 1)
        return self.sem.add(1)

    def dma(self, out, in_, sem):
        self.e.dma_start(out, in_).then_inc(sem.h, 16)
        return sem.add(16)


class Slot:

    def __init__(self, prog, name, ap, free=()):
        self.prog, self.name, self.ap, self.free, self.home = prog, name, ap, list(free), ()
        self.turns, self.held = None, False

    def claim(self, engine):
        engine.wait(*self.free)
        if self.prog.loops and self.home != tuple(self.prog.loops):
            for t in self.prog.plan.released.get((self.prog.loops[-1].number, self.name), []):
                sem = next(s for s in self.prog.sems if s.name == t[0])
                token = Token(sem, t[1], tuple(self.prog.loops))
                engine.e.wait_ge(sem.h, self.prog.value(token, turns_back=1))
        return self.ap

    def release(self, *tokens):
        self.free, self.home = list(tokens), tuple(self.prog.loops)
        if self.held:
            self.held = False
            self.turns.idle.append(self)
        if self.prog.loops and not self.prog.final:
            self.prog.plan.released[(self.prog.loops[-1].number, self.name)] = [
                (t.sem.name, t.count) for t in tokens]


class Turns:

    def __init__(self, slots):
        self.slots, self.idle = slots, list(slots)
        for s in slots:
            s.turns = self

    def only(self, n):
        aside = self.idle[n:]
        self.idle = self.idle[:n]
        return aside

    def back(self, aside):
        self.idle += aside

    def next(self):
        s = self.idle.pop(0)
        s.held = True
        return s


def interleave(*tasks, beside=()):
    for _ in together(*tasks):
        for b in beside:
            next(b, None)


def together(*tasks):
    tasks = list(tasks)
    while tasks:
        for t in list(tasks):
            if next(t, "done") == "done":
                tasks.remove(t)
        yield


def abreast(width, tasks, apart=0):
    waiting, running, rest = list(tasks), [], 0
    while waiting or running:
        rest -= 1
        while waiting and len(running) < width and rest <= 0:
            running.append(waiting.pop(0))
            rest = apart
        for t in list(running):
            if next(t, "done") == "done":
                running.remove(t)
        yield


def quickened(task, every):
    for n, _ in enumerate(task):
        if n % every:
            yield


def slowly(task, steps):
    for _ in task:
        for _ in range(steps):
            yield


def in_turn(*tasks):
    for t in tasks:
        yield from t


def build(nc, a, plan, final):
    g = Prog(nc, plan, final)
    PE, ACTE, V, POOL, SP = (Engine(g, n, e) for n, e in (
        ("pe", nc.tensor), ("act", nc.scalar), ("dve", nc.vector), ("pool", nc.gpsimd), ("sp", nc.sync)))
    A = ACTE

    at_byte = {}

    def sb(name, *shape):
        at_byte[name] = -(-nc.sbuf_base // 32) * 32
        return nc.alloc_sbuf_tensor("sb_" + name, [P, *shape], F32)

    def rounded(name, *shape):
        return nc.alloc_sbuf_tensor_at("r_" + name, [P, *shape], F32R, offset=at_byte[name])

    ring_mem = [sb(f"ring{i}", CHUNK) for i in range(2)]
    ring = Turns([Slot(g, f"ring{i}", ring_mem[i]) for i in range(2)])
    ring_full = [Sem(g, f"weights_landed{i}") for i in range(2)]
    ring_r = [rounded(f"ring{i}", CHUNK) for i in range(2)]
    quarter_full = [Sem(g, f"quarter_landed{i}") for i in range(4)]
    lo_made = Sem(g, "low_parts_made")
    modring = Turns([Slot(g, f"modring{i}", sb(f"modring{i}", MODCHUNK)) for i in range(2)])
    modring_r = rounded("modring1", MODCHUNK)
    mod_full = [Sem(g, f"mod_weights_landed{i}") for i in range(2)]
    param_full = [Sem(g, f"params_landed{i}") for i in range(2)]
    setup_full = Sem(g, "setup_landed")
    out_full = Sem(g, "out_landed")

    x = sb("x", KT, 2 * T)
    h = sb("h", KT, 2 * T)
    mix = sb("mix", KT, 2 * T)
    h_slot, mix_slot = Slot(g, "h", h), Slot(g, "mix", mix)
    h_r, mix_r = rounded("h", KT, 2 * T), rounded("mix", KT, 2 * T)
    arena = sb("arena", ARENA)
    hid_r = rounded("arena", HT, 2 * T)
    arena_slot = Slot(g, "arena", arena)
    const = sb("const", NC)
    params = [sb(f"params{i}", max(N1, N2)) for i in range(2)]
    params_r = rounded("params1", 2 * GROUP)
    mods = sb("mods", 4 * NT2, 2)
    acoef = sb("acoef", 2, KT)
    acoef_slot = Slot(g, "acoef", acoef)
    tmps = Turns([Slot(g, f"tmp{i}", sb(f"tmp{i}", 2 * T)) for i in range(8)])
    cols = Turns([Slot(g, f"cols{i}", sb(f"cols{i}", 16)) for i in range(16)])
    probs_t = Turns([Slot(g, f"probsT{i}", sb(f"probsT{i}", 4, T)) for i in range(2)])
    probs_r = [rounded(f"probsT{i}", GROUP) for i in range(2)]
    psum = nc.alloc_psum_tensor("psum", [P, 8, 512], F32)
    banks = Turns([Slot(g, f"bank{i}", psum[:, i, :]) for i in range(7)])
    mod_bank = Slot(g, "mod_bank", psum[:, 7, :])
    cos2, sin2 = sb("cos2", T), sb("sin2", T)

    def C(name, n):
        return const[:, CC[name]:CC[name] + n]

    ident, ones, half = C("ident", P), C("ones", P), C("half", P)
    eps = C("eps", 1)

    SP.dma(const[:], a["const"], setup_full)
    SP.dma(x[:, :, 0:T], a["x"], setup_full)
    s_x = SP.dma(x[:, :, T:2 * T], a["ctx"], setup_full)
    for e in (PE, A, V, POOL):
        e.wait(s_x)

    stream = {"main": 0}

    def load_chunk(index=None, src=None, width=CHUNK):
        slot = ring.next()
        n = ring.slots.index(slot)
        slot.claim(SP)
        if src is None:
            src = a["w_main"][bass.ds(index, 1)].rearrange("a p n -> p (a n)")
        return slot, SP.dma(slot.ap[:, 0:width], src, ring_full[n])

    def next_chunk():
        i = stream["main"]
        stream["main"] += 1
        return load_chunk(i)

    def btile(w, rhs, col, width=512, m=P, kts=KT, n=T, ready=None, pause=KT):
        bank = banks.next()
        bank.claim(PE)
        for k in range(kts):
            if ready is not None:
                PE.wait(ready[k])
            i = nc.tensor.matmul(bank.ap[0:m, 0:n], w[:, k * width + col:k * width + col + m],
                                 rhs[:, k, 0:n], start=k == 0, stop=k == kts - 1)
            if k % pause == pause - 1 and k < kts - 1:
                yield
        return bank, PE.did(i)

    def atile(w, lhs, tok0, col, ncols, width=512, pause=KT):
        bank = banks.next()
        bank.claim(PE)
        for k in range(KT):
            i = nc.tensor.matmul(bank.ap[:, 0:ncols], lhs[:, k, tok0:tok0 + P],
                                 w[:, k * width + col:k * width + col + ncols],
                                 start=k == 0, stop=k == KT - 1)
            if k % pause == pause - 1 and k < KT - 1:
                yield
        return bank, PE.did(i)

    class Quarters:

        def __init__(self, his):
            self.his, self.waiting, self.landed, self.split_up = Turns(his), [], {}, []
            self.todo, self.unsplit, self.later = [], [], None
            self.ahead = len(his) - 1
            slots = []
            for big in ring.idle + [s for s in ring.slots if s.held]:
                b = ring.slots.index(big)
                for half in range(2):
                    at = slice(half * FCHUNK, (half + 1) * FCHUNK)
                    slot = Slot(g, f"quarter{len(slots)}", ring_mem[b][:, at], big.free)
                    slot.rounded, slot.big = ring_r[b][:, at], big
                    slots.append(slot)
            self.ring = Turns(slots)

        def refresh(self):
            for slot in self.ring.slots[2:]:
                slot.free = slot.big.free

        def load(self, src, width, groups):
            slot = self.ring.next()
            slot.claim(SP)
            self.landed[slot] = SP.dma(slot.ap[:, 0:width], src, quarter_full[self.ring.slots.index(slot)])
            to = self.waiting if self.later is None else self.later
            to += [(slot, n == len(groups) - 1, *gr) for n, gr in enumerate(groups)]
            if not groups:
                self.unsplit.append(slot)

        def refill(self):
            if self.todo:
                self.load(*self.todo.pop(0))

        def split(self):
            slot, last, at, stride, k0, nk = self.waiting.pop(0)

            wide = min(stride, GROUP // nk) if nk < KT else P

            def view(ap):
                if wide == stride:
                    return ap[:, at:at + nk * stride].rearrange("p (k m) -> p k m", k=nk)
                return ap[:, :].rearrange("p (k m) -> p k m", k=nk)[:, :, at:at + wide]
            hs = self.his.next()
            hs.claim(A)
            A.wait(self.landed[slot])
            hi = hs.ap[:, 0:nk * wide].rearrange("p (k m) -> p k m", k=nk)
            t = A.did(nc.scalar.activation(hi, view(slot.ap), ACT.Copy))
            V.wait(t)
            nc.vector.tensor_tensor(view(slot.rounded), view(slot.ap), hi.bitcast(F32),
                                    ALU.subtract).then_inc(lo_made.h, 1)
            self.split_up.append([slot, last, hs, hi, view(slot.rounded), k0, nk, lo_made.add(1)])

        def carried(self):
            here = tuple(g.loops)
            for slot in self.landed:
                sem = quarter_full[self.ring.slots.index(slot)]
                self.landed[slot] = Token(sem, sem.count, here)
            for n, entry in enumerate(reversed(self.split_up)):
                entry[-1] = Token(lo_made, lo_made.count - n, here)
            return [e[2] for e in self.split_up]

        def values(self, outs, h_hi, h_lo, last_group):
            while self.waiting and len(self.split_up) <= self.ahead:
                self.split()
            slot, last, hs, hi, lo, k0, nk, made = self.split_up.pop(0)
            PE.wait(made)
            for k in range(nk):
                for w, z in ((hi, h_hi), (hi, h_lo), (lo, h_hi)):
                    for bank, tok, c in outs:
                        start = k0 == 0 and k == 0 and w is hi and z is h_hi
                        stop = last_group and k == nk - 1 and w is lo
                        if tok is None:
                            i = nc.tensor.matmul(bank.ap[:, 0:T], w[:, k, c], z[:, k0 + k, :], start=start, stop=stop)
                        else:
                            i = nc.tensor.matmul(bank.ap[:, 0:c.stop], z[:, k0 + k, tok], w[:, k, c],
                                                 start=start, stop=stop)
                    yield
            t = PE.did(i)
            hs.release(t)
            if last:
                slot.release(t)
                self.refill()
            return t

        def products(self, bank, rhs_hi, rhs_lo, n, start, stop, ready=None, pause=3):
            def split_later():
                while self.waiting and len(self.split_up) < self.ahead + early:
                    self.split()
            early = self.ahead == 1 or not self.split_up
            split_later()
            slot, last, hs, hi, lo, k0, nk, made = self.split_up.pop(0)
            PE.wait(made)
            for k in range(nk):
                if k == min(pause, nk - 1):
                    early = 0
                    split_later()
                if ready is not None:
                    PE.wait(ready[k0 + k])
                for w, z in ((hi, rhs_hi), (hi, rhs_lo), (lo, rhs_hi)):
                    i = nc.tensor.matmul(bank.ap[:, 0:n], w[:, k, :], z[:, k0 + k, :],
                                         start=start and k == 0 and z is rhs_hi and w is hi,
                                         stop=stop and k == nk - 1 and w is lo)
                if k % pause == pause - 1 and k < nk - 1:
                    yield
            t = PE.did(i)
            hs.release(t)
            if last:
                slot.release(t)
                self.refill()
            return t

        def close(self):
            for s in probs_t.slots:
                s.free = [PE.sem.now()]
            for big in ring.slots:
                big.free = [t for s in self.ring.slots if s.big is big for t in s.free]

    c_cols = sb("c_cols", 3 * KT)
    t_c = A.did(nc.scalar.activation(c_cols[:], C("c", 3 * KT), ACT.Silu))
    V.wait(t_c)
    acc = Turns([Slot(g, f"modacc{i}", sb(f"modacc{i}", 256)) for i in range(4)])
    mods_done = [None]

    def load_mod_chunk(j):
        slot = modring.next()
        slot.claim(POOL)
        return slot, POOL.dma(slot.ap[:], a["w_mod"][bass.ds(j, 1)].rearrange("a p n -> p (a n)"),
                              mod_full[modring.slots.index(slot)])

    def mod_out(j, vectors, t_sum):
        V.wait(t_sum)
        for v in range(vectors):
            t_mod = V.did(nc.vector.tensor_tensor(
                mods[:, bass.ds(j * 2, 2), v], mod_bank.ap[:, 2 * v:2 * v + 2],
                const[:, bass.ds(j * 2 + CC["b_mod"], 2)], ALU.add))
        mod_bank.release(t_mod)
        mods_done[0] = t_mod

    def mod_tasks(chunks):
        sums = []
        for j, vectors in chunks:
            for k in mod_over_k(j, vectors):
                if isinstance(k, tuple):
                    sums.append(k)
                    break
                if k == KT - 2:
                    while sums and sum(len(s[1]) for s in sums) + len(vectors) > 2:
                        mod_over_partitions(*sums.pop(0))
                yield
        for s in sums:
            for _ in range(5):
                yield
            mod_over_partitions(*s)

    def mod_over_k(j, vectors):
        slot, landed = load_mod_chunk(j)
        V.wait(landed)
        accs = [acc.next() for _ in vectors]
        last = [None] * len(vectors)
        for ac in accs:
            ac.claim(V)
        for k in range(KT):
            for v, cv in enumerate(vectors):
                w = slot.ap[:, k * 256:(k + 1) * 256]
                if k == 0:
                    last[v] = V.did(nc.vector.tensor_scalar(accs[v].ap[:], w, cv[:, k:k + 1], None, ALU.mult))
                else:
                    V.wait(last[v])
                    last[v] = V.did(nc.vector.scalar_tensor_tensor(
                        accs[v].ap[:], w, cv[:, k:k + 1], accs[v].ap[:], ALU.mult, ALU.add))
            if k < KT - 1:
                yield k
        slot.release(last[-1])
        yield j, accs, last

    def mod_over_partitions(j, accs, last):
        mod_bank.claim(PE)
        for v, ac in enumerate(accs):
            PE.wait(last[v])
            for t in range(2):
                i = nc.tensor.matmul(mod_bank.ap[:, 2 * v + t:2 * v + t + 1], ac.ap[:, t * P:(t + 1) * P],
                                     ones[:, 0:1], start=True, stop=True)
            t_sum = PE.did(i)
            ac.release(t_sum)
        mod_out(j, len(accs), t_sum)

    def mod_direct(j):
        slot, landed = load_mod_chunk(j)
        PE.wait(landed, t_c)
        mod_bank.claim(PE)
        both = c_cols[:, 0:2 * KT].rearrange("p (v k) -> p k v", v=2)
        for t in range(2):
            for k in range(KT):
                i = nc.tensor.matmul(mod_bank.ap[:, 0:4].rearrange("p (v t) -> p t v", t=2)[:, t, :],
                                     slot.ap[:, k * 256 + t * P:k * 256 + (t + 1) * P], both[:, k, :],
                                     start=k == 0, stop=k == KT - 1)
            yield
        t_sum = PE.did(i)
        slot.release(t_sum)
        mod_out(j, 2, t_sum)

    lat_c, ctx_c, c2 = (c_cols[:, v * KT:(v + 1) * KT] for v in range(3))

    def mod(layer, which, k, v):
        t = layer * NT2 + which * KT + k
        return mods[:, t, v:v + 1]

    def rstd_of(bank, token, n, scale, tmp=None):
        s = tmp or tmps.next()
        s.claim(A)
        A.wait(token)
        t = A.did(nc.scalar.activation(s.ap[:, 0:n], bank.ap[:, 0:n], ACT.Sqrt, bias=eps, scale=scale))
        bank.release(t)
        V.wait(t)
        return s, V.did(nc.vector.reciprocal(s.ap[:, 0:n], s.ap[:, 0:n]))

    def sum_squares(src, tiles, n, sum_matrix=None, after=()):
        bank = banks.next()
        bank.claim(PE)
        for k in range(tiles):
            sq = tmps.next()
            sq.claim(A)
            A.wait(*after)
            t = A.did(nc.scalar.activation(sq.ap[:, 0:n], src(k), ACT.Square))
            PE.wait(t)
            t = PE.did(nc.tensor.matmul(bank.ap[:, 0:n], sum_matrix if sum_matrix is not None else ones,
                                        sq.ap[:, 0:n], start=k == 0, stop=k == tiles - 1))
            sq.release(t)
        return bank, t

    sqacc = arena[:, ARENA - 2 * T:ARENA]

    def add_squares(k, n, t_x, first=False):
        V.wait(t_x)
        xs = x[:, bass.ds(k, 1), 0:n].rearrange("p a n -> p (a n)")
        if first:
            return V.did(nc.vector.tensor_tensor(sqacc[:, 0:n], xs, xs, ALU.mult))
        sq = tmps.next()
        sq.claim(V)
        t = V.did(nc.vector.tensor_tensor(sq.ap[:, 0:n], xs, xs, ALU.mult))
        V.wait(t)
        t = V.did(nc.vector.tensor_tensor(sqacc[:, 0:n], sqacc[:, 0:n], sq.ap[:, 0:n], ALU.add))
        sq.release(t)
        return t

    def x_rstd(n, t_sq):
        scratch = cols.next()
        scratch.claim(A)
        scratch.release(A.did(nc.scalar.activation(scratch.ap[:, 0:1], eps, ACT.Sqrt)))
        bank = banks.next()
        bank.claim(PE)
        PE.wait(t_sq)
        t = PE.did(nc.tensor.matmul(bank.ap[:, 0:n], ones, sqacc[:, 0:n], start=True, stop=True))
        return rstd_of(bank, t, n, 1.0 / D)

    def norm_modulated(layer, norm_g, scale_v, shift_v, n, rs, t_r, parts=None):
        V.wait(mods_done[0])
        A.wait(mods_done[0])
        acoef_slot.claim(V)
        for v in range(n // T):
            base = layer * NT2 + scale_v * KT
            t_a = V.did(nc.vector.scalar_tensor_tensor(
                acoef[:, v, :], mods[:, base:base + KT, v], 1.0, norm_g, ALU.add, ALU.mult))
        V.wait(t_a, t_r)
        h_slot.claim(V)
        ready = []
        if parts:
            hi, lo = parts
            late = []

            def low_part():
                k, seg, tmp, shift, t_hi = late.pop(0)
                V.wait(t_hi)
                t_lo = V.did(nc.vector.scalar_tensor_tensor(lo[:, k, seg], tmp.ap[:, 0:T], shift,
                                                            hi[:, k, seg].bitcast(F32), ALU.add, ALU.subtract))
                tmp.release(t_lo)
                if seg.stop == n:
                    ready.append(t_lo)
            for k in range(KT):
                for v in range(n // T):
                    seg = slice(v * T, (v + 1) * T)
                    tmp, shift = tmps.next(), mod(layer, shift_v, k, v)
                    tmp.claim(V)
                    t = V.did(nc.vector.scalar_tensor_tensor(
                        tmp.ap[:, 0:T], x[:, k, seg], acoef[:, v, k:k + 1], rs.ap[:, seg], ALU.mult, ALU.mult))
                    A.wait(t)
                    t_hi = A.did(nc.scalar.activation(hi[:, k, seg], tmp.ap[:, 0:T], ACT.Identity, bias=shift))
                    late.append((k, seg, tmp, shift, t_hi))
                    if len(late) > 1:
                        low_part()
            low_part()
            rs.release(t)
            acoef_slot.release(t)
            return ready
        for k in range(KT):
            for v in range(n // T):
                seg = slice(v * T, (v + 1) * T)
                t = V.did(nc.vector.scalar_tensor_tensor(
                    h[:, k, seg], x[:, k, seg], acoef[:, v, k:k + 1], rs.ap[:, seg], ALU.mult, ALU.mult))
                A.wait(t)
                t_h = A.did(nc.scalar.activation(h[:, k, seg], h[:, k, seg], ACT.Identity,
                                                 bias=mod(layer, shift_v, k, v)))
            ready.append(t_h)
        rs.release(t)
        acoef_slot.release(t)
        return ready

    def residual(bank, token, k, gate, n):
        V.wait(token)
        for v in range(n // T):
            seg = slice(v * T, (v + 1) * T)
            xs = x[:, bass.ds(k, 1), seg].rearrange("p a n -> p (a n)")
            t = V.did(nc.vector.scalar_tensor_tensor(xs, bank.ap[:, seg], gate(v), xs, ALU.mult, ALU.add))
        bank.release(t)
        return t

    def project_residual(layer, which, n, src, ready, late=None):
        V.wait(mods_done[0])
        for c in range(2):
            slot, landed = next_chunk()
            PE.wait(landed)
            for i in range(4):
                k = c * 4 + i
                bank, t_pe = yield from btile(slot.ap, src, i * P, n=n, ready=ready)
                t = residual(bank, t_pe, k, lambda v: mod(layer, which, k, v), n)
                t = add_squares(k, n, t, first=k == 0)
                if late and k == KT - 2:
                    late()
                yield
            slot.release(t_pe)
        return t, t_pe

    hid = arena[:, 0:HT * 2 * T].rearrange("p (k n) -> p k n", k=HT)

    def gate_value_chunk(j):
        return a["w_ffn"][bass.ds(j, 1)].rearrange("a p n -> p (a n)")

    def down_chunk(j):
        return a["w_downh"][bass.ds(j, 1)].rearrange("a p n -> p (a n)")

    def ffn_parts(n):
        each = len(probs_t.slots) // 2
        his = [Slot(g, f"hi{i}", probs_r[i], [t for s in probs_t.slots[i * each:(i + 1) * each] for t in s.free])
               for i in range(2)]
        if n == 2 * T:
            return (h_r, mix_r), his
        his += [Slot(g, f"hi{i}", mix_r.rearrange("p k n -> p (k n)")[:, (i - 2) * GROUP:(i - 1) * GROUP])
                for i in (2, 3)]
        return (h_r[:, :, 0:T], h_r[:, :, T:2 * T]), his

    def feed_forward(layer, par, n, ready, parts, quarters, mods_beside, mods_down, following=()):
        arena_slot.claim(V)
        V.wait(mods_done[0])
        h_hi, h_lo = parts
        aside, accs_aside = banks.only(4), acc.only(3)
        per_turn, turns = 4, (HT - 2) // 4 - 1
        first, first_down = layer * HT, (layer - 1) * 2 * KT
        tokens, before = {}, [None]

        def finish(tile, gate, value, t_gate, t_value):
            act = tmps.next()
            act.claim(A)
            A.wait(t_gate)
            if par is None:
                t_act = A.did(nc.scalar.activation(act.ap[:, 0:n], gate.ap[:, 0:n], ACT.Silu))
                gate.release(t_act)
            else:
                def tap(d):
                    return par[:, bass.ds(tile * 3 + (C1["fw"] + d), 1)]
                t_act = A.did(nc.scalar.activation(
                    act.ap[:, 0:n], gate.ap[:, 0:n], ACT.Identity,
                    bias=par[:, bass.ds(tile + C1["fb"], 1)], scale=tap(1)))
                V.wait(t_act)
                a3 = act.ap[:, 0:n].rearrange("p (g t) -> p g t", t=T)
                g3 = gate.ap[:, 0:n].rearrange("p (g t) -> p g t", t=T)
                t_tap = V.did(nc.vector.scalar_tensor_tensor(
                    a3[:, :, 1:T], g3[:, :, 0:T - 1], tap(0), a3[:, :, 1:T], ALU.mult, ALU.add))
                V.wait(t_tap)
                t_tap = V.did(nc.vector.scalar_tensor_tensor(
                    a3[:, :, 0:T - 1], g3[:, :, 1:T], tap(2), a3[:, :, 0:T - 1], ALU.mult, ALU.add))
                gate.release(t_tap)
                yield
                A.wait(t_tap)
                t_act = A.did(nc.scalar.activation(act.ap[:, 0:n], act.ap[:, 0:n], ACT.Silu))
            yield
            V.wait(t_act, t_value)
            if n == 2 * T:
                out = hid[:, bass.ds(tile, 1), 0:n].rearrange("p a n -> p (a n)")
                tokens["hid"] = V.did(nc.vector.tensor_tensor(out, act.ap[:, 0:n], value.ap[:, 0:n], ALU.mult))
                act.release(tokens["hid"])
                value.release(tokens["hid"])
                return
            t = V.did(nc.vector.tensor_tensor(act.ap[:, 0:n], act.ap[:, 0:n], value.ap[:, 0:n], ALU.mult))
            value.release(t)
            yield
            hid_hi, hid_lo = (hid_r[:, bass.ds(tile, 1), half * T:(half + 1) * T].rearrange("p a n -> p (a n)")
                              for half in range(2))
            A.wait(t)
            t_hi = A.did(nc.scalar.activation(hid_hi, act.ap[:, 0:T], ACT.Copy))
            POOL.wait(t_hi)
            tokens["hid"] = POOL.did(nc.gpsimd.tensor_tensor(hid_lo, act.ap[:, 0:T], hid_hi.bitcast(F32), ALU.subtract))
            act.release(tokens["hid"])
            yield

        def tile_task(tile, load, ready=None):
            got = {}

            def products():
                for name, r in (("gate", ready), ("value", None)):
                    bank = banks.next()
                    bank.claim(PE)
                    got["t_" + name] = yield from quarters.products(bank, h_hi, h_lo, n, True, True, r,
                                                                    pause=1 if n == 2 * T else 2)
                    got[name] = bank
                    yield
            yield from together(products(), *([before[0]] if before[0] else []))
            tokens["pe"] = got["t_value"]
            load()
            before[0] = finish(tile, got["gate"], got["value"], got["t_gate"], got["t_value"])

        def last_finish():
            yield from before[0]
            before[0] = None

        def loads_next(j):
            return lambda: quarters.load(gate_value_chunk(j), FCHUNK, COLUMN_GROUPS)

        def load_down(j):
            quarters.load(down_chunk(j), DOWN_K * P,
                          [(k0 * P, P, k0, k1 - k0) for k0, k1 in zip(DOWN_KS, DOWN_KS[1:])])

        interleave(in_turn(tile_task(0, loads_next(first + 4), ready), last_finish()), mods_beside("first", 0))

        def body(it):
            held = quarters.carried()
            interleave(in_turn(*[tile_task(it * per_turn + (1 + i), loads_next(it * per_turn + (first + 5 + i)))
                                 for i in range(per_turn)], last_finish()), mods_beside("loop", it))
            assert held == [e[2] for e in quarters.split_up]
        g.loop(turns, body)

        done_tiles = 1 + turns * per_turn

        def load_after(tile):
            if tile + 4 < HT:
                return loads_next(first + tile + 4)
            if n == T:
                return lambda: load_down(first_down + tile + 4 - HT)
            return lambda: None
        interleave(in_turn(*[tile_task(tile, load_after(tile)) for tile in range(done_tiles, HT)], last_finish()),
                   mods_beside("last", 0))
        banks.back(aside)
        acc.back(accs_aside)
        h_slot.release(tokens["pe"])
        if n == 2 * T:
            mix_slot.release(tokens["pe"])
            quarters.close()
        t_zero = V.did(nc.vector.memset(sqacc[:, 0:n], 0.0))
        V.wait(t_zero)

        def add_to_x(tile, bank, t):
            t = residual(bank, t, tile,
                         lambda v: mods[:, bass.ds(tile + (layer * NT2 + 5 * KT), 1), v], n)
            tokens["sq"] = add_squares(tile, n, t)

        def down_tile(tile):
            slot, landed = load_chunk(width=HT * P, src=a["w_down"][bass.ds(tile, 1)]
                                      .rearrange("a p n -> p (a n)"))
            PE.wait(landed)
            bank, t = yield from btile(slot.ap, hid, 0, width=P, kts=HT, n=n, pause=1)
            slot.release(t)
            tokens["pe"] = t
            add_to_x(tile, bank, t)
            yield

        def split_down_tile(tile, load):
            bank = banks.next()
            bank.claim(PE)
            for half in range(2):
                for part in range(2):
                    t = yield from quarters.products(
                        bank, hid_r[:, half * DOWN_K:(half + 1) * DOWN_K, 0:T],
                        hid_r[:, half * DOWN_K:(half + 1) * DOWN_K, T:2 * T], n,
                        half == 0 and part == 0, half == 1 and part == 1)
                load(half)
            tokens["pe"] = t
            add_to_x(tile, bank, t)
            yield

        if n == T:
            PE.wait(tokens["hid"])

            def down_body(it):
                held = quarters.carried()
                for i in range(2):
                    interleave(split_down_tile(it * 2 + i, lambda half: load_down(
                        it * 4 + (first_down + 4 + 2 * i + half))))
                assert held == [e[2] for e in quarters.split_up]
            g.loop(KT // 2 - 1, down_body)
            if layer == 1:
                quarters.later = []
            quarters.todo = list(following)
            for tile in range(KT - 2, KT):
                interleave(split_down_tile(tile, lambda half: None))
            if layer == 1:
                quarters.close()
            mix_slot.release(tokens["pe"])
        else:
            PE.wait(tokens["hid"])

            def down_body(it):
                interleave(in_turn(down_tile(it * 2), down_tile(it * 2 + 1)), mods_down(it))
            g.loop(KT // 2, down_body)
        arena_slot.release(tokens["pe"], tokens["sq"])
        return tokens["sq"]

    class FeedForwardStart:

        def __init__(self, layer, n):
            self.layer, self.n = layer, n

        def load(self, chunks):
            for c in chunks:
                self.quarters.load(gate_value_chunk(self.layer * HT + c), FCHUNK, COLUMN_GROUPS)

        def early(self):
            self.parts, his = ffn_parts(self.n)
            self.quarters = Quarters(his)
            self.load((0, 1))
            for _ in range(2):
                self.quarters.split()

        def rest(self):
            self.quarters.refresh()
            self.load((2, 3))
            if self.n == T:
                for s in self.quarters.his.slots[2:]:
                    s.free = mix_slot.free
            else:
                V.wait(*mix_slot.free)
                A.wait(*mix_slot.free)
            return self.parts, self.quarters

    par_slots = [Slot(g, "params0", params[0]), Slot(g, "params1", params[1])]

    def load_params(layer):
        slot = par_slots[layer % 2 if layer < 2 else 0]
        slot.claim(POOL)
        if layer < 2:
            return POOL.dma(slot.ap[:, 0:N1], a["p1"][layer], param_full[layer % 2])
        return POOL.dma(slot.ap[:, 0:N2], a["p2"][layer - 2], param_full[0])

    def rope(src, t_src, rot, cos, sin, out, wait_steps=0):
        for _ in range(wait_steps):
            yield
        bank = banks.next()
        bank.claim(PE)
        PE.wait(t_src)
        t_rot = PE.did(nc.tensor.matmul(bank.ap[:, 0:T], rot, src, start=True, stop=True))
        yield
        tc, ts = tmps.next(), tmps.next()
        tc.claim(POOL)
        POOL.wait(t_src)
        t_c = POOL.did(nc.gpsimd.tensor_tensor(tc.ap[:, 0:T], src, cos, ALU.mult))
        ts.claim(V)
        V.wait(t_rot)
        t_s = V.did(nc.vector.tensor_tensor(ts.ap[:, 0:T], bank.ap[:, 0:T], sin, ALU.mult))
        bank.release(t_s)
        yield
        V.wait(t_c, t_s)
        t = V.did(nc.vector.tensor_tensor(out, tc.ap[:, 0:T], ts.ap[:, 0:T], ALU.add))
        tc.release(t)
        ts.release(t)
        return t

    def tiles_then(jobs, last=None):
        before = last
        for product, finisher in jobs:
            got = {}

            def run(product=product):
                got["r"] = yield from product
            yield from together(run(), *([before] if before else []))
            before = finisher(*got["r"]) if finisher else None
        if before:
            yield from before

    def carve(at, *shape):
        n = 1
        for s in shape:
            n *= s
        ap = arena[:, at:at + n]
        if len(shape) == 2:
            ap = ap.rearrange("p (a b) -> p a b", a=shape[0])
        if len(shape) == 3:
            ap = ap.rearrange("p (a b c) -> p a b c", a=shape[0], b=shape[1])
        return ap, at + n

    qT, at = carve(0, H1, 2 * T)
    kT, at = carve(at, H1, 2 * T)
    vtok, at = carve(at, 2 * TT, H1 * V1)
    u, at = carve(at, 2, 2 * T)
    vg, at = carve(at, 2 * TT, 256)
    cpad, at = carve(at, 2, 2, T + 2 * HALO)
    assert at <= ARENA

    def first_layer(layer, par_full, rs, t_r, spare):
        last = layer == DEPTH - 1
        nq = T if last else 2 * T
        groups = nq // T
        lam_init = 0.8 - 0.6 * math.exp(-0.3 * layer)
        par = params[layer % 2]

        def pc(name, n, off=0):
            return par[:, C1[name] + off:C1[name] + off + n]

        for e in (PE, A, V, POOL):
            e.wait(par_full)
        ready = norm_modulated(layer, pc("norm1", KT), 1, 0, 2 * T, rs, t_r)

        dots = cols.next()
        dots.claim(V)
        prod = tmps.next()
        prod.claim(V)
        for i in range(2):
            t = V.did(nc.vector.tensor_tensor(prod.ap[:, i * QK1:(i + 1) * QK1], pc("lam", QK1, 2 * i * QK1),
                                              pc("lam", QK1, (2 * i + 1) * QK1), ALU.mult))
            V.wait(t)
            t = V.did(nc.vector.reduce_sum(dots.ap[:, i:i + 1], prod.ap[:, i * QK1:(i + 1) * QK1], AX))
        prod.release(t)
        A.wait(t)
        t = A.did(nc.scalar.activation(dots.ap[:, 2:4], dots.ap[:, 0:2], ACT.Exp))
        V.wait(t)
        t = V.did(nc.vector.tensor_tensor(dots.ap[:, 4:5], dots.ap[:, 3:4], dots.ap[:, 2:3], ALU.subtract))
        V.wait(t)
        lam_neg = sb(f"lam_neg{layer}", 2)
        t = V.did(nc.vector.tensor_scalar(lam_neg[:, 0:1], dots.ap[:, 4:5], -lam_init, None, ALU.add))
        t_lam = V.did(nc.vector.tensor_scalar(lam_neg[:, 1:2], pc("subg", 1), 1.0 - lam_init, None, ALU.mult))
        dots.release(t)
        for e in (A, V, POOL):
            arena_slot.claim(e)
            mix_slot.claim(e)
        done = {}

        def conv_inputs():
            slot, landed = next_chunk()
            PE.wait(landed)
            t_pad = V.did(nc.vector.memset(cpad[:, :, :, :], 0.0))
            V.wait(t_pad)
            for i in range(2):
                gb, t_gb = yield from btile(slot.ap, h, (2 + i) * P, n=nq, ready=ready)
                ab, t_ab = yield from btile(slot.ap, h, i * P, n=nq)
                sg = tmps.next()
                sg.claim(A)
                A.wait(t_gb)
                t_sg = A.did(nc.scalar.activation(sg.ap[:, 0:nq], gb.ap[:, 0:nq], ACT.Sigmoid))
                gb.release(t_sg)
                V.wait(t_sg, t_ab)
                done["cin"] = V.did(nc.vector.tensor_tensor(
                    cpad[:, i, 0:groups, HALO:HALO + T], ab.ap[:, 0:nq].rearrange("p (g t) -> p g t", t=T),
                    sg.ap[:, 0:nq].rearrange("p (g t) -> p g t", t=T), ALU.mult))
                ab.release(done["cin"])
                sg.release(done["cin"])
                yield
            slot.release(t_ab)

        def convolution():
            ys, ts = [], [None, None]
            for i in range(2):
                y = tmps.next()
                y.claim(V)
                ys.append(y)
            V.wait(done["cin"])
            for d in range(TAPS):
                for i in range(2):
                    y3 = ys[i].ap[:, 0:nq].rearrange("p (g t) -> p g t", t=T)
                    if d == 0:
                        ts[i] = V.did(nc.vector.tensor_scalar(y3, cpad[:, i, 0:groups, 0:T], pc("conv_w", 1, i * TAPS),
                                                              pc("conv_b", 1, i), ALU.mult, ALU.add))
                    else:
                        V.wait(ts[i])
                        ts[i] = V.did(nc.vector.scalar_tensor_tensor(
                            y3, cpad[:, i, 0:groups, d:d + T], pc("conv_w", 1, i * TAPS + d), y3, ALU.mult, ALU.add))
                yield
            PE.wait(*ts)
            bank = banks.next()
            bank.claim(PE)
            for i in range(2):
                ins = nc.tensor.matmul(bank.ap[:, 0:nq], ones, ys[i].ap[:, 0:nq], start=i == 0, stop=i == 1)
            t = PE.did(ins)
            yield
            V.wait(t)
            for i in range(2):
                t = V.did(nc.vector.scalar_tensor_tensor(ys[i].ap[:, 0:nq], bank.ap[:, 0:nq], -1.0 / 256,
                                                         ys[i].ap[:, 0:nq], ALU.mult, ALU.add))
            bank.release(t)
            yield
            bank, t = sum_squares(lambda k: ys[k].ap[:, 0:nq], 2, nq, after=[t])
            yield
            rs, t_rs = rstd_of(bank, t, nq, 1.0 / 256)
            yield
            for i in range(2):
                V.wait(t_rs)
                t = V.did(nc.vector.tensor_tensor(ys[i].ap[:, 0:nq], ys[i].ap[:, 0:nq], rs.ap[:, 0:nq], ALU.mult))
                A.wait(t)
                done["yc"] = A.did(nc.scalar.activation(mix[:, 6 + i, 0:nq], ys[i].ap[:, 0:nq], ACT.Silu,
                                                        bias=pc("lnc_b", 1, i), scale=pc("lnc_g", 1, i)))
                ys[i].release(done["yc"])
            rs.release(t)
            yield

        def qk_finish(bank, t_pe, name, hd, out, gain, n):
            A.wait(t_pe)
            raw, sq = tmps.next(), tmps.next()
            raw.claim(A)
            t_raw = A.did(nc.scalar.activation(raw.ap[:, 0:n], bank.ap[:, 0:n], ACT.Copy))
            sq.claim(A)
            t_sq = A.did(nc.scalar.activation(sq.ap[:, 0:n], bank.ap[:, 0:n], ACT.Square))
            bank.release(t_sq)
            yield
            ss = banks.next()
            ss.claim(PE)
            PE.wait(t_sq)
            t_ss = PE.did(nc.tensor.matmul(ss.ap[:, 0:n], half, sq.ap[:, 0:n], start=True, stop=True))
            yield
            rs, t_rs = rstd_of(ss, t_ss, n, 1.0 / QK1, tmp=sq)
            V.wait(t_raw, t_rs)
            t_n = V.did(nc.vector.scalar_tensor_tensor(
                raw.ap[:, 0:T], raw.ap[:, 0:T], gain, rs.ap[:, 0:T], ALU.mult, ALU.mult))
            t_c = t_n
            if n > T:
                t_c = V.did(nc.vector.scalar_tensor_tensor(
                    out[:, hd, T:n], raw.ap[:, T:n], gain, rs.ap[:, T:n], ALU.mult, ALU.mult))
            rs.release(t_c)
            yield
            done[name, hd] = yield from rope(raw.ap[:, 0:T], t_n, C("rot1", P), C("cos1", T), C("sin1", T),
                                             out[:, hd, 0:T])
            raw.release(done[name, hd])

        def in_chunk(jobs):
            slot, landed = next_chunk()
            PE.wait(landed)
            jobs = jobs(slot.ap)
            for n, (product, finisher) in enumerate(jobs):
                def run(product=product, n=n):
                    bank, t = yield from product
                    if n == len(jobs) - 1:
                        slot.release(t)
                    return bank, t
                yield run(), finisher

        def finish_value(tt):
            def f(bank, t_pe):
                A.wait(t_pe)
                done["v"] = A.did(nc.scalar.activation(vtok[:, tt, :], bank.ap[:, :], ACT.Copy))
                bank.release(done["v"])
                yield
            return f

        def gmlp():
            slot, landed = next_chunk()
            PE.wait(landed)
            for i in range(2):
                bank, t_pe = yield from btile(slot.ap, h, i * P, n=nq, pause=2)
                A.wait(t_pe)
                t_u = A.did(nc.scalar.activation(u[:, i, 0:nq], bank.ap[:, 0:nq], ACT.Gelu_apprx_tanh))
                bank.release(t_u)
                yield
            for tt in range(nq // P):
                bank, t_pe = yield from atile(slot.ap, h, tt * P, 256, 256, pause=2)
                A.wait(t_pe)
                t_vg = A.did(nc.scalar.activation(vg[:, tt, :], bank.ap[:, 0:256], ACT.Gelu_apprx_tanh))
                bank.release(t_vg)
                yield
            slot.release(t_pe)
            h_slot.release(t_pe)
            V.wait(t_vg)
            stats = [cols.next() for _ in range(nq // P)]
            for tt, st in enumerate(stats):
                st.claim(V)
                t = V.did(nc.vector.bn_stats(st.ap[:, 0:6], vg[:, tt, :]))
            V.wait(t)
            for st in stats:
                t = V.did(nc.vector.bn_aggr(st.ap[:, 6:8], st.ap[:, 0:6]))
            yield
            A.wait(t)
            for st in stats:
                t = A.did(nc.scalar.activation(st.ap[:, 8:9], st.ap[:, 7:8], ACT.Sqrt, bias=eps))
            yield
            V.wait(t)
            for st in stats:
                t = V.did(nc.vector.reciprocal(st.ap[:, 9:10], st.ap[:, 8:9]))
            V.wait(t)
            for tt, st in enumerate(stats):
                t = V.did(nc.vector.tensor_scalar(vg[:, tt, :], vg[:, tt, :], st.ap[:, 6:7], st.ap[:, 9:10],
                                                  ALU.subtract, ALU.mult))
                st.release(t)
            yield
            V.wait(t)
            for tt in range(nq // P):
                t = V.did(nc.vector.tensor_tensor(vg[:, tt, :], vg[:, tt, :], pc("lnv_g", 256), ALU.mult))
            yield
            V.wait(t)
            for tt in range(nq // P):
                t = V.did(nc.vector.tensor_tensor(vg[:, tt, :], vg[:, tt, :], pc("lnv_b", 256), ALU.add))
            yield
            PE.wait(t)
            for i in range(2):
                bank = banks.next()
                bank.claim(PE)
                for j in range(2):
                    hd = 2 * i + j
                    for tt in range(nq // P):
                        ins = nc.tensor.matmul(bank.ap[64 * j:64 * j + 64, tt * P:(tt + 1) * P],
                                               vg[:, tt, hd * 64:hd * 64 + 64], pc("w_sT", P, hd * P),
                                               start=True, stop=True)
                t = PE.did(ins)
                gated = tmps.next()
                gated.claim(V)
                V.wait(t)
                for tt in range(nq // P):
                    t = V.did(nc.vector.tensor_tensor(gated.ap[:, tt * P:(tt + 1) * P],
                                                      bank.ap[:, tt * P:(tt + 1) * P], pc("b_s", P, i * P), ALU.add))
                bank.release(t)
                V.wait(t, t_u)
                done["ya"] = V.did(nc.vector.tensor_tensor(mix[:, i, 0:nq], gated.ap[:, 0:nq], u[:, i, 0:nq], ALU.mult))
                gated.release(done["ya"])
                yield

        def diff_head(hd, qtiles, k0, nk):
            nkt = nk // P
            pt = probs_t.next()
            pt.claim(A)
            for i, qt in enumerate(qtiles):
                sm, pm = [], []
                stat = cols.next()
                stat.claim(V)
                PE.wait(done["q", hd], done["k", hd])
                for m in range(2):
                    s = banks.next()
                    s.claim(PE)
                    t_s = PE.did(nc.tensor.matmul(s.ap[:, 0:nk], qT[64 * m:64 * m + 64, hd, qt * P:(qt + 1) * P],
                                                  kT[64 * m:64 * m + 64, hd, k0:k0 + nk], start=True, stop=True))
                    sm.append((s, t_s))
                yield
                for m, (s, t_s) in enumerate(sm):
                    V.wait(t_s)
                    t = V.did(nc.vector.reduce_max(stat.ap[:, m:m + 1], s.ap[:, 0:nk], AX))
                V.wait(t)
                t = V.did(nc.vector.tensor_scalar(stat.ap[:, 2:4], stat.ap[:, 0:2], -QK1 ** -0.5, None, ALU.mult))
                yield
                A.wait(t)
                for m, (s, _) in enumerate(sm):
                    p = tmps.next()
                    p.claim(A)
                    t = A.did(nc.scalar.activation(p.ap[:, 0:nk], s.ap[:, 0:nk], ACT.Exp, bias=stat.ap[:, 2 + m:3 + m],
                                                   scale=QK1 ** -0.5, accum_out=stat.ap[:, 4 + m:5 + m]))
                    s.release(t)
                    pm.append(p)
                yield
                V.wait(t)
                t = V.did(nc.vector.reciprocal(stat.ap[:, 6:8], stat.ap[:, 4:6]))
                V.wait(t, t_lam)
                t1 = V.did(nc.vector.tensor_scalar(stat.ap[:, 8:9], stat.ap[:, 7:8], lam_neg[:, 0:1], None, ALU.mult))
                t0 = V.did(nc.vector.tensor_scalar(pm[0].ap[:, 0:nk], pm[0].ap[:, 0:nk], stat.ap[:, 6:7], None, ALU.mult))
                V.wait(t0, t1)
                t = V.did(nc.vector.scalar_tensor_tensor(pm[0].ap[:, 0:nk], pm[1].ap[:, 0:nk], stat.ap[:, 8:9],
                                                         pm[0].ap[:, 0:nk], ALU.mult, ALU.add))
                pm[1].release(t)
                stat.release(t)
                yield
                yield
                yield
                PE.wait(t)
                tr = banks.next()
                tr.claim(PE)
                for kt in range(nkt):
                    ins = nc.tensor.transpose(tr.ap[:, kt * P:(kt + 1) * P], pm[0].ap[:, kt * P:(kt + 1) * P], ident)
                t = PE.did(ins)
                pm[0].release(t)
                yield
                A.wait(t)
                t_pt = A.did(nc.scalar.activation(pt.ap[:, 0:nkt, i * P:(i + 1) * P],
                                                  tr.ap[:, 0:nk].rearrange("p (k q) -> p k q", q=P), ACT.Copy))
                tr.release(t_pt)
                yield
            PE.wait(t_pt, done["v"])
            o = banks.next()
            o.claim(PE)
            for kt in range(nkt):
                ins = nc.tensor.matmul(o.ap[:, 0:T], vtok[:, k0 // P + kt, hd * V1:(hd + 1) * V1],
                                       pt.ap[:, kt, :], start=kt == 0, stop=kt == nkt - 1)
            t = PE.did(ins)
            pt.release(t)
            yield
            V.wait(t)
            q0 = qtiles[0] * P
            done["o", hd] = V.did(nc.vector.tensor_copy(mix[:, 2 + hd, q0:q0 + T], o.ap[:, 0:T]))
            o.release(done["o", hd])
            yield

        def sub_norm(hd):
            m = mix[:, 2 + hd, 0:nq]
            bank, t = sum_squares(lambda k: m, 1, nq, after=[done["o", hd]])
            yield
            rs, t = rstd_of(bank, t, nq, 1.0 / V1)
            yield
            V.wait(t)
            done["yb", hd] = V.did(nc.vector.scalar_tensor_tensor(m, m, lam_neg[:, 1:2], rs.ap[:, 0:nq],
                                                                  ALU.mult, ALU.mult))
            rs.release(done["yb", hd])
            yield

        interleave(conv_inputs(), beside=[spare])

        def projections():
            for name, out, gain, n in (("k", kT, pc("kg", 1), 2 * T), ("q", qT, pc("qg", 1), nq)):
                yield from in_chunk(lambda w: [
                    (btile(w, h, hd * P, n=n, pause=2, ready=ready),
                     lambda bank, t, hd=hd: qk_finish(bank, t, name, hd, out, gain, n)) for hd in range(H1)])
            yield from in_chunk(lambda w: [(atile(w, h, tt * P, 0, H1 * V1, pause=2), finish_value(tt))
                                           for tt in range(2 * TT)])

        interleave(tiles_then(projections()), convolution(), beside=[spare])
        units = []
        for hd in range(H1):
            units.append(diff_head(hd, (0, 1), 0, 2 * T))
            if not last:
                units.append(diff_head(hd, (2, 3), T, T))
        interleave(abreast(2, units), gmlp(), beside=[spare])
        interleave(abreast(2, [sub_norm(hd) for hd in range(H1)]), beside=[spare])
        ffn_start = FeedForwardStart(layer, nq)
        outs = [done["ya"], done["ya"], *(done["yb", hd] for hd in range(H1)), done["yc"], done["yc"]]
        got = {}

        def out_task():
            got["r"] = yield from project_residual(layer, 2, nq, mix, outs, ffn_start.early)
        interleave(out_task(), spare)
        t_sq, t_pe = got["r"]
        mix_slot.release(t_pe)
        arena_slot.release(t_pe, done["yc"], t_sq)
        parts, quarters = ffn_start.rest()
        rs, t_r = x_rstd(nq, t_sq)
        ready = norm_modulated(layer, pc("norm2", KT), 4, 3, nq, rs, t_r, parts)
        return nq, par, ready, parts, quarters

    def finished(task):
        while True:
            try:
                next(task)
            except StopIteration as e:
                return e.value

    def none(*_):
        return iter(())

    pos_i = nc.alloc_sbuf_tensor("sb_pos", [P, T], I32)
    t = SP.dma(pos_i[:], a["pos"], Sem(g, "positions_landed"))
    ang, turns_f = tmps.next(), tmps.next()
    turns_i = nc.alloc_sbuf_tensor("sb_turns", [P, T], I32)
    ang.claim(V)
    turns_f.claim(V)
    V.wait(t)
    t = V.did(nc.vector.tensor_copy(ang.ap[:, 0:T], pos_i[:]))
    V.wait(t)
    t_ang = V.did(nc.vector.tensor_scalar(ang.ap[:, 0:T], ang.ap[:, 0:T], C("inv", 1), None, ALU.mult))
    parts, rest = [], 2 * math.pi
    for bits in (8, 11, 11):
        e = 2.0 ** (math.floor(math.log2(rest)) - bits + 1)
        parts.append(math.floor(rest / e) * e)
        rest -= parts[-1]
    parts.append(rest)
    for table, shift in ((sin2, 0.0), (cos2, 0.25)):
        V.wait(t_ang)
        t = V.did(nc.vector.tensor_scalar(turns_f.ap[:, 0:T], ang.ap[:, 0:T], 1 / (2 * math.pi), shift, ALU.mult, ALU.add))
        V.wait(t)
        t = V.did(nc.vector.tensor_copy(turns_i[:], turns_f.ap[:, 0:T]))
        V.wait(t)
        t = V.did(nc.vector.tensor_copy(turns_f.ap[:, 0:T], turns_i[:]))
        V.wait(t)
        t = V.did(nc.vector.tensor_copy(table[:], ang.ap[:, 0:T]))
        for part in parts:
            V.wait(t)
            t = V.did(nc.vector.scalar_tensor_tensor(table[:], turns_f.ap[:, 0:T], -part, table[:], ALU.mult, ALU.add))
        V.wait(t)
        t = V.did(nc.vector.tensor_scalar(table[:], table[:], shift * 2 * math.pi, math.pi, ALU.add, ALU.min))
        V.wait(t)
        t = V.did(nc.vector.tensor_scalar(table[:], table[:], -math.pi, None, ALU.max))
        A.wait(t)
        t_tab = A.did(nc.scalar.activation(table[:], table[:], ACT.Sin))
    ang.release(t)
    turns_f.release(t)
    for e in (V, POOL):
        e.wait(t_tab)

    interleave(in_turn(*[mod_direct(j) for j in range(0, 8, 2)]),
               mod_tasks((j, [lat_c, ctx_c]) for j in range(1, 8, 2)))
    par_tok = [load_params(0), load_params(1)]
    bank, t = sum_squares(lambda k: x[:, k, :], KT, 2 * T)
    rs, t_r = rstd_of(bank, t, 2 * T, 1.0 / D)
    spare = mod_tasks((j, [lat_c, ctx_c]) for j in range(8, 24))
    nq, par, ready, parts, quarters = first_layer(0, par_tok[0], rs, t_r, spare)

    def beside_first(place, turn):
        j, n = {"first": (48, 2), "loop": (turn * 6 + 50, 6), "last": (74, 8)}[place]
        return mod_tasks((j + m, [c2]) for m in range(n))

    def beside_down(turn):
        return quickened(mod_tasks([((turn * 2 + (24 + n), [lat_c, ctx_c]) if m == 0 else
                                     (turn * 4 + (31 + 2 * n + m), [lat_c])) for n in range(2) for m in range(3)]), 3)

    t_sq = feed_forward(0, par, nq, ready, parts, quarters, beside_first, beside_down)
    par_slots[0].release(t_sq)
    par_tok.append(load_params(2))
    rs, t_r = x_rstd(nq, t_sq)
    nq, par, ready, parts, quarters = first_layer(1, par_tok[1], rs, t_r, mod_tasks((j, [c2]) for j in range(82, 96)))

    def projection_chunks(layer):
        count = [0]

        def chunks(n, groups):
            for _ in range(n):
                i = (layer - 2) * B2_CHUNKS + count[0]
                count[0] += 1
                yield a["w_second"][i], FCHUNK, groups
        values = lambda: [c for k0 in (0, 4) for c in chunks(1, value_groups(k0))]
        return [*values(), *chunks(6, COLUMN_GROUPS), *values(), *chunks(4, COLUMN_GROUPS), *values(),
                *chunks(12, COLUMN_GROUPS), *chunks(1, COLUMN_GROUPS[:1]), *chunks(4, ()), *chunks(4, COLUMN_GROUPS),
                *((gate_value_chunk(layer * HT + c), FCHUNK, COLUMN_GROUPS) for c in range(4))]

    t_sq = feed_forward(1, par, nq, ready, parts, quarters, none, none, projection_chunks(2))
    pe_now = PE.sem.now()
    his_free = [modring.slots[1].free, [pe_now, V.sem.now(), A.sem.now(), POOL.sem.now()]]
    quarters.his = Turns([Slot(g, f"hi_b{i}", (modring_r, params_r)[i // 2][:, i % 2 * GROUP:(i % 2 + 1) * GROUP],
                               his_free[i // 2]) for i in range(4)])
    quarters.waiting, quarters.later = quarters.later, None
    for _ in range(2):
        quarters.split()

    qT2 = mix[:, :, T:2 * T]
    kT2 = modring.slots[0].ap.rearrange("p (k n) -> p k n", k=KT)
    h_hi, h_lo = h_r[:, :, 0:T], h_r[:, :, T:2 * T]
    qiT, at = carve(0, 4, T)
    kiT, at = carve(at, T)
    v2, at = carve(at, TT, VW)
    gates, at = carve(at, 3 * KT, T)
    idx, at = carve(at, TT, T)
    work, at = carve(at, TT, T)
    wi, at = carve(at, TT, IDX_H)
    cmask, at = carve(at, NHC, 3 * P)
    fcum, at = carve(at, T)
    fcol, at = carve(at, TT, NHC)
    assert at <= ARENA, at

    for e in (A, V, POOL):
        e.wait(pe_now)

    def second_layer(layer, par_full, t_sq, following):
        par = params[0]

        def pc(name, n, off=0):
            return par[:, C2[name] + off:C2[name] + off + n]

        rel = pc("rel", NHB * T).rearrange("p (h n) -> p h n", h=NHB)
        for e in (PE, A, V, POOL):
            e.wait(par_full)
        t_rel = V.did(nc.vector.memset(rel[0:64, :, T - 64:T], MASKED))
        rs, t_r = x_rstd(T, t_sq)
        for e in (A, V, POOL):
            arena_slot.claim(e)
            mix_slot.claim(e)
            h_slot.claim(e)
        ready = norm_modulated(layer, pc("norm1", KT), 1, 0, T, rs, t_r, (h_hi, h_lo))
        done = {}
        n5, nb = slice(0, NHC), NHB * HD

        def tile_product(ready=None):
            bank = banks.next()
            bank.claim(PE)
            return bank, (yield from quarters.products(bank, h_hi, h_lo, T, True, True, ready, pause=1))

        def placed(bias, out, name):
            def f(bank, t_pe):
                A.wait(t_pe)
                done[name] = A.did(nc.scalar.activation(out, bank.ap[:, 0:T], ACT.Identity, bias=pc("bin", 1, bias)))
                bank.release(done[name])
                yield
            return f

        def rotated(bias, out, name):
            def f(bank, t_pe):
                raw = tmps.next()
                raw.claim(A)
                A.wait(t_pe)
                t = A.did(nc.scalar.activation(raw.ap[:, 0:T], bank.ap[:, 0:T], ACT.Identity, bias=pc("bin", 1, bias)))
                bank.release(t)
                yield
                done[name] = yield from rope(raw.ap[:, 0:T], t, C("rot2", P), cos2[:], sin2[:], out, 3)
                raw.release(done[name])
            return f

        def forget_start(bank, t_pe):
            f = tmps.next()
            f.claim(A)
            A.wait(t_pe)
            t = A.did(nc.scalar.activation(f.ap[n5, 0:T], bank.ap[n5, 0:T], ACT.Identity, bias=pc("bf", 1)[n5, :]))
            bank.release(t)
            done["f"] = f, t
            yield

        def forget_gates():
            while "f" not in done:
                yield
            (f, t), e = done["f"], tmps.next()
            e.claim(A)
            A.wait(t)
            t = A.did(nc.scalar.activation(e.ap[n5, 0:T], f.ap[n5, 0:T], ACT.Abs))
            A.wait(t)
            t = A.did(nc.scalar.activation(e.ap[n5, 0:T], e.ap[n5, 0:T], ACT.Exp, scale=-1.0))
            A.wait(t)
            t = A.did(nc.scalar.activation(e.ap[n5, 0:T], e.ap[n5, 0:T], ACT.Ln, bias=ones[n5, 0:1]))
            yield
            V.wait(t)
            t = V.did(nc.vector.scalar_tensor_tensor(f.ap[n5, 0:T], f.ap[n5, 0:T], 0.0, e.ap[n5, 0:T], ALU.min, ALU.subtract))
            V.wait(t)
            t = V.did(nc.vector.memset(e.ap[n5, 0:T], 1.0))
            V.wait(t)
            t_f = V.did(nc.vector.tensor_tensor_scan(fcum[n5, :], e.ap[n5, 0:T], f.ap[n5, 0:T], 0.0, ALU.mult, ALU.add))
            f.release(t_f)
            e.release(t_f)
            yield
            PE.wait(t_f)
            for tt in range(TT):
                bank = banks.next()
                bank.claim(PE)
                t = PE.did(nc.tensor.transpose(bank.ap[:, 0:NHC], fcum[n5, tt * P:(tt + 1) * P], ident[n5, n5]))
                V.wait(t)
                t = V.did(nc.vector.tensor_copy(fcol[:, tt, :], bank.ap[:, 0:NHC]))
                bank.release(t)
                yield
            for hd in range(NHC):
                bank = banks.next()
                bank.claim(PE)
                t = PE.did(nc.tensor.matmul(bank.ap[:, 0:T], C("onehot", NHC * P)[n5, hd * P:(hd + 1) * P],
                                            fcum[n5, :], start=True, stop=True))
                yield
                A.wait(t)
                A.did(nc.scalar.activation(cmask[:, hd, 0:P], bank.ap[:, 0:P], ACT.Copy, scale=-1.0))
                t = A.did(nc.scalar.activation(cmask[:, hd, P:3 * P], bank.ap[:, 0:T], ACT.Copy, scale=-1.0))
                bank.release(t)
                POOL.wait(t)
                for c0, n, base in ((0, P, 0), (P, T, P)):
                    done["cmask"] = POOL.did(nc.gpsimd.affine_select(
                        out=cmask[:, hd, c0:c0 + n], in_=cmask[:, hd, c0:c0 + n], compare_op=ALU.is_ge,
                        fill=MASKED, base=base, pattern=[[-1, n]], channel_multiplier=1))
                yield

        def index(qt):
            nk = (qt + 1) * P
            PE.wait(done["qi3"], done["ki"], done["qi0"], done["qi1"], done["qi2"])
            for hd in range(IDX_H):
                p0 = 64 * (hd % 2)
                bank = banks.next()
                bank.claim(PE)
                t = PE.did(nc.tensor.matmul(bank.ap[:, 0:nk], qiT[p0:p0 + 64, hd // 2, qt * P:(qt + 1) * P],
                                            kiT[p0:p0 + 64, 0:nk], start=True, stop=True))
                r = tmps.next()
                r.claim(A)
                A.wait(t)
                t = A.did(nc.scalar.activation(r.ap[:, 0:nk], bank.ap[:, 0:nk], ACT.Relu))
                bank.release(t)
                yield
                V.wait(t, done["wi"])
                w = wi[:, qt, hd:hd + 1]
                if hd == 0:
                    t = V.did(nc.vector.tensor_scalar(idx[:, qt, 0:nk], r.ap[:, 0:nk], w, None, ALU.mult))
                else:
                    V.wait(t_idx)
                    t = V.did(nc.vector.scalar_tensor_tensor(idx[:, qt, 0:nk], r.ap[:, 0:nk], w, idx[:, qt, 0:nk],
                                                             ALU.mult, ALU.add))
                t_idx = t
                r.release(t)
            V.wait(t_idx)
            t = V.did(nc.vector.memset(idx[0:64, qt, nk - 64:nk], FILL))
            for _ in range(TOPK // 8):
                best = cols.next()
                best.claim(V)
                V.wait(t)
                t = V.did(nc.vector.max(best.ap[:, 0:8], idx[:, qt, 0:nk]))
                V.wait(t)
                t = V.did(nc.vector.match_replace(idx[:, qt, 0:nk], best.ap[:, 0:8], idx[:, qt, 0:nk], TAKEN))
                best.release(t)
                yield
            V.wait(t)
            done["sel"] = V.did(nc.vector.tensor_scalar(work[:, qt, 0:nk], idx[:, qt, 0:nk], TAKEN_UNDER, MASKED,
                                                        ALU.is_gt, ALU.mult))
            yield

        def head(tile, p0, vcol, bias, needs):
            rows = slice(p0, p0 + 64)
            pt = probs_t.next()
            pt.claim(A)
            PE.wait(*(done[n] for n in needs if n[0] in "qk"))
            V.wait(*(done[n] for n in needs))
            for qt in range(TT):
                nk = (qt + 1) * P
                s = banks.next()
                s.claim(PE)
                t = PE.did(nc.tensor.matmul(s.ap[:, 0:nk], qT2[rows, tile, qt * P:(qt + 1) * P],
                                            kT2[rows, tile, 0:nk], start=True, stop=True))
                yield
                lg, stat = tmps.next(), cols.next()
                lg.claim(V)
                stat.claim(V)
                V.wait(t)
                t = bias(lg.ap[:, 0:nk], s.ap[:, 0:nk], qt, nk)
                s.release(t)
                V.wait(t)
                t = V.did(nc.vector.reduce_max(stat.ap[:, 0:1], lg.ap[:, 0:nk], AX))
                V.wait(t)
                t = V.did(nc.vector.tensor_scalar(stat.ap[:, 1:2], stat.ap[:, 0:1], -1.0, None, ALU.mult))
                yield
                A.wait(t)
                p = tmps.next()
                p.claim(A)
                t = A.did(nc.scalar.activation(p.ap[:, 0:nk], lg.ap[:, 0:nk], ACT.Exp, bias=stat.ap[:, 1:2],
                                               accum_out=stat.ap[:, 2:3]))
                lg.release(t)
                yield
                V.wait(t)
                t = V.did(nc.vector.reciprocal(stat.ap[:, 3:4], stat.ap[:, 2:3]))
                V.wait(t)
                t = V.did(nc.vector.tensor_scalar(p.ap[:, 0:nk], p.ap[:, 0:nk], stat.ap[:, 3:4], None, ALU.mult))
                stat.release(t)
                yield
                yield
                yield
                PE.wait(t)
                tr = banks.next()
                tr.claim(PE)
                for kt in range(qt + 1):
                    ins = nc.tensor.transpose(tr.ap[:, kt * P:(kt + 1) * P], p.ap[:, kt * P:(kt + 1) * P], ident)
                t = PE.did(ins)
                p.release(t)
                yield
                A.wait(t)
                t_pt = A.did(nc.scalar.activation(pt.ap[:, 0:qt + 1, qt * P:(qt + 1) * P],
                                                  tr.ap[:, 0:nk].rearrange("p (k q) -> p k q", q=P), ACT.Copy))
                tr.release(t_pt)
                yield
            PE.wait(t_pt, *(done[n] for n in needs))
            o = banks.next()
            o.claim(PE)
            for qt in range(TT):
                for kt in range(qt + 1):
                    ins = nc.tensor.matmul(o.ap[rows, qt * P:(qt + 1) * P], v2[:, kt, vcol:vcol + HD],
                                           pt.ap[:, kt, qt * P:(qt + 1) * P], start=kt == 0, stop=kt == qt)
            t = PE.did(ins)
            pt.release(t)
            yield
            A.wait(t)
            done["o"] = A.did(nc.scalar.activation(mix[rows, tile, 0:T], o.ap[rows, 0:T], ACT.Copy))
            o.release(done["o"])
            yield

        def scaled_plus(table):
            def f(out, s, qt, nk):
                return V.did(nc.vector.scalar_tensor_tensor(out, s, HD ** -0.5, table(qt, nk), ALU.mult, ALU.add))
            return f

        def forget(hd):
            def f(out, s, qt, nk):
                lg = tmps.next()
                lg.claim(V)
                t = V.did(nc.vector.tensor_scalar(lg.ap[:, 0:nk], s, HD ** -0.5, fcol[:, qt, hd:hd + 1], ALU.mult, ALU.add))
                V.wait(t)
                c0 = qt * P
                t = V.did(nc.vector.tensor_tensor(out, lg.ap[:, 0:nk], cmask[:, hd, c0:c0 + nk], ALU.add))
                lg.release(t)
                return t
            return f

        places = {f"{n}{i}": (m[:, t0 + i, :]) for t0, b, c in ((0, "a", 3), (3, "b", 2), (5, "c", 2))
                  for i in range(c) for n, m in (("q" + b, qT2), ("k" + b, kT2))}
        places |= {"qbc4": qT2[:, 7, :], "kbc4": kT2[:, 7, :], "ki": kiT, **{f"qi{i}": qiT[:, i, :] for i in range(4)}}
        order = B2_ORDER

        def tile_jobs(names):
            for n in names:
                yield tile_product(), (rotated if n[1] in "ai" else placed)(order.index(n), places[n], n)

        def value_job(v0, n, name, extras=False):
            def product():
                outs = []
                for tok in (slice(0, P), slice(P, 2 * P), *([None] if extras else [])):
                    bank = banks.next()
                    bank.claim(PE)
                    more = IDX_H if extras else 0
                    outs.append((bank, tok, slice(0, n + more) if tok else slice(n + more, n + more + P)))
                for group in range(4):
                    PE.wait(*ready[2 * group:2 * group + 2])
                    t = yield from quarters.values(outs, h_hi, h_lo, group == 3)
                return [bank for bank, _, _ in outs], t

            def finish(used, t_pe):
                V.wait(t_pe)
                for tt in range(TT):
                    done[name] = V.did(nc.vector.tensor_tensor(v2[:, tt, v0:v0 + n], used[tt].ap[:, 0:n], pc("bv", n, v0), ALU.add))
                    if extras:
                        t = V.did(nc.vector.tensor_tensor(wi[:, tt, :], used[tt].ap[:, n:n + IDX_H], pc("bwi", IDX_H), ALU.add))
                        V.wait(t)
                        done["wi"] = V.did(nc.vector.tensor_scalar(wi[:, tt, :], wi[:, tt, :], IDX_H ** -0.5 * HD ** -0.5,
                                                                   None, ALU.mult))
                    used[tt].release(V.sem.now())
                    yield
                if extras:
                    for _ in forget_start(used[2], t_pe):
                        yield
            return product(), finish

        def first_jobs():
            yield value_job(NHA * HD, nb, "vb", True)
            yield from tile_jobs(FIRST_TILES)

        def other_jobs():
            yield from tile_jobs(MORE_TILES)
            yield value_job(NHA * HD + nb, NHC * HD, "vc")
            yield from tile_jobs(LAST_TILES)
            yield value_job(0, NHA * HD, "va")
            yield from tile_jobs(("qa2",))

        def gated(j):
            def f(bank, t_pe):
                A.wait(t_pe)
                done["logits", j] = A.did(nc.scalar.activation(gates[:, j, :], bank.ap[:, 0:T], ACT.Identity,
                                                               bias=pc("bgate", 1, j)))
                bank.release(done["logits", j])
                yield
            return f

        def gate_jobs():
            for j in range(3 * KT):
                yield tile_product(), gated(j)

        forget_task = slowly(forget_gates(), 3)
        interleave(tiles_then(first_jobs()), beside=[forget_task])
        indexer = in_turn(index(0), index(1))
        interleave(tiles_then(other_jobs()), beside=[in_turn(forget_task, slowly(indexer, 3))])
        done["rel"] = t_rel
        bc_heads, a_heads = [], []
        for hd in range(NHB):
            tile, p0, q = (3 + hd // 2, 64 * (hd % 2), f"b{hd // 2}") if hd < 4 else (7, 0, "bc4")
            bc_heads.append(head(tile, p0, NHA * HD + hd * HD, scaled_plus(lambda qt, nk, hd=hd: rel[:, hd, T - nk:T]),
                                 ("q" + q, "k" + q, "rel", "vb")))
        for hd in range(NHC):
            tile, p0, q = (5 + hd // 2, 64 * (hd % 2), f"c{hd // 2}") if hd < 4 else (7, 64, "bc4")
            bc_heads.append(head(tile, p0, (NHA + NHB) * HD + hd * HD, forget(hd), ("q" + q, "k" + q, "cmask", "vc")))
        for hd in range(NHA):
            a_heads.append(head(hd // 2, 64 * (hd % 2), hd * HD, scaled_plus(lambda qt, nk: work[:, qt, 0:nk]),
                                (f"qa{hd // 2}", f"ka{hd // 2}", "sel", "va")))
        interleave(tiles_then(gate_jobs()), slowly(abreast(2, bc_heads, 6), 2),
                   slowly(in_turn(indexer, abreast(2, a_heads, 6)), 2))

        h_slot.release(PE.sem.now())
        PE.wait(done["o"])
        h_slot.claim(V)
        A.wait(done["logits", 3 * KT - 1])
        for c in range(4):
            j = slice(2 * c, 2 * c + 2)
            g4 = gates.rearrange("p (b k) n -> p b k n", b=3)[:, :, j, :]
            done["gates", c] = A.did(nc.scalar.activation(g4, g4, ACT.Sigmoid))
        y_ready, late = [], []

        def low_part():
            j, m, t_hi = late.pop(0)
            V.wait(t_hi)
            t_lo = V.did(nc.vector.tensor_tensor(h_lo[:, j, :], m.ap[:, 0:T], h_hi[:, j, :].bitcast(F32), ALU.subtract))
            m.release(t_lo)
            y_ready.append(t_lo)
        for c in range(4):
            slot = quarters.unsplit.pop(0)
            PE.wait(quarters.landed[slot])
            for i in range(2):
                j = c * 2 + i
                parts = []
                for br, kts in enumerate((((0, 0, P), (1, 0, P), (2, 0, P)), ((3, 0, P), (4, 0, P), (7, 0, 64)),
                                          ((5, 0, P), (6, 0, P), (7, 64, P)))):
                    bank = banks.next()
                    bank.claim(PE)
                    for n, (k, r0, r1) in enumerate(kts):
                        ins = nc.tensor.matmul(bank.ap[:, 0:T], slot.ap[r0:r1, k * 2 * P + i * P:k * 2 * P + (i + 1) * P],
                                               mix[r0:r1, k, 0:T], start=n == 0, stop=n == 2)
                    t_pe = PE.did(ins)
                    m = tmps.next()
                    m.claim(V)
                    V.wait(t_pe, done["gates", c])
                    t = V.did(nc.vector.tensor_tensor(m.ap[:, 0:T], bank.ap[:, 0:T], gates[:, br * KT + j, :], ALU.mult))
                    bank.release(t)
                    parts.append(m)
                V.wait(t)
                for other in parts[1:]:
                    t = V.did(nc.vector.tensor_tensor(parts[0].ap[:, 0:T], parts[0].ap[:, 0:T], other.ap[:, 0:T], ALU.add))
                    other.release(t)
                    V.wait(t)
                A.wait(t)
                late.append((j, parts[0], A.did(nc.scalar.activation(h_hi[:, j, :], parts[0].ap[:, 0:T], ACT.Copy))))
                if len(late) > 1:
                    low_part()
            slot.release(t_pe)
            quarters.refill()
            if c == 3:
                low_part()
        mix_slot.release(t_pe)

        def out_task():
            for k in range(KT):
                bank = banks.next()
                bank.claim(PE)
                t_pe = yield from quarters.products(bank, h_hi, h_lo, T, True, True, y_ready)
                t = residual(bank, t_pe, k, lambda v: mod(layer, 2, k, v), T)
                done["sq"] = add_squares(k, T, t, first=k == 0)
                done["out"] = t_pe
                yield
        interleave(out_task())
        h_slot.release(done["out"])
        arena_slot.release(done["out"], done["sq"])
        rs, t_r = x_rstd(T, done["sq"])
        ready = norm_modulated(layer, pc("norm2", KT), 4, 3, T, rs, t_r, (h_hi, h_lo))
        par_slots[0].release(PE.sem.now(), A.sem.now(), V.sem.now(), POOL.sem.now())
        par_next = load_params(3) if layer == 2 else None
        return feed_forward(layer, None, T, ready, (h_hi, h_lo), quarters, none, none, following), par_next

    tmps = Turns([Slot(g, f"half{2 * i + j}", s.ap[:, j * T:(j + 1) * T], s.free)
                  for i, s in enumerate(tmps.slots) for j in range(2)])
    probs_t = Turns([Slot(g, f"half_probsT{2 * i + j}", s.ap[:, 2 * j:2 * j + 2, :], s.free)
                     for i, s in enumerate(probs_t.slots) for j in range(2)])
    t_sq, par_full = second_layer(2, par_tok[2], t_sq, projection_chunks(3))
    t_sq, _ = second_layer(3, par_full, t_sq, ())

    rs, t_rs = x_rstd(T, t_sq)
    V.wait(t_rs)
    h_slot.claim(V)
    for k in range(KT):
        t = V.did(nc.vector.scalar_tensor_tensor(h[:, k, 0:T], x[:, k, 0:T], const[:, CC["final"] + k:CC["final"] + k + 1],
                                                 rs.ap[:, 0:T], ALU.mult, ALU.mult))
        SP.wait(t)
        t_out = SP.dma(a["out"][:, k, :], h[:, k, 0:T], out_full)
    SP.wait(t_out)
    return g.plan


def k_major(w):
    k, n = w.shape
    return w.reshape(k // P, P, n).transpose(1, 0, 2).reshape(P, -1)


def by_column(v):
    return v.reshape(-1, P).T


def on_all(v):
    return np.broadcast_to(v.reshape(1, -1), (P, v.size))


def lay_out(i):
    i = {n: np.asarray(v) for n, v in i.items()}
    f32 = np.float32

    def padded(w, n=CHUNK):
        out = np.zeros((P, n), f32)
        out[:, :w.shape[1]] = w
        return out

    main, second, ffn, down, downh = [], [], [], [], []

    def add_feed_forward(gate, value, w_down, split_down):
        ffn.extend(k_major(np.concatenate([gate[:, c:c + P], value[:, c:c + P]], 1)) for c in range(0, FF, P))
        tiles = [k_major(w_down[:, c:c + P]) for c in range(0, D, P)]
        if split_down:
            downh.extend(t[:, n:n + DOWN_K * P] for t in tiles for n in (0, DOWN_K * P))
        else:
            down.extend(tiles)
    A0, Q0, K0, V0, CV0 = 0, 512, 1024, 1536, 2048
    for l in range(DEPTH):
        w = i["w_in"][l]
        main += [k_major(w[:, c:c + 512]) for c in (CV0, K0, Q0, V0, A0)]
        main += [k_major(i["w_out"][l][:, c:c + 512]) for c in (0, 512)]
        add_feed_forward(i["w_gate"][l], i["w_val"][l], i["w_down"][l], l > 0)
    qa, ka, va, qi, ki, wi = 0, 384, 768, 1152, 1664, 1728
    qb, kb, vb, qc, kc, vc, fc, ga = 1736, 2056, 2376, 2696, 3016, 3336, 3656, 3661
    r = lambda c, n: list(range(c, c + n))
    cols = {"ki": r(ki, 64) + r(ki, 64), "qbc4": r(qb + 256, 64) + r(qc + 256, 64),
            "kbc4": r(kb + 256, 64) + r(kc + 256, 64)}
    for name, at in (("qi", qi), ("qa", qa), ("ka", ka), ("qb", qb), ("kb", kb), ("qc", qc), ("kc", kc)):
        cols |= {f"{name}{n}": r(at + n * P, P) for n in range(4)}
    tiles = [cols[n] for n in B2_ORDER]
    rows = r(0, 384) + r(384, 256) + r(704, 256) + r(640, 64) + r(960, 64)

    def take(w, cols, n=512):
        out = np.zeros((D, n), f32)
        out[:, :len(cols)] = w[:, cols]
        return k_major(out)

    def halves(w):
        return [w[:, :FCHUNK], w[:, FCHUNK:]]

    n1, n2, n3 = len(FIRST_TILES), len(MORE_TILES), len(LAST_TILES)
    for l in range(DEPTH):
        w = i["w_in_2"][l]

        def column_chunks(names):
            joined = sum(names, [])
            return [take(w, joined[c:c + 2 * P], 2 * P) for c in range(0, len(joined), 2 * P)]
        second += halves(take(w, r(vb, 320) + r(wi, 8) + r(fc, 5)))
        second += column_chunks(tiles[:n1 + n2])
        second += halves(take(w, r(vc, 320)))
        second += column_chunks(tiles[n1 + n2:n1 + n2 + n3])
        second += halves(take(w, r(va, 384)))
        second += column_chunks([tiles[-1]] + [r(ga + c, P) for c in range(0, 3 * D, P)])
        wb = i["w_branch_2"][l][rows]
        second += [k_major(wb[:, c:c + 2 * P]) for c in range(0, D, 2 * P)]
        second += [k_major(i["w_out_2"][l][:, c:c + 2 * P]) for c in range(0, D, 2 * P)]
        wf = i["w_ffn_in_2"][l]
        add_feed_forward(wf[:, :FF], wf[:, FF:], i["w_ffn_out_2"][l], True)
    mod = [k_major(w[l][:, c:c + 256]) for w in (i["w_mod"], i["ada_w_2"]) for l in range(DEPTH)
           for c in range(0, 6 * D, 256)]

    p1 = np.zeros((DEPTH, P, N1), f32)
    p2 = np.zeros((DEPTH, P, N2), f32)

    def put(dst, where, name, v):
        dst[:, where[name]:where[name] + v.shape[1]] = v

    for l in range(DEPTH):
        q = p1[l]
        put(q, C1, "norm1", by_column(i["norm1_g"][l]))
        put(q, C1, "norm2", by_column(i["norm2_g"][l]))
        put(q, C1, "qg", np.concatenate([i["q_norm_g"][l]] * 2)[:, None])
        put(q, C1, "kg", np.concatenate([i["k_norm_g"][l]] * 2)[:, None])
        put(q, C1, "subg", i["subln_g"][l][:, None])
        put(q, C1, "conv_b", by_column(i["conv_b"][l]))
        put(q, C1, "lnc_g", by_column(i["ln_c_g"][l]))
        put(q, C1, "lnc_b", by_column(i["ln_c_b"][l]))
        put(q, C1, "fw", i["ffn_conv_w"][l].reshape(3, HT, P).transpose(2, 1, 0).reshape(P, -1))
        put(q, C1, "fb", by_column(i["ffn_conv_b"][l]))
        put(q, C1, "conv_w", i["conv_w"][l].reshape(TAPS, 2, P).transpose(2, 1, 0).reshape(P, -1))
        put(q, C1, "lnv_g", on_all(i["ln_v_g"][l]))
        put(q, C1, "lnv_b", on_all(i["ln_v_b"][l]))
        put(q, C1, "lam", on_all(np.concatenate([i[n][l] for n in ("lam_q1", "lam_k1", "lam_q2", "lam_k2")])))
        bs = np.repeat(i["b_s"][l].reshape(2, 2, P), 64, axis=1)
        put(q, C1, "b_s", bs.transpose(1, 0, 2).reshape(P, -1))
        put(q, C1, "w_sT", i["w_s"][l].transpose(2, 0, 1).reshape(P, -1))
        q = p2[l]
        b = i["b_in_2"][l]
        put(q, C2, "norm1", by_column(i["norm1_g_2"][l]))
        put(q, C2, "norm2", by_column(i["norm2_g_2"][l]))
        put(q, C2, "bin", np.stack([b[t] for t in tiles], 1))
        put(q, C2, "bgate", by_column(b[ga:ga + 3 * D]))
        q[0:NHC, C2["bf"]] = b[fc:fc + NHC]
        put(q, C2, "bv", on_all(np.concatenate([b[va:va + 384], b[vb:vb + 320], b[vc:vc + 320]])))
        put(q, C2, "bwi", on_all(b[wi:wi + IDX_H]))
        apart = np.minimum(np.arange(P)[:, None] + P - np.arange(T)[None], 128) + 128
        put(q, C2, "rel", i["rel_bias_2"][l][:, apart].transpose(1, 0, 2).reshape(P, -1))
    const = np.zeros((P, NC), f32)
    put(const, CC, "ident", np.eye(P, dtype=f32))
    put(const, CC, "ones", np.ones((P, P), f32))
    put(const, CC, "half", np.kron(np.eye(2), np.ones((64, 64))).astype(f32))
    rot1, rot2 = np.zeros((P, P), f32), np.zeros((P, P), f32)
    for blk in range(0, P, 32):
        for j in range(16):
            rot1[blk + 16 + j, blk + j], rot1[blk + j, blk + 16 + j] = -1, 1
    for blk in range(0, P, 64):
        for j in range(8):
            rot2[blk + 8 + j, blk + j], rot2[blk + j, blk + 8 + j] = -1, 1
    put(const, CC, "rot1", rot1)
    put(const, CC, "rot2", rot2)
    n = np.arange(T)
    inv1 = (10000.0 ** (-np.arange(0, 32, 2, dtype=np.float64) / 32)).astype(f32)
    ang = np.zeros((P, T), f32)
    for p in range(P):
        axis, j = (p % 64) // 32, p % 16
        ang[p] = ((n // 64) if axis == 0 else (n % 64)).astype(f32) * inv1[j]
    put(const, CC, "cos1", np.cos(ang.astype(np.float64)).astype(f32))
    put(const, CC, "sin1", np.sin(ang.astype(np.float64)).astype(f32))
    inv2 = (500000.0 ** (-np.arange(0, 16, 2, dtype=np.float64) / 16)).astype(f32)
    for p in range(P):
        if p % 64 < 16:
            const[p, CC["inv"]] = inv2[p % 8]
    const[:, CC["eps"]] = EPS
    put(const, CC, "final", by_column(i["final_g_2"]))
    put(const, CC, "c", np.concatenate([by_column(i["c"][0]), by_column(i["c_ctx"]), by_column(i["c_2"][0])], 1))
    put(const, CC, "b_mod", np.concatenate([by_column(b[l]) for b in (i["b_mod"], i["ada_b_2"]) for l in range(DEPTH)], 1))
    for hd in range(NHC):
        const[hd, CC["onehot"] + hd * P:CC["onehot"] + (hd + 1) * P] = 1

    tokens = lambda t: np.ascontiguousarray(t[0].T.reshape(KT, P, T).transpose(1, 0, 2))
    return {
        "w_main": np.stack(main), "w_second": np.stack(second), "w_down": np.stack(down), "w_ffn": np.stack(ffn), "w_downh": np.stack(downh), "w_mod": np.stack(mod), "p1": p1, "p2": p2,
        "const": const, "x": tokens(i["x"]), "ctx": tokens(i["ctx"]),
        "pos": np.ascontiguousarray(np.broadcast_to(i["positions_2"].astype(np.int32), (P, T))),
    }


def kernel(**inputs):
    import concourse.bacc as bacc
    from concourse.bass_utils import run_bass_kernel_spmd

    arrays = lay_out(inputs)
    plan = Plan()
    for final in (False, True):
        nc = bacc.Bacc("TRN2", target_bir_lowering=False, num_devices=1)
        aps = {n: nc.dram_tensor(n, list(v.shape), mybir.dt.from_np(v.dtype), kind="ExternalInput").ap()
               for n, v in arrays.items()}
        aps["out"] = nc.dram_tensor("out", [P, KT, T], F32, kind="ExternalOutput").ap()
        build(nc, aps, plan, final)
    r = run_bass_kernel_spmd(nc, [arrays], core_ids=[0])
    out = r.results[0]["out"]
    return np.ascontiguousarray(out.transpose(1, 0, 2).reshape(D, T).T)[None]
```
